# Optimizing a Trainium2 kernel written in Bass

```python
import math
import jax, jax.numpy as jnp
from jax import lax
import numpy as np

D_MODEL = 1024
BATCH = 1
SEQ = 256
DEPTH = 2

CTX_LEN = 256
GRID_W = 64
EPS = 1e-6
SSM_WIDTH = 512
SSM_GROUP = 16
SSM_GROUPS = SSM_WIDTH // SSM_GROUP
SSM_STATE = 64
DT_MIN = 0.001
DT_MAX = 0.1
RET_WIDTH = 512
RET_HEADS = 4
RET_HEAD_DIM = RET_WIDTH // RET_HEADS
RET_CHUNK = 128
ROPE_BASE = 10000.0
PEER_HEADS = 8
PEER_NKEYS = 128
PEER_EXPERTS = PEER_NKEYS * PEER_NKEYS
PEER_DKEY = 128
PEER_TOPK = 16
PEER_BLOCK = 128
IN_COLS = SSM_WIDTH + 4 * RET_WIDTH + 2 * D_MODEL
IN_SPLITS = (SSM_WIDTH, SSM_WIDTH + RET_WIDTH, SSM_WIDTH + 2 * RET_WIDTH,
             SSM_WIDTH + 3 * RET_WIDTH, SSM_WIDTH + 4 * RET_WIDTH,
             SSM_WIDTH + 4 * RET_WIDTH + D_MODEL)

kernel_name = "hybrid_s5_retention_peer_diffusion_trunk"

def _rmsnorm(x, g):
    xf = x.astype(jnp.float32)
    y = xf * lax.rsqrt(jnp.mean(xf * xf, axis=-1, keepdims=True) + EPS)
    return (y * g.astype(jnp.float32)).astype(x.dtype)

def _modulate(h, shift, scale):
    return h * (1.0 + scale) + shift

def _s5_discretise(lam_re, lam_im, log_dt):
    lam = lax.complex(lam_re.astype(jnp.float32), lam_im.astype(jnp.float32))
    dt = jnp.exp(log_dt.astype(jnp.float32))[:, None]
    lam_bar = jnp.exp(lam * dt)
    b_fac = (lam_bar - 1.0) / lam
    return lam_bar, b_fac

def _ssm_combine(e1, e2):
    a1, b1 = e1
    a2, b2 = e2
    return a1 * a2, a2 * b1 + b2

def _s5_scan(bu, lam_bar, b_fac, h0):
    b = bu * b_fac
    if h0 is not None:
        b = b.at[:, 0].add(lam_bar * h0)
    a = jnp.broadcast_to(lam_bar, b.shape)
    _, h = lax.associative_scan(_ssm_combine, (a, b), axis=1)
    return h

def _s5(u, uc, B_re, B_im, C_re, C_im, d_skip, lam_re_f, lam_im_f, log_dt_f,
        lam_re_b, lam_im_b, log_dt_b, with_ctx_out):
    f32 = jnp.float32
    b_in = lax.complex(B_re.astype(f32), B_im.astype(f32))
    c_out = lax.complex(C_re.astype(f32), C_im.astype(f32))
    d = d_skip.astype(f32).reshape(SSM_GROUPS, SSM_GROUP)

    def grouped(t):
        return t.astype(f32).reshape(t.shape[0], t.shape[1], SSM_GROUPS, SSM_GROUP)

    def drive(tg):
        return jnp.einsum('blgi,gpi->blgp', tg.astype(jnp.complex64), b_in)

    def readout(h, tg):
        y = jnp.einsum('blgp,gip->blgi', h, c_out).real + d * tg
        return y.reshape(y.shape[0], y.shape[1], SSM_WIDTH)

    fwd = _s5_discretise(lam_re_f, lam_im_f, log_dt_f)
    bwd = _s5_discretise(lam_re_b, lam_im_b, log_dt_b)
    flip = lambda t: jnp.flip(t, axis=1)
    ug, ucg = grouped(u), grouped(uc)
    bu, bu_c = drive(ug), drive(ucg)
    hc_f = _s5_scan(bu_c, *fwd, None)
    hc_b = flip(_s5_scan(flip(bu_c), *bwd, None))
    h_f = _s5_scan(bu, *fwd, hc_f[:, -1])
    h_b = flip(_s5_scan(flip(bu), *bwd, hc_b[:, 0]))
    y = readout(h_f + h_b, ug)
    yc = readout(hc_f + hc_b, ucg) if with_ctx_out else None
    return y, yc

def _rotate(t, cos, sin):
    t1, t2 = jnp.split(t, 2, axis=-1)
    return jnp.concatenate([t1 * cos - t2 * sin, t1 * sin + t2 * cos], axis=-1)

def _rope2d(t, cos_r, sin_r, cos_c, sin_c):
    tf = t.astype(jnp.float32)
    tr, tc = jnp.split(tf, 2, axis=-1)
    out = jnp.concatenate([_rotate(tr, cos_r, sin_r), _rotate(tc, cos_c, sin_c)], axis=-1)
    return out.astype(t.dtype)

def _heads(t):
    nb, l, _ = t.shape
    return t.reshape(nb, l, RET_HEADS, RET_HEAD_DIM).transpose(0, 2, 1, 3)

def _retention_dir(q, k, v, log_gamma, state0, strict, with_out):
    f32 = jnp.float32
    nb, nh, l, dh = q.shape
    nc = l // RET_CHUNK
    blk = lambda t: t.astype(f32).reshape(nb, nh, nc, RET_CHUNK, dh)
    qb, kb, vb = blk(q), blk(k), blk(v)
    pos = jnp.arange(RET_CHUNK, dtype=f32)
    lg = log_gamma[:, None]
    k_decay = jnp.exp((RET_CHUNK - 1.0 - pos)[None] * lg)
    kv = jnp.einsum('bhncd,bhnce,hc->bhnde', kb, vb, k_decay)
    chunk_decay = jnp.exp(RET_CHUNK * log_gamma)[None, :, None, None]

    def step(s, kv_n):
        return chunk_decay * s + kv_n, s

    final, s_before = lax.scan(step, state0, jnp.moveaxis(kv, 2, 0))
    if not with_out:
        return None, final
    s_before = jnp.moveaxis(s_before, 0, 2)
    diff = pos[:, None] - pos[None, :]
    mask = diff > 0 if strict else diff >= 0
    dmat = jnp.where(mask[None], jnp.exp(jnp.where(mask, diff, 0.0)[None] * log_gamma[:, None, None]), 0.0)
    scores = jnp.einsum('bhncd,bhnmd->bhncm', qb, kb) * dmat[None, :, None]
    inner = jnp.einsum('bhncm,bhnme->bhnce', scores, vb)
    q_decay = jnp.exp((pos + 1.0)[None] * lg)
    cross = jnp.einsum('bhncd,bhnde,hc->bhnce', qb, s_before, q_decay)
    return (inner + cross).reshape(nb, nh, l, dh), final

def _retention(q, k, v, qc, kc, vc, lg_f, lg_b, with_ctx_out):
    nb, nh, _, dh = q.shape
    zero = jnp.zeros((nb, nh, dh, dh), jnp.float32)
    flip = lambda t: jnp.flip(t, axis=2)
    oc_f, sc_f = _retention_dir(qc, kc, vc, lg_f, zero, False, with_ctx_out)
    oc_b, sc_b = _retention_dir(flip(qc), flip(kc), flip(vc), lg_b, zero, True, with_ctx_out)
    o_f, _ = _retention_dir(q, k, v, lg_f, sc_f, False, True)
    o_b, _ = _retention_dir(flip(q), flip(k), flip(v), lg_b, sc_b, True, True)
    o = o_f + flip(o_b)
    oc = oc_f + flip(oc_b) if with_ctx_out else None
    return o, oc

def _ret_out(o, g):
    nb, nh, l, dh = o.shape
    of = o.transpose(0, 2, 1, 3)
    of = of * lax.rsqrt(jnp.mean(of * of, axis=-1, keepdims=True) + EPS)
    return of.reshape(nb, l, nh * dh).astype(g.dtype) * jax.nn.silu(g)

def _merge(y_s, y_r, gate_s, gate_r, w_ssm_glu, w_ret_up, w_out):
    a, b = jnp.split(jax.nn.gelu(y_s) @ w_ssm_glu, 2, axis=-1)
    ys = a * jax.nn.sigmoid(b)
    yr = y_r @ w_ret_up
    m = jax.nn.sigmoid(gate_s) * ys + jax.nn.sigmoid(gate_r) * yr
    return m @ w_out

def _mixer(h, hc, rope, w_in, B_re, B_im, C_re, C_im, d_skip, lam_re_f, lam_im_f, log_dt_f,
           lam_re_b, lam_im_b, log_dt_b, w_ssm_glu, ret_decay_f, ret_decay_b, w_ret_up, w_out,
           with_ctx_out):
    u, q, k, v, g, gs, gr = jnp.split(h @ w_in, IN_SPLITS, axis=-1)
    uc, qc, kc, vc, gc, gsc, grc = jnp.split(hc @ w_in, IN_SPLITS, axis=-1)
    ys, ysc = _s5(u, uc, B_re, B_im, C_re, C_im, d_skip, lam_re_f, lam_im_f, log_dt_f,
                  lam_re_b, lam_im_b, log_dt_b, with_ctx_out)
    k_scale = RET_HEAD_DIM ** -0.5
    q_h = _rope2d(_heads(q), *rope)
    k_h = _rope2d(_heads(k), *rope) * k_scale
    qc_h, kc_h = _heads(qc), _heads(kc) * k_scale
    lg_f = -jnp.exp(ret_decay_f.astype(jnp.float32))
    lg_b = -jnp.exp(ret_decay_b.astype(jnp.float32))
    o, oc = _retention(q_h, k_h, _heads(v), qc_h, kc_h, _heads(vc), lg_f, lg_b, with_ctx_out)
    y = _merge(ys.astype(h.dtype), _ret_out(o, g), gs, gr, w_ssm_glu, w_ret_up, w_out)
    if not with_ctx_out:
        return y, None
    yc = _merge(ysc.astype(hc.dtype), _ret_out(oc, gc), gsc, grc, w_ssm_glu, w_ret_up, w_out)
    return y, yc

def _peer(h, w_q, sub_keys, expert_u, expert_v):
    shape = h.shape
    tokens = h.reshape(-1, D_MODEL)
    n_blocks = tokens.shape[0] // PEER_BLOCK
    half = PEER_DKEY // 2

    def block(tb):
        t = tb.shape[0]
        qr = (tb @ w_q).reshape(t, PEER_HEADS, 2, half)
        s = jnp.einsum('thsk,hsnk->thsn', qr, sub_keys).astype(jnp.float32)
        top_s, top_i = lax.top_k(s, PEER_TOPK)
        cand_s = top_s[:, :, 0, :, None] + top_s[:, :, 1, None, :]
        cand_i = top_i[:, :, 0, :, None] * PEER_NKEYS + top_i[:, :, 1, None, :]
        best_s, best_j = lax.top_k(cand_s.reshape(t, PEER_HEADS, PEER_TOPK * PEER_TOPK), PEER_TOPK)
        idx = jnp.take_along_axis(cand_i.reshape(t, PEER_HEADS, PEER_TOPK * PEER_TOPK), best_j, axis=-1)
        gate = jax.nn.softmax(best_s, axis=-1)
        act = jax.nn.gelu(jnp.einsum('td,thkd->thk', tb, expert_u[idx]).astype(jnp.float32),
                          approximate=False)
        w = (gate * act).astype(tb.dtype)
        return jnp.einsum('thk,thkd->td', w, expert_v[idx])

    out = lax.map(block, tokens.reshape(n_blocks, PEER_BLOCK, D_MODEL))
    return out.reshape(shape)

def setup_inputs(seed: int = 0) -> dict:
    key = jax.random.key(seed)
    ks = iter(jax.random.split(key, 40))
    nrm = lambda shape, s: jax.random.normal(next(ks), shape, jnp.float32) * s
    G, P, I, H = SSM_GROUPS, SSM_STATE, SSM_GROUP, RET_HEADS
    lam_im0 = math.pi * jnp.arange(P, dtype=jnp.float32)
    ret0 = jnp.log(-jnp.log(1.0 - 2.0 ** (-5.0 - jnp.arange(H, dtype=jnp.float32))))
    log_dt = lambda: jax.random.uniform(next(ks), (DEPTH, G), jnp.float32,
                                        math.log(DT_MIN), math.log(DT_MAX))
    return {
        "x": nrm((BATCH, SEQ, D_MODEL), 1.0),
        "c": nrm((BATCH, D_MODEL), 1.0),
        "ctx": nrm((BATCH, CTX_LEN, D_MODEL), 1.0),
        "c_ctx": nrm((D_MODEL,), 1.0),
        "w_mod": nrm((DEPTH, D_MODEL, 6 * D_MODEL), 0.5 * D_MODEL ** -0.5),
        "b_mod": nrm((DEPTH, 6 * D_MODEL), 0.02),
        "norm1_g": 1.0 + nrm((DEPTH, D_MODEL), 0.02),
        "norm2_g": 1.0 + nrm((DEPTH, D_MODEL), 0.02),
        "w_in": nrm((DEPTH, D_MODEL, IN_COLS), D_MODEL ** -0.5),
        "ssm_B_re": nrm((DEPTH, G, P, I), (2.0 * I) ** -0.5),
        "ssm_B_im": nrm((DEPTH, G, P, I), (2.0 * I) ** -0.5),
        "ssm_C_re": nrm((DEPTH, G, I, P), 0.5),
        "ssm_C_im": nrm((DEPTH, G, I, P), 0.5),
        "ssm_D": nrm((DEPTH, SSM_WIDTH), 1.0),
        "ssm_lam_re_f": -0.5 + nrm((DEPTH, G, P), 0.01),
        "ssm_lam_im_f": lam_im0 + nrm((DEPTH, G, P), 0.01),
        "ssm_log_dt_f": log_dt(),
        "ssm_lam_re_b": -0.5 + nrm((DEPTH, G, P), 0.01),
        "ssm_lam_im_b": lam_im0 + nrm((DEPTH, G, P), 0.01),
        "ssm_log_dt_b": log_dt(),
        "w_ssm_glu": nrm((DEPTH, SSM_WIDTH, 2 * D_MODEL), SSM_WIDTH ** -0.5),
        "ret_decay_f": ret0 + nrm((DEPTH, H), 0.05),
        "ret_decay_b": ret0 + nrm((DEPTH, H), 0.05),
        "w_ret_up": nrm((DEPTH, RET_WIDTH, D_MODEL), RET_WIDTH ** -0.5),
        "w_out": nrm((DEPTH, D_MODEL, D_MODEL), D_MODEL ** -0.5),
        "peer_w_q": nrm((DEPTH, D_MODEL, PEER_HEADS * PEER_DKEY), D_MODEL ** -0.5),
        "peer_sub_keys": nrm((DEPTH, PEER_HEADS, 2, PEER_NKEYS, PEER_DKEY // 2), (PEER_DKEY // 2) ** -0.5),
        "peer_u": nrm((DEPTH, PEER_EXPERTS, D_MODEL), D_MODEL ** -0.5),
        "peer_v": nrm((DEPTH, PEER_EXPERTS, D_MODEL), 0.5),
        "final_norm_g": 1.0 + nrm((D_MODEL,), 0.02),
    }

def reference(x, c, ctx, c_ctx, w_mod, b_mod, norm1_g, norm2_g, w_in, ssm_B_re, ssm_B_im,
              ssm_C_re, ssm_C_im, ssm_D, ssm_lam_re_f, ssm_lam_im_f, ssm_log_dt_f,
              ssm_lam_re_b, ssm_lam_im_b, ssm_log_dt_b, w_ssm_glu, ret_decay_f, ret_decay_b,
              w_ret_up, w_out, peer_w_q, peer_sub_keys, peer_u, peer_v, final_norm_g):
    seq = x.shape[1]
    rows = seq // GRID_W
    row_ids = jnp.repeat(jnp.arange(rows, dtype=jnp.float32), GRID_W)
    col_ids = jnp.tile(jnp.arange(GRID_W, dtype=jnp.float32), rows)
    n_freq = RET_HEAD_DIM // 4
    freqs = ROPE_BASE ** (-jnp.arange(n_freq, dtype=jnp.float32) / n_freq)
    ang_r = row_ids[:, None] * freqs[None]
    ang_c = col_ids[:, None] * freqs[None]
    rope = (jnp.cos(ang_r), jnp.sin(ang_r), jnp.cos(ang_c), jnp.sin(ang_c))

    xc = ctx
    for i in range(DEPTH):
        last = i == DEPTH - 1
        mod = jax.nn.silu(c) @ w_mod[i] + b_mod[i]
        mod_c = jax.nn.silu(c_ctx) @ w_mod[i] + b_mod[i]
        sh1, sc1, g1, sh2, sc2, g2 = jnp.split(mod[:, None, :], 6, axis=-1)
        sh1c, sc1c, g1c, sh2c, sc2c, g2c = jnp.split(mod_c, 6, axis=-1)
        h = _modulate(_rmsnorm(x, norm1_g[i]), sh1, sc1)
        hc = _modulate(_rmsnorm(xc, norm1_g[i]), sh1c, sc1c)
        y, yc = _mixer(h, hc, rope, w_in[i], ssm_B_re[i], ssm_B_im[i], ssm_C_re[i], ssm_C_im[i],
                       ssm_D[i], ssm_lam_re_f[i], ssm_lam_im_f[i], ssm_log_dt_f[i],
                       ssm_lam_re_b[i], ssm_lam_im_b[i], ssm_log_dt_b[i], w_ssm_glu[i],
                       ret_decay_f[i], ret_decay_b[i], w_ret_up[i], w_out[i], not last)
        x = x + g1 * y
        h2 = _modulate(_rmsnorm(x, norm2_g[i]), sh2, sc2)
        x = x + g2 * _peer(h2, peer_w_q[i], peer_sub_keys[i], peer_u[i], peer_v[i])
        if not last:
            xc = xc + g1c * yc
            hc2 = _modulate(_rmsnorm(xc, norm2_g[i]), sh2c, sc2c)
            xc = xc + g2c * _peer(hc2, peer_w_q[i], peer_sub_keys[i], peer_u[i], peer_v[i])
    return _rmsnorm(x, final_norm_g)


_drawn_inputs = setup_inputs


def setup_inputs(seed=0):
    import zlib

    import numpy as np

    out = dict(_drawn_inputs(seed))
    spreads = {}
    factors = {'norm1_g': 4.664,
     'norm2_g': 3.085,
     'ssm_lam_re_f': 8.0,
     'ssm_lam_re_b': 8.0,
     'final_norm_g': 2.933}
    for name, (base, spread) in spreads.items():
        noise = np.random.default_rng([zlib.crc32(name.encode()), seed]).standard_normal(out[name].shape)
        drawn = base * np.exp(spread * noise) if base else spread * noise
        out[name] = __import__('jax').numpy.asarray(drawn.astype(out[name].dtype))
    for name, factor in factors.items():
        out[name] = (out[name] * factor).astype(out[name].dtype)
    return out
```

```python
import math
from contextlib import ExitStack

import concourse.bass as bass
import numpy as np
from concourse import mybir

P = 128
DM = 1024
KD = DM // P
CTX, SEQ = 256, 256
TL = CTX + SEQ
DEPTH = 2
SSM = 512
NT = 16
CT = SSM // P
RH = 4
GRID_W = 64
EPS = 1e-6
NH, NK, TOPK = 8, 128, 16
HALF = 64
RING = 4
SLOT = 2048
MOD_UNITS = 24
FRONT_UNITS = 6
DIST_UNIT = 1
S5_ITER = 4
MERGE_UNITS, OUT_UNITS, WQ_UNITS = 8, 4, 4

F32 = mybir.dt.float32
I32 = mybir.dt.int32
U32 = mybir.dt.uint32
ALU = mybir.AluOpType
ACT = mybir.ActivationFunctionType
AX_X = mybir.AxisListType.X

C_ID, C_ONES_D, C_ONES_H, C_IOTA, C_PERM, C_T, C_I16, C_EPS, C_HPI, C_COS, C_SIN = (
    0, 128, 256, 384, 512, 640, 1152, 1168, 1169, 1170, 1426)
C_N = 1682
N_BMOD, N_G, N_FG, N_LAM, N_DEC, N_D, N_C = 0, 96, 128, 136, 328, 344, 352
N_N = 368
TP1 = 6.28125
TP2 = float(np.float32(2 * math.pi - TP1))
TP3 = float(np.float32(2 * math.pi - TP1 - float(np.float32(2 * math.pi - TP1))))
INV2PI = float(np.float32(1 / (2 * math.pi)))
TWO_PI_IN = 6.283185
(S_DT, S_R, S_TH, S_RHO, S_RHI, S_RLO, S_BR, S_BI, S_NBR, S_NBI, S_T0, S_T1, S_T2, S_COS, S_SIN,
 S_K) = range(16)

STAGES = [("mod", 0, 0)]
for _l in range(DEPTH):
    STAGES += [("norm1", _l, 0), ("front", _l, 0), ("s5", _l, 0), ("ret", _l, 0), ("merge", _l, 0)]
    for _h in ((1, 0) if _l < DEPTH - 1 else (1,)):
        STAGES += [("norm2", _l, _h), ("route", _l, _h), ("gates", _l, _h), ("experts", _l, _h)]
STAGES += [("final", 0, 1)]


def units_of(stage):
    return {"mod": MOD_UNITS * DEPTH, "front": FRONT_UNITS, "s5": 4 * S5_ITER, "ret": DIST_UNIT,
            "merge": MERGE_UNITS + OUT_UNITS, "route": WQ_UNITS, "experts": NK}.get(stage[0], 0)


def first_units():
    base, out = 0, {}
    for st in STAGES:
        out[st] = base
        base += units_of(st)
    return out


BASE = first_units()
X_COUNT, _n = {}, 0
for _st in STAGES:
    X_COUNT[_st] = _n
    _n += OUT_UNITS if _st[0] == "merge" else _st[0] == "experts"
S5_LINKS = 72


def passes_before(st):
    return [s for s in STAGES if s[0] == "norm2"].index(("norm2", st[1], st[2]))


def norms_before(st):
    return [s for s in STAGES if s[0] in ("norm1", "norm2", "final")].index(st)


class Chain:

    def __init__(self, eng, sem):
        self.eng, self.sem, self.n, self.extra = eng, sem, 0, None

    def value(self):
        return self.n if self.extra is None else self.extra + self.n

    def link(self, ins):
        self.mark(ins)
        self.eng.wait_ge(self.sem, self.value())

    def mark(self, ins):
        ins.then_inc(self.sem, 1)
        self.n += 1

    def loop(self, i, per):
        self.start, self.per, self.extra = self.n, per, i * per

    def end(self, turns):
        assert self.n - self.start == self.per, (self.n - self.start, self.per)
        self.n, self.extra = self.start + turns * self.per, None


def build_program(nc, a, until=None):
    stages = STAGES if until is None else STAGES[:until]
    ctx = ExitStack()
    with ctx:
        def sb(name, shape, dt=F32, on=ctx):
            return on.enter_context(nc.sbuf_tensor(name, shape, dt))

        def sem(name):
            return ctx.enter_context(nc.semaphore(name))

        xT = sb("xT", [P, KD, TL])
        cst = sb("cst", [P, C_N])
        par = sb("par", [P, N_N])
        s5p = sb("s5p", [P, 16, DEPTH * 2 * NT])
        lg = sb("lg", [P, DEPTH * 2 * RH])
        modT = sb("modT", [P, DEPTH, 6, KD, 2])
        gain = sb("gain", [P, DEPTH, 2, KD, 2])
        ring = sb("ring", [P, RING, SLOT])
        zeros = sb("zeros", [P, P])
        s5k = sb("s5k", [P, DEPTH * 2 * NT], I32)
        mix = ExitStack()
        hT = sb("hT", [P, KD, TL], on=mix)
        uT = sb("uT", [P, CT, TL], on=mix)
        vN = sb("vN", [P, TL // P, SSM], on=mix)
        kT = sb("kT", [P, RH, TL], on=mix)
        pj = sb("pj", [P, 24, TL], on=mix)
        qT, gT, gsT, grT = pj[:, 0:4, :], pj[:, 4:8, :], pj[:, 8:16, :], pj[:, 16:24, :]
        sub = ExitStack()
        mrow = sb("mrow", [2, 6 * DM], on=sub)
        sub.close()
        sub = ExitStack()
        sq1 = sb("sq1", [P, KD, TL], on=sub)
        rs1 = sb("rs1", [P, TL], on=sub)
        sub.close()
        sub = ExitStack()
        phase = sb("phase", [P, 2, TL], on=sub)
        turns = sb("turns", [P, TL], I32, on=sub)
        absp = sb("absp", [P, TL], on=sub)
        tab = sb("tab", [P, 2, 2, TL], on=sub)
        bu = sb("bu", [P, 2, 2, TL], on=sub)
        rot = sb("rot", [P, 2, 2, TL], on=sub)
        gst = sb("gst", [P, 2, 2, TL], on=sub)
        prod = sb("prod", [P, 2, 4, TL], on=sub)
        cpr = sb("cpr", [P, 2, 3, 32], on=sub)
        ctmp = sb("ctmp", [P, 2, 32], on=sub)
        sub.close()
        sub = ExitStack()
        decay = sb("decay", [P, RH, 2, 512], on=sub)
        dtmp = sb("dtmp", [P, RH, 512], on=sub)
        sd = sb("sd", [P, 2, 6, 256], on=sub)
        oT = sb("oT", [P, RH, TL], on=sub)
        osq = sb("osq", [P, RH, TL], on=sub)
        sub.close()
        sub = ExitStack()
        mT = sb("mT", [P, KD, TL], on=sub)
        sgb = sb("sgb", [P, 2, TL], on=sub)
        mt1 = sb("mt1", [P, 2, TL], on=sub)
        mt2 = sb("mt2", [P, 2, TL], on=sub)
        sub.close()
        mix.close()
        peer = ExitStack()
        h2T = sb("h2T", [P, KD, 256], on=peer)
        idxT = sb("idxT", [P, 3, 256], on=peer)
        tiny = ExitStack()
        hot = sb("hot", [P, 2, 4, P], on=tiny)
        tiny.close()
        tiny = ExitStack()
        actT = sb("actT", [P, 2, 256], on=tiny)
        wT = sb("wT", [P, 2, 256], on=tiny)
        tiny.close()
        sb("tiny_hold", [P, 2 * 4 * P], on=peer)
        over = ExitStack()
        gate = sb("gate", [P, NK, 256], on=over)
        over.close()
        over = ExitStack()
        sq2 = sb("sq2", [P, KD, 256], on=over)
        rs2 = sb("rs2", [P, 256], on=over)
        qrT = sb("qrT", [P, NH, 256], on=over)
        keys = sb("keys", [P, NH, 256], on=over)
        sc = sb("sc", [P, 2, NH * 2, NK], on=over)
        sc2 = sb("sc2", [P, 2, NK], on=over)
        cand = sb("cand", [P, 256], on=over)
        cand2 = sb("cand2", [P, 256], on=over)
        top = sb("top", [P, NH * 2, TOPK], on=over)
        topi = sb("topi", [P, NH * 2, TOPK], U32, on=over)
        topf = sb("topf", [P, NH * 2, TOPK], on=over)
        best = sb("best", [P, NH, TOPK], on=over)
        besti = sb("besti", [P, NH, TOPK], U32, on=over)
        bab = sb("bab", [P, 2, NH * TOPK], U32, on=over)
        babf = sb("babf", [P, 2, NH * TOPK], on=over)
        eq = sb("eq", [P, 2, NH * TOPK, TOPK], on=over)
        pick = sb("pick", [P, 3, NH * TOPK], on=over)
        ssum = sb("ssum", [P, NH], on=over)
        over.close()
        over = ExitStack()
        yout = sb("yout", [P, 2, DM], on=over)
        over.close()
        over = ExitStack()
        fout = sb("fout", [P, KD, 256], on=over)
        over.close()
        peer.close()
        ps = ctx.enter_context(nc.psum_tensor("ps", [P, 8, 512], F32))

        const_in = sem("const_in")
        unit_in = [sem(f"unit_in{s}") for s in range(RING)]
        keys_in = sem("keys_in")
        stored = sem("stored")
        used = [sem(f"used{s}") for s in range(RING)]
        dve_own, act_own, pool_own = sem("dve_own"), sem("act_own"), sem("pool_own")
        cond_ready, mod_row, mod_col, mod_done = sem("cond_ready"), sem("mod_row"), sem("mod_col"), sem("mod_done")
        s5_lam, s5_angle, s5_trig = sem("s5_lam"), sem("s5_angle"), sem("s5_trig")
        sq_ready, mean_ready, std_ready, h_ready = sem("sq_ready"), sem("mean_ready"), sem("std_ready"), sem("h_ready")
        proj_out = sem("proj_out")
        bu_ready, bu_copied = sem("bu_ready"), sem("bu_copied")
        phase_ready, table_ready = sem("phase_ready"), sem("table_ready")
        g_ready, prod_ready, cprime_ready, readout = sem("g_ready"), sem("prod_ready"), sem("cprime_ready"), sem("readout")
        rope_ps, roped = sem("rope_ps"), sem("roped")
        decay_arg, decay_ready = sem("decay_arg"), sem("decay_ready")
        score_ps, sd_ready, o_ps, o_copied = sem("score_ps"), sem("sd_ready"), sem("o_ps"), sem("o_copied")
        osq_ready, omean_ready, ostd_ready, yr_ready, ys_ready = (
            sem("osq_ready"), sem("omean_ready"), sem("ostd_ready"), sem("yr_ready"), sem("ys_ready"))
        gates_on, sg_ready, m_ready, x_ready = sem("gates_on"), sem("sg_ready"), sem("m_ready"), sem("x_ready")
        qr_ready, score_out, score_ready = sem("qr_ready"), sem("score_out"), sem("score_ready")
        exp_in, exp_out, pick_ready, pick_ps, pick_col = (
            sem("exp_in"), sem("exp_out"), sem("pick_ready"), sem("pick_ps"), sem("pick_col"))
        hot_ready, gate_ps, gate_ready = sem("hot_ready"), sem("gate_ps"), sem("gate_ready")
        a_ready, act_ready, w_ready, y_ready, y_col = (
            sem("a_ready"), sem("act_ready"), sem("w_ready"), sem("y_ready"), sem("y_col"))
        y_copied = sem("y_copied")
        fin_ready = sem("fin_ready")

        ident = cst[:, C_ID:C_ID + P]
        iota = cst[:, C_IOTA:C_IOTA + P]
        eps = cst[:, C_EPS:C_EPS + 1]

        def arrived(eng, u, i=None, per=0):
            n = 16 * (u // RING + 1)
            eng.wait_ge(unit_in[u % RING], n if i is None else i * (16 * per // RING) + n)

        def unit_used(eng, u, i=None, per=0):
            n = u // RING + 1
            eng.wait_ge(used[u % RING], n if i is None else i * (per // RING) + n)

        def slot(u, k, n):
            return ring[:, u % RING, 0:k * n].rearrange("p (k n) -> p k n", n=n)

        CREDIT = {s.name: n for s, n in ((readout, 2), (g_ready, 4), (table_ready, 2), (prod_ready, 2), (bu_copied, 1),
                                         (mod_row, 4), (gate_ready, 4), (gate_ps, 4), (w_ready, 2))}

        def count(eng, s, n):
            eng.wait_ge(s, n + CREDIT[s.name])

        def layer_width(l):
            return (0, TL) if l < DEPTH - 1 else (CTX, TL)

        block = ctx.enter_context(nc.Block())

        @block.sync
        def _(sp):
            sp.dma_start(cst[:, :], a["consts"]).then_inc(const_in, 16)
            sp.dma_start(par[:, :], a["params"]).then_inc(const_in, 16)
            sp.dma_start(xT[:, :, :], a["x_t"]).then_inc(const_in, 16)

            def load(u, src, i=None, per=0):
                n = u // RING
                if i is None:
                    if n >= 1:
                        sp.wait_ge(used[u % RING], n)
                else:
                    sp.wait_ge(used[u % RING], i * (per // RING) + n)
                w = src.shape[-1]
                sp.dma_start(ring[:, u % RING, 0:w], src).then_inc(unit_in[u % RING], 16)

            def stream(u, src, count):
                head = RING if u < RING else 0
                for k in range(head):
                    load(u + k, src[k])
                turns_ = (count - head) // RING
                with sp.Fori(0, turns_) as i:
                    for k in range(RING):
                        load(u + head + k, src[bass.ds(i * RING + (head + k), 1)].rearrange("o p n -> (o p) n"), i, RING)

            for st in stages:
                kind, l, h = st
                u = BASE[st]
                if kind == "mod":
                    stream(u, a["w_mod"], MOD_UNITS * DEPTH)
                elif kind == "front":
                    for k in range(FRONT_UNITS):
                        load(u + k, a["w_front"][l, k])
                elif kind == "s5":
                    with sp.Fori(0, S5_ITER) as i:
                        load(u, a["s5_bc"][l, bass.ds(i, 1)].rearrange("o p n -> (o p) n"), i, 4)
                        for k in range(3):
                            load(u + 1 + k, a["w_side"][l, bass.ds(i * 3 + k, 1)].rearrange("o p n -> (o p) n"), i, 4)
                elif kind == "ret":
                    load(u, a["dist"])
                elif kind == "merge":
                    stream(u, a["w_merge"][l], MERGE_UNITS)
                    stream(u + MERGE_UNITS, a["w_out"][l], OUT_UNITS)
                elif kind == "route":
                    stream(u, a["w_q"][l], WQ_UNITS)
                    sp.wait_ge(h_ready, norms_before(("norm2", l, h)) + 1)
                    sp.dma_start(keys[:, :, :], a["keys"][l]).then_inc(keys_in, 16)
                elif kind == "experts":
                    stream(u, a["experts"][l], NK)
                elif kind == "final":
                    sp.wait_ge(fin_ready, 1)
                    sp.dma_start(a["out"], fout[:, :, :]).then_inc(stored, 16)
                    sp.wait_ge(stored, 16)

        @block.gpsimd
        def _(pool):
            own = Chain(pool, pool_own)
            for st in stages:
                kind, l, h = st
                if kind == "s5":
                    with pool.Fori(0, S5_ITER) as i:
                        for n in range(8):
                            d = n % 2
                            count(pool, g_ready, i * 8 + (l * 32 + n + 1))
                            count(pool, readout, i * 8 + (l * 32 + n - 1))
                            lo = layer_width(l)[0]
                            w = TL - lo
                            for k in range(2):
                                src = gst[:, d, :, lo:TL]
                                t = tab[:, d, :, lo:TL] if k == 0 else tab[:, d, ::-1, lo:TL]
                                for c in range(2):
                                    dst = prod[:, d, 2 * k + c, 0:w]
                                    if d == 1:
                                        dst = dst.rearrange("p (h t) -> p h t", t=256)[:, :, ::-1]
                                        s_ = src[:, c, :].rearrange("p (h t) -> p h t", t=256)
                                        t_ = t[:, c, :].rearrange("p (h t) -> p h t", t=256)
                                    else:
                                        s_, t_ = src[:, c, :], t[:, c, :]
                                    last = pool.tensor_tensor(dst, s_, t_, ALU.mult)
                            last.then_inc(prod_ready, 1)

        @block.tensor
        def _(pe):
            pe.wait_ge(const_in, 48)

            def mm(out, w, x, start, stop, **k):
                return pe.matmul(out, w, x, start=start, stop=stop, **k)

            def norm_mean(st, sqb, w):
                n = norms_before(st)
                pe.wait_ge(sq_ready, n + 1)
                for k in range(KD):
                    last = mm(ps[:, 7, 0:w], cst[:, C_ONES_D:C_ONES_D + P], sqb[:, k, :], k == 0, k == KD - 1)
                last.then_inc(mean_ready, 1)

            for st in stages:
                kind, l, h = st
                u = BASE[st]
                if kind == "mod":
                    pe.wait_ge(cond_ready, 1)
                    for ll in range(DEPTH):
                        with pe.Fori(0, MOD_UNITS // RING) as i:
                            for k in range(RING):
                                v = ll * MOD_UNITS + k
                                arrived(pe, v, i, RING)
                                count(pe, mod_row, i * RING + (v - 3))
                                w = slot(v, KD, 256)
                                for c in range(KD):
                                    last = mm(ps[0:2, k, 0:256], par[:, N_C + 2 * c:N_C + 2 * c + 2], w[:, c, :],
                                              c == 0, c == KD - 1)
                                last.then_inc(used[v % RING], 1)
                        count(pe, mod_row, (ll + 1) * MOD_UNITS)
                        if ll:
                            pe.wait_ge(mod_done, ll)
                        for c in range(6 * KD):
                            last = mm(ps[:, 4, 2 * c:2 * c + 2], mrow[0:2, c * P:(c + 1) * P], ident[0:2, 0:2],
                                      True, True)
                        last.then_inc(mod_col, 1)
                elif kind == "norm1":
                    norm_mean(st, sq1, TL)
                elif kind == "norm2":
                    norm_mean(st, sq2, 256)
                elif kind == "final":
                    norm_mean(st, sq2, 256)
                elif kind == "front":
                    pe.wait_ge(h_ready, norms_before(("norm1", l, 0)) + 1)
                    for k in range(FRONT_UNITS):
                        arrived(pe, u + k)
                        if k >= 2:
                            pe.wait_ge(proj_out, 18 * l + k - 1)
                        b = 2 * (k % 2)
                        w = slot(u + k, 2 * KD, P)
                        if k in (2, 3):
                            for t in range(TL // P):
                                for j in range(2):
                                    for c in range(KD):
                                        last = mm(ps[:, b + t // 2, (t % 2) * 256 + j * P:(t % 2) * 256 + j * P + P],
                                                  hT[:, c, t * P:(t + 1) * P], w[:, j * KD + c, :], c == 0, c == KD - 1)
                        else:
                            for j in range(2):
                                for c in range(KD):
                                    last = mm(ps[:, b + j, :], w[:, j * KD + c, :], hT[:, c, :], c == 0, c == KD - 1)
                        last.then_inc(used[(u + k) % RING], 1)
                elif kind == "s5":
                    lo, hi = layer_width(l)
                    w_ = hi - lo
                    pe.wait_ge(proj_out, 18 * l + FRONT_UNITS)
                    bc = slot(u, 8, P)
                    with pe.Fori(0, S5_ITER) as i:
                        def drive(q):
                            count(pe, bu_copied, i * 4 + (l * 16 + q))
                            for c in range(2):
                                last = mm(ps[:, 4 + c, :], bc[:, 2 * q + c, :],
                                          uT[:, bass.ds(i, 1), :].rearrange("p o t -> p (o t)"), True, True)
                            last.then_inc(bu_ready, 1)

                        def side(k):
                            v = u + 1 + k
                            arrived(pe, v, i, 4)
                            pe.wait_ge(proj_out, i * 3 + (18 * l + FRONT_UNITS + max(k - 1, 0)))
                            b = 2 * (k % 2)
                            w = slot(v, 2 * KD, P)
                            for j in range(2):
                                for c in range(KD):
                                    last = mm(ps[:, b + j, 0:w_], w[:, j * KD + c, :], hT[:, c, lo:hi],
                                              c == 0, c == KD - 1)
                            last.then_inc(used[v % RING], 1)

                        def read(q):
                            for d in range(2):
                                n = 2 * q + d
                                count(pe, prod_ready, i * 8 + (l * 32 + n + 1))
                                pe.wait_ge(cprime_ready, i * 8 + (l * 32 + n + 1))
                                for k in range(4):
                                    last = mm(ps[32 * q:32 * q + 32, 6, 0:w_], cpr[:, d, (0, 1, 2, 2)[k], :],
                                              prod[:, d, k, 0:w_], n % 2 == 0 and k == 0, d == 1 and k == 3)
                                last.then_inc(readout, 1)

                        arrived(pe, u, i, 4)
                        drive(0)
                        side(0)
                        drive(1)
                        pe.wait_ge(used[u % RING], i + u // RING)
                        read(0)
                        side(1)
                        drive(2)
                        read(1)
                        side(2)
                        drive(3)
                        read(2)
                        read(3)
                elif kind == "ret":
                    lo = layer_width(l)[0]
                    pe.wait_ge(proj_out, 18 * (l + 1))
                    for j, src in enumerate((qT, kT)):
                        for hd in range(RH):
                            last = mm(ps[:, 2 * j + hd // 2, (hd % 2) * 256:(hd % 2) * 256 + 256],
                                      cst[:, C_PERM:C_PERM + P], src[:, hd, CTX:TL], True, True)
                        last.then_inc(rope_ps, 1)
                    pe.wait_ge(roped, 2 * (l + 1))

                    def outs(hd):
                        b = 3 * (hd % 2)
                        pe.wait_ge(sd_ready, l * RH + hd + 1)
                        if hd >= 2:
                            pe.wait_ge(o_copied, l * RH + hd - 1)
                        ob = ps[:, 6 + hd % 2, :]
                        for t in range(4):
                            last = mm(ob[:, CTX:TL], vN[:, t, hd * P:(hd + 1) * P], sd[:, hd % 2, t, :], t == 0, t == 3)
                        if lo == 0:
                            for t in range(2):
                                last = mm(ob[:, 0:CTX], vN[:, t, hd * P:(hd + 1) * P], sd[:, hd % 2, 4 + t, :],
                                          t == 0, t == 1)
                        last.then_inc(o_ps, 1)

                    for hd in range(RH):
                        b = 3 * (hd % 2)
                        if hd >= 2:
                            pe.wait_ge(sd_ready, l * RH + hd - 1)
                        for t in range(4):
                            last = mm(ps[:, b + t // 2, (t % 2) * 256:(t % 2) * 256 + 256], kT[:, hd, t * P:(t + 1) * P],
                                      qT[:, hd, CTX:TL], True, True)
                        if lo == 0:
                            for t in range(2):
                                last = mm(ps[:, b + 2, t * 256:t * 256 + 256], kT[:, hd, t * P:(t + 1) * P],
                                          qT[:, hd, 0:CTX], True, True)
                        last.then_inc(score_ps, 1)
                        if hd >= 1:
                            outs(hd - 1)
                    outs(RH - 1)
                    pe.wait_ge(osq_ready, l + 1)
                    for hd in range(RH):
                        last = mm(ps[:, hd, lo:TL], cst[:, C_ONES_H:C_ONES_H + P], osq[:, hd, lo:TL], True, True)
                    last.then_inc(omean_ready, 1)
                elif kind == "merge":
                    lo, hi = layer_width(l)
                    w_ = hi - lo
                    pe.wait_ge(ys_ready, l + 1)
                    pe.wait_ge(yr_ready, l + 1)
                    for j in range(MERGE_UNITS):
                        arrived(pe, u + j)
                        if j >= 2:
                            pe.wait_ge(m_ready, KD * l + j - 1)
                        w = slot(u + j, 12, P)
                        for part in range(3):
                            src = gT if part == 2 else uT
                            for c in range(CT):
                                last = mm(ps[:, 2 * part + j % 2, 0:w_], w[:, 4 * part + c, :], src[:, c, lo:hi],
                                          c == 0, c == CT - 1)
                        last.then_inc(used[(u + j) % RING], 1)
                    pe.wait_ge(m_ready, KD * (l + 1))
                    for j in range(OUT_UNITS):
                        v = u + MERGE_UNITS + j
                        arrived(pe, v)
                        if j >= 2:
                            pe.wait_ge(x_ready, X_COUNT[st] + j - 1)
                        w = slot(v, 2 * KD, P)
                        for t in range(2):
                            for c in range(KD):
                                last = mm(ps[:, 2 * (j % 2) + t, 0:w_], w[:, t * KD + c, :], mT[:, c, 0:w_],
                                          c == 0, c == KD - 1)
                        last.then_inc(used[v % RING], 1)
                elif kind == "route":
                    p = passes_before(st)
                    pe.wait_ge(h_ready, norms_before(("norm2", l, h)) + 1)
                    for k in range(WQ_UNITS):
                        arrived(pe, u + k)
                        if k >= 2:
                            pe.wait_ge(qr_ready, WQ_UNITS * p + k - 1)
                        w = slot(u + k, 2 * KD, P)
                        for j in range(2):
                            for c in range(KD):
                                last = mm(ps[:, k % 2, j * 256:j * 256 + 256], w[:, j * KD + c, :], h2T[:, c, :],
                                          c == 0, c == KD - 1)
                        last.then_inc(used[(u + k) % RING], 1)
                    pe.wait_ge(keys_in, 16 * (p + 1))
                    pe.wait_ge(qr_ready, WQ_UNITS * (p + 1))
                    for tb in range(2):
                        for hd in range(NH):
                            last = mm(ps[:, 4 * tb + hd // 2, (hd % 2) * 256:(hd % 2) * 256 + 256],
                                      qrT[:, hd, tb * P:(tb + 1) * P], keys[:, hd, :], True, True)
                        last.then_inc(score_out, 1)
                    for tb in range(2):
                        pe.wait_ge(pick_ready, 2 * p + tb + 1)
                        pe.wait_ge(score_ready, 2 * p + 2)
                        for k in range(3):
                            last = pe.transpose(ps[:, tb, k * P:(k + 1) * P], pick[:, k, :], ident)
                        last.then_inc(pick_ps, 1)
                elif kind == "gates":
                    p = passes_before(st)
                    with pe.Fori(0, 16) as i:
                        for g in range(4):
                            count(pe, gate_ready, i * 4 + (64 * p + g - 3))
                            for t in range(4):
                                pe.wait_ge(hot_ready, i * 16 + (256 * p + 4 * g + t + 1))
                                last = mm(ps[:, 4 + g, t * P:(t + 1) * P], hot[:, 0, t, :], hot[:, 1, t, :], True, True)
                                last.then_inc(gate_ps, 1)
                elif kind == "experts":
                    p = passes_before(st)
                    count(pe, gate_ready, 64 * (p + 1))
                    pe.wait_ge(pick_col, 2 * (p + 1))
                    pe.wait_ge(y_copied, 2 * p) if p else None
                    for b in range(4):
                        mm(ps[:, b, :], zeros[:, :], cst[:, 0:512], True, False)

                    def up(k, i):
                        v = u + k
                        arrived(pe, v, i, RING)
                        w = slot(v, 2 * KD, P)
                        for c in range(KD):
                            last = mm(ps[:, 4 + k % 4, 0:256], w[:, c, :], h2T[:, c, :], c == 0, c == KD - 1)
                        last.then_inc(a_ready, 1)

                    def down(k, i):
                        v = u + k
                        count(pe, w_ready, i * RING + (NK * p + k + 1))
                        val = slot(v, 2 * KD, P)[:, KD:, :].rearrange("p k n -> p (k n)")
                        for tb in range(2):
                            for n in range(2):
                                last = mm(ps[:, 2 * tb + n, :], wT[:, k % 2, tb * P:(tb + 1) * P],
                                          val[:, n * 512:(n + 1) * 512], False, False)
                        last.then_inc(used[v % RING], 1)

                    with pe.Fori(0, NK // RING) as i:
                        up(0, i)
                        for k in range(RING):
                            if k < RING - 1:
                                up(k + 1, i)
                            down(k, i)
                    for b in range(4):
                        last = mm(ps[:, b, :], zeros[:, :], cst[:, 0:512], False, True)
                    last.then_inc(y_ready, 1)
                    for tb in range(2):
                        pe.wait_ge(y_copied, 2 * p + tb + 1)
                        for d in range(KD):
                            last = pe.transpose(ps[:, 4 + d // 2, (d % 2) * 256 + tb * P:(d % 2) * 256 + tb * P + P],
                                                yout[:, tb, d * P:(d + 1) * P], ident)
                    last.then_inc(y_col, 1)

        @block.scalar
        def _(act):
            own = Chain(act, act_own)
            act.wait_ge(const_in, 48)

            def squares(st, sqb, lo, w):
                act.activation(sqb[:, :, :], xT[:, :, lo:lo + w], ACT.Square).then_inc(sq_ready, 1)

            def stddev(st, rs, w):
                n = norms_before(st)
                act.wait_ge(mean_ready, n + 1)
                act.activation(rs[:, 0:w], ps[:, 7, 0:w], ACT.Sqrt, bias=eps).then_inc(std_ready, 1)

            for st in stages:
                kind, l, h = st
                u = BASE[st]
                if kind == "mod":
                    act.activation(par[:, N_C:N_C + 16], par[:, N_C:N_C + 16], ACT.Silu).then_inc(cond_ready, 1)
                    own.link(act.activation(lg[:, :], par[:, N_DEC:N_DEC + 16], ACT.Exp))
                    own.link(act.activation(lg[:, :], lg[:, :], ACT.Copy, scale=-1.0))
                    act.activation(s5p[:, S_DT, :], par[:, N_LAM + 128:N_LAM + 192], ACT.Exp).then_inc(s5_lam, 1)
                    act.wait_ge(s5_angle, 1)
                    act.activation(s5p[:, S_R, :], s5p[:, S_T0, :], ACT.Exp)
                    act.activation(s5p[:, S_SIN, :], s5p[:, S_T1, :], ACT.Sin)
                    act.activation(s5p[:, S_COS, :], s5p[:, S_T2, :], ACT.Sin, scale=-1.0,
                                   bias=cst[:, C_HPI:C_HPI + 1]).then_inc(s5_trig, 1)
                    for ll in range(DEPTH):
                        if ll:
                            act.wait_ge(mod_col, ll)
                        with act.Fori(0, MOD_UNITS // RING) as i:
                            for k in range(RING):
                                unit_used(act, ll * MOD_UNITS + k, i, RING)
                                act.activation(mrow[0:2, bass.ds(i * (256 * RING) + 256 * k, 256)],
                                               ps[0:2, k, 0:256], ACT.Copy).then_inc(mod_row, 1)
                elif kind == "norm1":
                    if l:
                        act.wait_ge(x_ready, X_COUNT[st])
                    else:
                        act.wait_ge(mod_done, DEPTH)
                    squares(st, sq1, 0, TL)
                    stddev(st, rs1, TL)
                elif kind == "norm2" or kind == "final":
                    act.wait_ge(x_ready, X_COUNT[st])
                    squares(st, sq2, CTX * h, 256)
                    stddev(st, rs2, 256)
                elif kind == "front":
                    for k in range(FRONT_UNITS):
                        unit_used(act, u + k)
                        b = 2 * (k % 2)
                        if k in (2, 3):
                            dst = vN[:, :, (k - 2) * 256:(k - 1) * 256]
                            src = ps[:, b:b + 2, :].rearrange("p b (t c) -> p (b t) c", c=256)
                        elif k < 2:
                            dst, src = uT[:, 2 * k:2 * k + 2, :], ps[:, b:b + 2, :]
                        else:
                            dst, src = kT[:, 2 * k - 8:2 * k - 6, :], ps[:, b:b + 2, :]
                        act.activation(dst, src, ACT.Copy).then_inc(proj_out, 1)
                elif kind == "s5":
                    lo, hi = layer_width(l)
                    w_ = hi - lo
                    with act.Fori(0, S5_ITER) as i:
                        own.loop(i, 8)
                        for q in range(4):
                            act.wait_ge(bu_ready, i * 4 + (l * 16 + q + 1))
                            count(act, g_ready, i * 8 + (l * 32 + 2 * q - 2))
                            act.activation(bu[:, q % 2, :, :], ps[:, 4:6, :], ACT.Copy).then_inc(bu_copied, 1)
                            for d in range(2):
                                n = 2 * q + d
                                act.wait_ge(phase_ready, i * 8 + (l * 32 + n + 1))
                                count(act, prod_ready, i * 8 + (l * 32 + n - 1))
                                count(act, table_ready, i * 8 + (l * 32 + n))
                                own.link(act.activation(absp[:, :], phase[:, d, :], ACT.Abs))
                                act.activation(tab[:, d, 0, :], absp[:, :], ACT.Sin, scale=-TWO_PI_IN,
                                               bias=cst[:, C_HPI:C_HPI + 1])
                                act.activation(tab[:, d, 1, :], phase[:, d, :], ACT.Sin, scale=TWO_PI_IN
                                               ).then_inc(table_ready, 1)
                            if q < 3:
                                unit_used(act, u + 1 + q, i, 4)
                                b = 2 * (q % 2)
                                act.activation(pj[:, bass.ds(i * 6 + 2 * q, 2), lo:hi], ps[:, b:b + 2, 0:w_],
                                               ACT.Copy).then_inc(proj_out, 1)
                        own.end(S5_ITER)
                elif kind == "ret":
                    lo, hi = layer_width(l)
                    dist = slot(u, 4, 512)
                    act.wait_ge(decay_arg, l + 1)
                    act.activation(decay[:, :, 0, :], decay[:, :, 0, :], ACT.Exp)
                    for hd in range(RH):
                        f, b = 2 * l * RH + hd, (2 * l + 1) * RH + hd
                        act.activation(decay[:, hd, 1, :], dist[:, 2, :], ACT.Exp, scale=lg[:, f:f + 1])
                        last = act.activation(dtmp[:, hd, :], dist[:, 3, :], ACT.Exp, scale=lg[:, b:b + 1])
                    last.then_inc(decay_ready, 1)
                    for hd in range(RH):
                        act.wait_ge(o_ps, l * RH + hd + 1)
                        act.activation(oT[:, hd, lo:hi], ps[:, 6 + hd % 2, lo:hi], ACT.Copy).then_inc(o_copied, 1)
                    act.wait_ge(o_copied, RH * (l + 1))
                    act.activation(osq[:, :, lo:hi], oT[:, :, lo:hi], ACT.Square).then_inc(osq_ready, 1)
                    act.wait_ge(omean_ready, l + 1)
                    act.activation(osq[:, :, lo:hi], ps[:, 0:4, lo:hi], ACT.Sqrt, bias=eps).then_inc(ostd_ready, 1)
                    unit_used(act, BASE[("s5", l, 0)] + 12)
                    act.activation(uT[:, :, lo:hi], uT[:, :, lo:hi], ACT.Gelu_apprx_tanh).then_inc(ys_ready, 1)
                    act.activation(gT[:, :, lo:hi], gT[:, :, lo:hi], ACT.Silu).then_inc(gates_on, 1)
                    act.activation(pj[:, 8:24, lo:hi], pj[:, 8:24, lo:hi], ACT.Sigmoid).then_inc(gates_on, 1)
                elif kind == "merge":
                    lo, hi = layer_width(l)
                    w_ = hi - lo
                    act.wait_ge(yr_ready, l + 1)
                    for j in range(MERGE_UNITS):
                        unit_used(act, u + j)
                        if j >= 2:
                            act.wait_ge(m_ready, KD * l + j - 1)
                        act.activation(sgb[:, j % 2, 0:w_], ps[:, 2 + j % 2, 0:w_], ACT.Sigmoid).then_inc(sg_ready, 1)
                elif kind == "route":
                    p = passes_before(st)
                    for k in range(WQ_UNITS):
                        unit_used(act, u + k)
                        act.activation(qrT[:, 2 * k:2 * k + 2, :],
                                       ps[:, k % 2, :].rearrange("p (a b) -> p a b", a=2), ACT.Copy).then_inc(qr_ready, 1)
                    for tb in range(2):
                        act.wait_ge(score_out, 2 * p + tb + 1)
                        act.activation(sc[:, tb, :, :], ps[:, 4 * tb:4 * tb + 4, :], ACT.Copy).then_inc(score_ready, 1)
                    for tb in range(2):
                        act.wait_ge(exp_in, 2 * p + tb + 1)
                        act.activation(best[:, :, :], best[:, :, :], ACT.Exp).then_inc(exp_out, 1)
                    for tb in range(2):
                        act.wait_ge(pick_ps, 2 * p + tb + 1)
                        act.activation(idxT[:, :, tb * P:(tb + 1) * P],
                                       ps[:, tb, 0:3 * P].rearrange("p (a b) -> p a b", a=3), ACT.Copy
                                       ).then_inc(pick_col, 1)
                elif kind == "gates":
                    p = passes_before(st)
                    with act.Fori(0, 16) as i:
                        for g in range(4):
                            count(act, gate_ps, i * 16 + (256 * p + 4 * g + 4))
                            src = ps[:, 4 + g, :].rearrange("p (t n) -> p n t", n=P)
                            act.activation(gate[:, :, bass.ds(i * 16 + 4 * g, 4)], src, ACT.Copy).then_inc(gate_ready, 1)
                elif kind == "experts":
                    p = passes_before(st)
                    with act.Fori(0, NK // RING) as i:
                        for k in range(RING):
                            act.wait_ge(a_ready, i * RING + (NK * p + k + 1))
                            count(act, w_ready, i * RING + (NK * p + k - 1))
                            act.activation(actT[:, k % 2, :], ps[:, 4 + k % 4, 0:256], ACT.Gelu).then_inc(act_ready, 1)
                    act.wait_ge(y_ready, p + 1)
                    for tb in range(2):
                        act.activation(yout[:, tb, :], ps[:, 2 * tb:2 * tb + 2, :], ACT.Copy).then_inc(y_copied, 1)

        @block.vector
        def _(dve):
            own = Chain(dve, dve_own)
            link = own.link
            v = nc.vector
            dve.wait_ge(const_in, 48)
            for s_ in (readout, g_ready, table_ready, prod_ready, bu_copied, mod_row, gate_ready, gate_ps, w_ready):
                dve.sem_inc(s_, CREDIT[s_.name])

            def sp_(k):
                return s5p[:, k, :]

            def normed(st, rs, w, dst, lo, which):
                n = norms_before(st)
                dve.wait_ge(std_ready, n + 1)
                link(v.reciprocal(rs[:, 0:w], rs[:, 0:w]))
                halves = range(w // 256)
                for k in range(KD):
                    for hf in halves:
                        side = hf if w > 256 else lo // CTX
                        s_ = slice(hf * 256, hf * 256 + 256)
                        last = v.scalar_tensor_tensor(dst[:, k, s_], xT[:, k, lo + hf * 256:lo + hf * 256 + 256],
                                                      which[0](k, side), rs[:, s_], ALU.mult, ALU.mult)
                if which[1] is None:
                    return last
                link(last)
                for k in range(KD):
                    for hf in halves:
                        side = hf if w > 256 else lo // CTX
                        s_ = slice(hf * 256, hf * 256 + 256)
                        last = v.tensor_scalar(dst[:, k, s_], dst[:, k, s_], which[1](k, side), None, ALU.add)
                return last

            for st in stages:
                kind, l, h = st
                u = BASE[st]
                if kind == "mod":
                    v.memset(zeros[:, :], 0.0)
                    lr, li = par[:, N_LAM:N_LAM + 64], par[:, N_LAM + 64:N_LAM + 128]
                    dve.wait_ge(s5_lam, 1)
                    link(v.tensor_tensor(sp_(S_TH), li, sp_(S_DT), ALU.mult))
                    v.tensor_tensor(sp_(S_T0), lr, sp_(S_DT), ALU.mult)
                    link(v.tensor_scalar(s5k[:, :], sp_(S_TH), INV2PI, None, ALU.mult))
                    link(v.tensor_copy(sp_(S_K), s5k[:, :]))
                    for part in (TP1, TP2, TP3):
                        link(v.scalar_tensor_tensor(sp_(S_TH), sp_(S_K), -part, sp_(S_TH), ALU.mult, ALU.add))
                    link(v.tensor_scalar(sp_(S_TH), sp_(S_TH), 3.1415925, -3.1415925, ALU.min, ALU.max))
                    link(v.tensor_scalar(sp_(S_RHO), sp_(S_TH), INV2PI, None, ALU.mult))
                    link(v.tensor_scalar(s5k[:, :], sp_(S_RHO), 32768.0, None, ALU.mult))
                    link(v.tensor_scalar(sp_(S_RHI), s5k[:, :], 1.0 / 32768.0, None, ALU.mult))
                    link(v.scalar_tensor_tensor(sp_(S_RLO), sp_(S_RHI), -TP1, sp_(S_TH), ALU.mult, ALU.add))
                    link(v.scalar_tensor_tensor(sp_(S_RLO), sp_(S_RHI), -TP2, sp_(S_RLO), ALU.mult, ALU.add))
                    link(v.tensor_scalar(sp_(S_RLO), sp_(S_RLO), INV2PI, None, ALU.mult))
                    link(v.tensor_copy(sp_(S_T1), sp_(S_TH)))
                    link(v.tensor_scalar(sp_(S_T2), sp_(S_TH), -1.0, None, ALU.mult))
                    v.tensor_tensor(sp_(S_T2), sp_(S_T2), sp_(S_TH), ALU.max).then_inc(s5_angle, 1)
                    dve.wait_ge(s5_trig, 1)
                    link(v.tensor_tensor(sp_(S_COS), sp_(S_COS), sp_(S_R), ALU.mult))
                    link(v.tensor_tensor(sp_(S_SIN), sp_(S_SIN), sp_(S_R), ALU.mult))
                    link(v.tensor_scalar(sp_(S_COS), sp_(S_COS), -1.0, None, ALU.add))
                    link(v.tensor_tensor(sp_(S_T0), lr, lr, ALU.mult))
                    link(v.tensor_tensor(sp_(S_T1), li, li, ALU.mult))
                    link(v.tensor_tensor(sp_(S_T0), sp_(S_T0), sp_(S_T1), ALU.add))
                    link(v.reciprocal(sp_(S_T2), sp_(S_T0)))
                    link(v.tensor_tensor(sp_(S_T0), sp_(S_COS), lr, ALU.mult))
                    link(v.tensor_tensor(sp_(S_T1), sp_(S_SIN), li, ALU.mult))
                    link(v.tensor_tensor(sp_(S_T0), sp_(S_T0), sp_(S_T1), ALU.add))
                    link(v.tensor_tensor(sp_(S_BR), sp_(S_T0), sp_(S_T2), ALU.mult))
                    link(v.tensor_tensor(sp_(S_T0), sp_(S_SIN), lr, ALU.mult))
                    link(v.tensor_tensor(sp_(S_T1), sp_(S_COS), li, ALU.mult))
                    link(v.tensor_tensor(sp_(S_T0), sp_(S_T0), sp_(S_T1), ALU.subtract))
                    link(v.tensor_tensor(sp_(S_BI), sp_(S_T0), sp_(S_T2), ALU.mult))
                    link(v.tensor_scalar(sp_(S_NBR), sp_(S_BR), -1.0, None, ALU.mult))
                    link(v.tensor_scalar(sp_(S_NBI), sp_(S_BI), -1.0, None, ALU.mult))
                    for ll in range(DEPTH):
                        dve.wait_ge(mod_col, ll + 1)
                        b = par[:, N_BMOD + 48 * ll:N_BMOD + 48 * ll + 48].unsqueeze(2).to_broadcast([P, 48, 2])
                        link(v.tensor_tensor(modT[:, ll, :, :, :].rearrange("p s k c -> p (s k) c"),
                                             ps[:, 4, 0:96].rearrange("p (a c) -> p a c", c=2), b, ALU.add))
                        for n in range(2):
                            g = par[:, N_G + 16 * ll + 8 * n:N_G + 16 * ll + 8 * n + 8].unsqueeze(2).to_broadcast([P, 8, 2])
                            s_ = gain[:, ll, n, :, :]
                            link(v.tensor_scalar(s_, modT[:, ll, 3 * n + 1, :, :], 1.0, None, ALU.add))
                            last = v.tensor_tensor(s_, s_, g, ALU.mult)
                            if n == 0:
                                link(last)
                        last.then_inc(mod_done, 1)
                        dve.wait_ge(mod_done, ll + 1)
                elif kind == "norm1":
                    normed(st, rs1, TL, hT, 0,
                           (lambda k, s: gain[:, l, 0, k, s:s + 1], lambda k, s: modT[:, l, 0, k, s:s + 1])
                           ).then_inc(h_ready, 1)
                elif kind == "norm2":
                    normed(st, rs2, 256, h2T, CTX * h,
                           (lambda k, s: gain[:, l, 1, k, s:s + 1], lambda k, s: modT[:, l, 3, k, s:s + 1])
                           ).then_inc(h_ready, 1)
                elif kind == "final":
                    normed(st, rs2, 256, fout, CTX,
                           (lambda k, s: par[:, N_FG + k:N_FG + k + 1], None)).then_inc(fin_ready, 1)
                elif kind == "s5":
                    lo, hi = layer_width(l)
                    w_ = hi - lo
                    with dve.Fori(0, S5_ITER) as i:
                        own.loop(i, S5_LINKS)
                        C = ring[:, u % RING, 8 * P:8 * P + 8 * 32].rearrange("p (q c n) -> p q c n", q=4, c=2)

                        def lane(k, n):
                            return s5p[:, k, bass.ds(i * 4 + ((2 * l + n % 2) * NT + n // 2), 1)]

                        def phases(n):
                            d = n % 2
                            t = cst[:, C_T:C_T + TL]
                            count(dve, table_ready, i * 8 + (l * 32 + n - 1))
                            link(v.tensor_scalar(turns[:, :], t, lane(S_RHO, n), None, ALU.mult))
                            link(v.scalar_tensor_tensor(phase[:, d, :], t, lane(S_RHI, n), turns[:, :], ALU.mult, ALU.subtract))
                            link(v.scalar_tensor_tensor(phase[:, d, :], t, lane(S_RLO, n), phase[:, d, :], ALU.mult, ALU.add))
                            v.tensor_scalar(phase[:, d, :], phase[:, d, :], 0.5, -0.5, ALU.min, ALU.max
                                            ).then_inc(phase_ready, 1)

                        phases(0)
                        arrived(dve, u, i, 4)
                        for n in range(8):
                            q, d = n // 2, n % 2
                            if n < 7:
                                phases(n + 1)
                            count(dve, readout, i * 8 + (l * 32 + n - 1))
                            v.tensor_scalar(ctmp[:, 0, :], C[:, q, 1, :], lane(S_NBI, n), None, ALU.mult)
                            link(v.tensor_scalar(ctmp[:, 1, :], C[:, q, 1, :], lane(S_NBR, n), None, ALU.mult))
                            link(v.scalar_tensor_tensor(cpr[:, d, 0, :], C[:, q, 0, :], lane(S_BR, n), ctmp[:, 0, :], ALU.mult, ALU.add))
                            v.tensor_scalar(cpr[:, d, 1, :], cpr[:, d, 0, :], -1.0, None, ALU.mult)
                            v.scalar_tensor_tensor(cpr[:, d, 2, :], C[:, q, 0, :], lane(S_NBI, n), ctmp[:, 1, :], ALU.mult, ALU.add
                                                   ).then_inc(cprime_ready, 1)
                            count(dve, table_ready, i * 8 + (l * 32 + n + 1))
                            count(dve, bu_copied, i * 4 + (l * 16 + q + 1))
                            T, G = tab[:, d, :, :], gst[:, d, :, :]

                            def turned(dst, t):
                                for c in range(2):
                                    b_ = bu[:, q % 2, c, :]
                                    if d:
                                        b_ = b_.rearrange("p (h t) -> p h t", t=256)[:, :, ::-1]
                                        v_ = v.tensor_tensor(dst[:, c, :].rearrange("p (h t) -> p h t", t=256), b_,
                                                             t[:, c, :].rearrange("p (h t) -> p h t", t=256), ALU.mult)
                                    else:
                                        v_ = v.tensor_tensor(dst[:, c, :], b_, t[:, c, :], ALU.mult)
                                return v_

                            own.mark(turned(rot[:, 0, :, :], T))
                            link(turned(rot[:, 1, :, :], T[:, ::-1, :]))
                            own.mark(v.tensor_tensor(G[:, 0, :], rot[:, 0, 0, :], rot[:, 0, 1, :], ALU.add))
                            link(v.tensor_tensor(G[:, 1, :], rot[:, 1, 1, :], rot[:, 1, 0, :], ALU.subtract))
                            r = lane(S_R, n).to_broadcast([P, TL])
                            for c in range(2):
                                last = v.tensor_tensor_scan(G[:, c, :], r, G[:, c, :], 0.0, ALU.mult, ALU.add)
                            last.then_inc(g_ready, 1)
                        count(dve, readout, i * 8 + (l * 32 + 8))
                        uq = uT[:, bass.ds(i, 1), lo:hi].rearrange("p o t -> p (o t)")
                        v.scalar_tensor_tensor(uq, uq, par[:, bass.ds(i + (N_D + 4 * l), 1)], ps[:, 6, 0:w_],
                                               ALU.mult, ALU.add).then_inc(used[u % RING], 1)
                        own.end(S5_ITER)
                elif kind == "ret":
                    lo, hi = layer_width(l)
                    dist = slot(u, 4, 512)
                    arrived(dve, u)
                    for hd in range(RH):
                        b = (2 * l + 1) * RH + hd
                        last = v.tensor_scalar(dtmp[:, hd, :], dist[:, 1, :], lg[:, b:b + 1], None, ALU.mult)
                    link(last)
                    for hd in range(RH):
                        f = 2 * l * RH + hd
                        last = v.scalar_tensor_tensor(decay[:, hd, 0, :], dist[:, 0, :], lg[:, f:f + 1], dtmp[:, hd, :],
                                                      ALU.mult, ALU.add)
                    last.then_inc(decay_arg, 1)
                    dve.wait_ge(decay_ready, l + 1)
                    v.tensor_tensor(decay[:, :, 1, :], decay[:, :, 1, :], dtmp[:, :, :], ALU.add).then_inc(used[u % RING], 1)
                    for j, src in enumerate((qT, kT)):
                        dve.wait_ge(rope_ps, 2 * l + j + 1)
                        cos = cst[:, C_COS:C_COS + 256].unsqueeze(1).to_broadcast([P, RH, 256])
                        sin = cst[:, C_SIN:C_SIN + 256].unsqueeze(1).to_broadcast([P, RH, 256])
                        pp = ps[:, 2 * j:2 * j + 2, :].rearrange("p b (a t) -> p (b a) t", a=2)
                        own.mark(v.tensor_tensor(oT[:, :, 0:256], pp, sin, ALU.mult))
                        link(v.tensor_tensor(src[:, :, CTX:TL], src[:, :, CTX:TL], cos, ALU.mult))
                        v.tensor_tensor(src[:, :, CTX:TL], src[:, :, CTX:TL], oT[:, :, 0:256], ALU.add).then_inc(roped, 1)
                        dve.wait_ge(roped, 2 * l + j + 1)
                    scale = P ** -0.5
                    for hd in range(RH):
                        b = 3 * (hd % 2)
                        dve.wait_ge(score_ps, l * RH + hd + 1)
                        if hd == 0:
                            unit_used(dve, u)
                        if hd >= 2:
                            dve.wait_ge(o_ps, l * RH + hd - 1)
                        for g, (bank, which) in enumerate(((0, 1), (1, 0), (2, 0))[:3 if lo == 0 else 2]):
                            last = v.scalar_tensor_tensor(
                                sd[:, hd % 2, 2 * g:2 * g + 2, :].rearrange("p a t -> p (a t)"), ps[:, b + bank, :],
                                scale, decay[:, hd, which, :], ALU.mult, ALU.mult)
                        last.then_inc(sd_ready, 1)
                    dve.wait_ge(ostd_ready, l + 1)
                    dve.wait_ge(o_copied, RH * (l + 1))
                    link(v.reciprocal(osq[:, :, lo:hi], osq[:, :, lo:hi]))
                    link(v.tensor_tensor(oT[:, :, lo:hi], oT[:, :, lo:hi], osq[:, :, lo:hi], ALU.mult))
                    dve.wait_ge(gates_on, 2 * l + 2)
                    v.tensor_tensor(gT[:, :, lo:hi], oT[:, :, lo:hi], gT[:, :, lo:hi], ALU.mult).then_inc(yr_ready, 1)
                elif kind == "merge":
                    lo, hi = layer_width(l)
                    w_ = hi - lo
                    for j in range(MERGE_UNITS):
                        dve.wait_ge(sg_ready, KD * l + j + 1)
                        unit_used(dve, u + j)
                        own.mark(v.tensor_tensor(mt1[:, j % 2, 0:w_], ps[:, j % 2, 0:w_], sgb[:, j % 2, 0:w_], ALU.mult))
                        link(v.tensor_tensor(mt2[:, j % 2, 0:w_], ps[:, 4 + j % 2, 0:w_], grT[:, j, lo:hi], ALU.mult))
                        link(v.tensor_tensor(mt1[:, j % 2, 0:w_], mt1[:, j % 2, 0:w_], gsT[:, j, lo:hi], ALU.mult))
                        v.tensor_tensor(mT[:, j, 0:w_], mt1[:, j % 2, 0:w_], mt2[:, j % 2, 0:w_], ALU.add).then_inc(m_ready, 1)
                    for j in range(OUT_UNITS):
                        unit_used(dve, u + MERGE_UNITS + j)
                        for t in range(2):
                            for side in range(lo // CTX, 2):
                                k = 2 * j + t
                                xs = xT[:, k, CTX * side:CTX * side + 256]
                                last = v.scalar_tensor_tensor(
                                    xs, ps[:, 2 * (j % 2) + t, CTX * side - lo:CTX * side - lo + 256],
                                    modT[:, l, 2, k, side:side + 1], xs, ALU.mult, ALU.add)
                        last.then_inc(x_ready, 1)
                elif kind == "route":
                    p = passes_before(st)
                    for tb in range(2):
                        dve.wait_ge(score_ready, 2 * p + tb + 1)
                        for hd in range(NH):
                            S = sc[:, tb, 2 * hd:2 * hd + 2, :]
                            tp = top[:, 2 * hd:2 * hd + 2, :]
                            ti = topi[:, 2 * hd:2 * hd + 2, :]
                            v.max(tp[:, 0, 0:8], S[:, 0, :])
                            link(v.max(tp[:, 1, 0:8], S[:, 1, :]))
                            for s_ in range(2):
                                v.max_index(ti[:, s_, 0:8], tp[:, s_, 0:8], S[:, s_, :])
                            v.match_replace(sc2[:, 0, :], tp[:, 0, 0:8], S[:, 0, :], -3e38)
                            link(v.match_replace(sc2[:, 1, :], tp[:, 1, 0:8], S[:, 1, :], -3e38))
                            v.max(tp[:, 0, 8:16], sc2[:, 0, :])
                            link(v.max(tp[:, 1, 8:16], sc2[:, 1, :]))
                            for s_ in range(2):
                                v.max_index(ti[:, s_, 8:16], tp[:, s_, 8:16], sc2[:, s_, :])
                            a_ = tp[:, 0, :].unsqueeze(2).to_broadcast([P, TOPK, TOPK])
                            b_ = tp[:, 1, :].unsqueeze(1).to_broadcast([P, TOPK, TOPK])
                            link(v.tensor_tensor(cand[:, :].rearrange("p (a b) -> p a b", a=TOPK), a_, b_, ALU.add))
                            be = best[:, hd, :]
                            bi = besti[:, hd, :]
                            link(v.max(be[:, 0:8], cand[:, :]))
                            v.max_index(bi[:, 0:8], be[:, 0:8], cand[:, :])
                            link(v.match_replace(cand2[:, :], be[:, 0:8], cand[:, :], -3e38))
                            link(v.max(be[:, 8:16], cand2[:, :]))
                            link(v.max_index(bi[:, 8:16], be[:, 8:16], cand2[:, :]))
                        top1 = best[:, :, 0:1].to_broadcast([P, NH, TOPK])
                        if tb or p:
                            dve.wait_ge(pick_ps, 2 * p + tb)
                        link(v.tensor_copy(pick[:, 2, :].rearrange("p (h k) -> p h k", h=NH), top1))
                        v.tensor_tensor(best[:, :, :], best[:, :, :], pick[:, 2, :].rearrange("p (h k) -> p h k", h=NH),
                                        ALU.subtract).then_inc(exp_in, 1)
                        v.tensor_copy(topf[:, :, :], topi[:, :, :])
                        bflat = besti[:, :, :].rearrange("p h k -> p (h k)")
                        v.tensor_scalar(bab[:, 0, :], bflat, 4, None, ALU.logical_shift_right)
                        link(v.tensor_scalar(bab[:, 1, :], bflat, 15, None, ALU.bitwise_and))
                        link(v.tensor_copy(babf[:, :, :], bab[:, :, :]))
                        i16 = cst[:, C_I16:C_I16 + TOPK].unsqueeze(1).to_broadcast([P, NH * TOPK, TOPK])
                        for s_ in range(2):
                            last = v.tensor_tensor(eq[:, s_, :, :], babf[:, s_, :].unsqueeze(2).to_broadcast([P, NH * TOPK, TOPK]),
                                                   i16, ALU.is_equal)
                        link(last)
                        for s_ in range(2):
                            e4 = eq[:, s_, :, :].rearrange("p (h k) a -> p h k a", h=NH)
                            t4 = topf[:, s_::2, :].unsqueeze(2).to_broadcast([P, NH, TOPK, TOPK])
                            last = v.tensor_tensor(e4, e4, t4, ALU.mult)
                        link(last)
                        for s_ in range(2):
                            v.tensor_reduce(pick[:, s_, :], eq[:, s_, :, :], AX_X, ALU.add)
                        dve.wait_ge(exp_out, 2 * p + tb + 1)
                        link(v.tensor_reduce(ssum[:, :], best[:, :, :], AX_X, ALU.add))
                        link(v.reciprocal(ssum[:, :], ssum[:, :]))
                        v.tensor_tensor(pick[:, 2, :].rearrange("p (h k) -> p h k", h=NH), best[:, :, :],
                                        ssum[:, :].unsqueeze(2).to_broadcast([P, NH, TOPK]), ALU.mult).then_inc(pick_ready, 1)
                elif kind == "gates":
                    p = passes_before(st)
                    dve.wait_ge(pick_col, 2 * (p + 1))
                    with dve.Fori(0, 16) as i:
                        for k in range(16):
                            count(dve, gate_ps, i * 16 + (256 * p + k - 3))
                            tok = [idxT[:, c, bass.ds(i * 16 + k, 1)] for c in range(3)]
                            v.tensor_scalar(hot[:, 0, k % 4, :], iota, tok[0], None, ALU.is_equal)
                            v.tensor_scalar(hot[:, 1, k % 4, :], iota, tok[1], tok[2], ALU.is_equal, ALU.mult
                                            ).then_inc(hot_ready, 1)
                elif kind == "experts":
                    p = passes_before(st)
                    with dve.Fori(0, NK // RING) as i:
                        for k in range(RING):
                            dve.wait_ge(act_ready, i * RING + (NK * p + k + 1))
                            unit_used(dve, u + k - 2, i, RING)
                            g = gate[:, bass.ds(i * RING + k, 1), :].rearrange("p o t -> p (o t)")
                            v.tensor_tensor(wT[:, k % 2, :], actT[:, k % 2, :], g, ALU.mult).then_inc(w_ready, 1)
                    dve.wait_ge(y_col, p + 1)
                    for k in range(KD):
                        xs = xT[:, k, CTX * h:CTX * h + 256]
                        last = v.scalar_tensor_tensor(xs, ps[:, 4 + k // 2, (k % 2) * 256:(k % 2) * 256 + 256],
                                                      modT[:, l, 5, k, h:h + 1], xs, ALU.mult, ALU.add)
                    last.then_inc(x_ready, 1)


def constants():
    c = np.zeros((P, C_N), np.float32)
    c[:, C_ID:C_ID + P] = np.eye(P)
    c[:, C_ONES_D:C_ONES_D + P] = 1.0 / DM
    c[:, C_ONES_H:C_ONES_H + P] = 1.0 / P
    c[:, C_IOTA:C_IOTA + P] = np.arange(P)
    for m in range(P):
        if m % 64 < 32:
            c[m + 32, C_PERM + m] = -1.0
        else:
            c[m - 32, C_PERM + m] = 1.0
    c[:, C_T:C_T + TL] = np.arange(TL)
    c[:, C_I16:C_I16 + TOPK] = np.arange(TOPK)
    c[:, C_EPS] = EPS
    c[:, C_HPI] = np.float32(1.5707962)
    freqs = np.float32(10000.0) ** (-np.arange(32, dtype=np.float32) / np.float32(32))
    t = np.arange(SEQ)
    for d in range(P):
        at = (t // GRID_W if d < 64 else t % GRID_W).astype(np.float32) * freqs[d % 32]
        c[d, C_COS:C_COS + SEQ] = np.cos(at)
        c[d, C_SIN:C_SIN + SEQ] = np.sin(at)
    s = (np.arange(2)[None, :, None] * P + np.arange(P)[:, None, None]).astype(np.float32)
    tt = np.arange(256, dtype=np.float32)[None, None, :]
    d = np.stack([np.maximum(tt - s, 0), np.maximum(s - tt, 0), 256 + tt - s, 256 - tt + s], 1)
    return c, np.ascontiguousarray(d.reshape(P, 4 * 512), np.float32)


def layouts(i):
    f = lambda k: np.asarray(i[k])
    L = DEPTH
    out = {}
    out["x_t"] = np.concatenate([f("ctx")[0], f("x")[0]]).T.reshape(KD, P, TL).transpose(1, 0, 2)

    def tiles(w, per, n=P):
        k, m = w.shape[1:]
        return w.reshape(L, k // P, P, m // (n * per), per, n).transpose(0, 3, 2, 4, 1, 5)

    out["w_mod"] = tiles(f("w_mod"), 1, 256).reshape(L * MOD_UNITS, P, 2048)
    w_in = f("w_in")
    u, q, k, v, g, gs, gr = np.split(w_in, [512, 1024, 1536, 2048, 2560, 3584], axis=2)
    out["w_front"] = tiles(np.concatenate([u, v, k], 2), 2).reshape(L, FRONT_UNITS, P, 2048)
    out["w_side"] = tiles(np.concatenate([q, g, gs, gr], 2), 2).reshape(L, 12, P, 2048)
    glu, up = f("w_ssm_glu"), f("w_ret_up")
    parts = [tiles(w, 1).reshape(L, 8, P, 512) for w in (glu[:, :, :DM], glu[:, :, DM:], up)]
    out["w_merge"] = np.concatenate(parts, 3)
    out["w_out"] = tiles(f("w_out"), 2).reshape(L, OUT_UNITS, P, 2048)
    out["w_q"] = tiles(f("peer_w_q"), 2).reshape(L, WQ_UNITS, P, 2048)
    bc = np.zeros((L, 4, P, 8 * P + 256), np.float32)
    for c, (B, C) in enumerate((("ssm_B_re", "ssm_C_re"), ("ssm_B_im", "ssm_C_im"))):
        B, C = f(B).reshape(L, 4, 4, 2, 64, 16), f(C).reshape(L, 4, 4, 2, 16, 64)
        for q in range(4):
            for gi in range(2):
                r = 32 * q + 16 * gi
                bc[:, :, r:r + 16, (2 * q + c) * P + 64 * gi:(2 * q + c) * P + 64 * gi + 64] = B[:, :, q, gi].transpose(0, 1, 3, 2)
                at = 8 * P + (2 * q + c) * 32 + 16 * gi
                bc[:, :, 64 * gi:64 * gi + 64, at:at + 16] = C[:, :, q, gi].transpose(0, 1, 3, 2)
    out["s5_bc"] = bc
    keys = np.zeros((L, P, NH, 256), np.float32)
    sk = f("peer_sub_keys")
    for s in range(2):
        keys[:, 64 * s:64 * s + 64, :, P * s:P * s + P] = sk[:, :, s].transpose(0, 3, 1, 2)
    out["keys"] = keys
    ut = f("peer_u").reshape(L, NK, NK, KD, P).transpose(0, 2, 4, 3, 1).reshape(L, NK, P, DM)
    vt = f("peer_v").reshape(L, NK, NK, DM).transpose(0, 2, 1, 3)
    out["experts"] = np.concatenate([ut, vt], 3)
    p = np.zeros((P, N_N), np.float32)
    col = lambda w, n: w.reshape(L, n, P).transpose(2, 0, 1).reshape(P, L * n)
    p[:, N_BMOD:N_BMOD + 96] = col(f("b_mod"), 48)
    p[:, N_G:N_G + 32] = np.stack([f("norm1_g"), f("norm2_g")], 1).reshape(L, 2, 8, P).transpose(3, 0, 1, 2).reshape(P, 32)
    p[:, N_FG:N_FG + 8] = f("final_norm_g").reshape(8, P).T
    dirs = lambda w: np.stack([f(w + "_f"), f(w + "_b")], 1)
    lanes = lambda w: w.reshape(L, 2, NT, P).transpose(3, 0, 1, 2).reshape(P, 64)
    p[:, N_LAM:N_LAM + 64] = lanes(dirs("ssm_lam_re"))
    p[:, N_LAM + 64:N_LAM + 128] = lanes(dirs("ssm_lam_im"))
    p[:, N_LAM + 128:N_LAM + 192] = lanes(np.repeat(dirs("ssm_log_dt"), 64, axis=2))
    p[:, N_DEC:N_DEC + 16] = dirs("ret_decay").reshape(1, 16)
    p[:, N_D:N_D + 8] = col(f("ssm_D"), 4)
    p[:, N_C:N_C + 16] = np.stack([f("c_ctx"), f("c")[0]], 1).reshape(8, P, 2).transpose(1, 0, 2).reshape(P, 16)
    out["params"] = p
    out["consts"], out["dist"] = constants()
    return {k: np.ascontiguousarray(a, np.float32) if a.dtype != np.float32 else np.ascontiguousarray(a) for k, a in out.items()}


def kernel(**inputs):
    import concourse.bacc as bacc
    from concourse.bass_utils import run_bass_kernel_spmd

    nc = bacc.Bacc("TRN2", target_bir_lowering=False, num_devices=1)
    arrays = layouts(inputs)
    aps = {k: nc.dram_tensor(f"in_{k}", a.shape, F32, kind="ExternalInput").ap() for k, a in arrays.items()}
    aps["out"] = nc.dram_tensor("out_t", (P, KD, SEQ), F32, kind="ExternalOutput").ap()
    build_program(nc, aps)
    r = run_bass_kernel_spmd(nc, [{f"in_{k}": a for k, a in arrays.items()}], core_ids=[0])
    got = r.results[0]["out_t"]
    return np.ascontiguousarray(got.transpose(1, 0, 2).reshape(DM, SEQ).T)[None]
```

```python
import math
from contextlib import ExitStack

import concourse.bass as bass
import numpy as np
from concourse import mybir

P = 128
DM = 1024
KD = DM // P
CTX, SEQ = 256, 256
TL = CTX + SEQ
DEPTH = 2
SSM = 512
NT = 16
CT = SSM // P
RH = 4
GRID_W = 64
EPS = 1e-6
NH, NK, TOPK = 8, 128, 16
HALF = 64
RING = 4
SLOT = 2048
MOD_UNITS = 24
FRONT_UNITS = 6
DIST_UNIT = 1
S5_ITER = 4
MERGE_UNITS, OUT_UNITS, WQ_UNITS = 8, 4, 4

F32 = mybir.dt.float32
F32R = mybir.dt.float32r
I32 = mybir.dt.int32
U32 = mybir.dt.uint32
ALU = mybir.AluOpType
ACT = mybir.ActivationFunctionType
AX_X = mybir.AxisListType.X

C_ID, C_ONES_D, C_ONES_H, C_IOTA, C_PERM, C_I16, C_EPS, C_HPI = 0, 128, 256, 384, 512, 640, 656, 657
C_N = 658
M_T, M_COS, M_SIN, M_N = 0, TL, TL + SEQ, TL + 2 * SEQ
N_BMOD, N_G, N_FG, N_LAM, N_DEC, N_D, N_C = 0, 96, 128, 136, 328, 344, 352
N_N = 368
TP1 = 6.28125
TP2 = float(np.float32(2 * math.pi - TP1))
TP3 = float(np.float32(2 * math.pi - TP1 - float(np.float32(2 * math.pi - TP1))))
INV2PI = float(np.float32(1 / (2 * math.pi)))
TWO_PI_IN = 6.283185
S_R, S_RHO, S_RHI, S_RLO, S_BR, S_BI, S_NBR, S_NBI = range(8)
S_DT, S_TH, S_T0, S_T1, S_T2, S_COS, S_SIN, S_K = range(8, 16)

STAGES = [("mod", 0, 0)]
for _l in range(DEPTH):
    STAGES += [("norm1", _l, 0), ("front", _l, 0), ("s5", _l, 0), ("ret", _l, 0), ("merge", _l, 0)]
    for _h in ((1, 0) if _l < DEPTH - 1 else (1,)):
        STAGES += [("norm2", _l, _h), ("route", _l, _h), ("gates", _l, _h), ("experts", _l, _h)]
STAGES += [("final", 0, 1)]


def next_mod(stage):
    return stage == ("route", 0, 1)


def units_of(stage):
    return {"mod": MOD_UNITS, "front": FRONT_UNITS, "s5": 4 * S5_ITER, "ret": DIST_UNIT,
            "merge": MERGE_UNITS + OUT_UNITS, "route": WQ_UNITS + MOD_UNITS * next_mod(stage), "experts": NK}.get(stage[0], 0)


def first_units():
    base, out = 0, {}
    for st in STAGES:
        out[st] = base
        base += units_of(st)
    return out


BASE = first_units()
X_COUNT, _n = {}, 0
for _st in STAGES:
    X_COUNT[_st] = _n
    _n += OUT_UNITS if _st[0] == "merge" else _st[0] == "experts"
S5_LINKS = 72


def passes_before(st):
    return [s for s in STAGES if s[0] == "norm2"].index(("norm2", st[1], st[2]))


def norms_before(st):
    return [s for s in STAGES if s[0] in ("norm1", "norm2", "final")].index(st)


class Chain:

    def __init__(self, eng, sem):
        self.eng, self.sem, self.n, self.extra = eng, sem, 0, None

    def value(self):
        return self.n if self.extra is None else self.extra + self.n

    def link(self, ins):
        self.mark(ins)
        self.eng.wait_ge(self.sem, self.value())

    def mark(self, ins):
        ins.then_inc(self.sem, 1)
        self.n += 1

    def loop(self, i, per):
        self.start, self.per, self.extra = self.n, per, i * per

    def end(self, turns):
        assert self.n - self.start == self.per, (self.n - self.start, self.per)
        self.n, self.extra = self.start + turns * self.per, None


def build_program(nc, a, until=None):
    stages = STAGES if until is None else STAGES[:until]
    ctx = ExitStack()
    with ctx:
        def sb(name, shape, dt=F32, on=ctx):
            return on.enter_context(nc.sbuf_tensor(name, shape, dt))

        def sem(name):
            return ctx.enter_context(nc.semaphore(name))

        lend = ExitStack()
        xT = sb("xT", [P, KD, TL], on=lend)
        lend.close()
        ehi = sb("ehi", [P, 4, DM], F32R)
        cst = sb("cst", [P, C_N])
        par = sb("par", [P, N_N])
        s5p = sb("s5p", [P, 8, DEPTH * 2 * NT])
        lg = sb("lg", [P, DEPTH * 2 * RH])
        modT = sb("modT", [P, DEPTH, 6, KD, 2])
        gain = sb("gain", [P, DEPTH, 2, KD, 2])
        lend = ExitStack()
        ring = sb("ring", [P, RING, SLOT], on=lend)
        lend.close()
        elo = sb("elo", [P, RING, SLOT], F32R)
        zeros = sb("zeros", [P, P])
        mix = ExitStack()
        mcst = sb("mcst", [P, M_N], on=mix)
        hT = sb("hT", [P, KD, TL], on=mix)
        uT = sb("uT", [P, CT, TL], on=mix)
        vN = sb("vN", [P, TL // P, SSM], on=mix)
        kT = sb("kT", [P, RH, TL], on=mix)
        pj = sb("pj", [P, 24, TL], on=mix)
        qT, gT, gsT, grT = pj[:, 0:4, :], pj[:, 4:8, :], pj[:, 8:16, :], pj[:, 16:24, :]
        sub = ExitStack()
        mrow0 = sb("mrow0", [2, 6 * DM], on=sub)
        s5w = sb("s5w", [P, 8, DEPTH * 2 * NT], on=sub)
        s5k = sb("s5k", [P, DEPTH * 2 * NT], I32, on=sub)
        sub.close()
        sub = ExitStack()
        sq1 = sb("sq1", [P, KD, TL], on=sub)
        rs1 = sb("rs1", [P, TL], on=sub)
        sub.close()
        sub = ExitStack()
        phase = sb("phase", [P, 2, TL], on=sub)
        turns = sb("turns", [P, TL], I32, on=sub)
        absp = sb("absp", [P, TL], on=sub)
        tab = sb("tab", [P, 2, 2, TL], on=sub)
        bu = sb("bu", [P, 2, 2, TL], on=sub)
        rot = sb("rot", [P, 2, 2, TL], on=sub)
        gst = sb("gst", [P, 2, 2, TL], on=sub)
        prod = sb("prod", [P, 2, 4, TL], on=sub)
        cpr = sb("cpr", [P, 2, 3, 32], on=sub)
        ctmp = sb("ctmp", [P, 2, 32], on=sub)
        sub.close()
        sub = ExitStack()
        decay = sb("decay", [P, RH, 2, 512], on=sub)
        dtmp = sb("dtmp", [P, RH, 512], on=sub)
        sd = sb("sd", [P, 2, 6, 256], on=sub)
        oT = sb("oT", [P, RH, TL], on=sub)
        osq = sb("osq", [P, RH, TL], on=sub)
        sub.close()
        sub = ExitStack()
        mT = sb("mT", [P, KD, TL], on=sub)
        sgb = sb("sgb", [P, 2, TL], on=sub)
        mt1 = sb("mt1", [P, 2, TL], on=sub)
        mt2 = sb("mt2", [P, 2, TL], on=sub)
        sub.close()
        mix.close()
        peer = ExitStack()
        h2h = sb("h2h", [P, KD, 256], F32R, on=peer)
        h2l = sb("h2l", [P, KD, 256], F32R, on=peer)
        tiny = ExitStack()
        idxT = sb("idxT", [P, 3, 256], on=tiny)
        hot = sb("hot", [P, 2, 4, P], on=tiny)
        tiny.close()
        tiny = ExitStack()
        actT = sb("actT", [P, 2, 256], on=tiny)
        wf = sb("wf", [P, 2, 256], on=tiny)
        wh = sb("wh", [P, 2, 256], F32R, on=tiny)
        wl = sb("wl", [P, 2, 256], F32R, on=tiny)
        tiny.close()
        sb("tiny_space", [P, 4 * 2 * 256], on=peer)
        over = ExitStack()
        gate = sb("gate", [P, NK, 256], on=over)
        over.close()
        over = ExitStack()
        sq2 = sb("sq2", [P, KD, 256], on=over)
        rs2 = sb("rs2", [P, 256], on=over)
        h2T = sb("h2T", [P, KD, 256], on=over)
        mrow1 = sb("mrow1", [2, 6 * DM], on=over)
        qrT = sb("qrT", [P, NH, 256], on=over)
        keys = sb("keys", [P, NH, 256], on=over)
        sc = sb("sc", [P, 2, NH * 2, NK], on=over)
        sc2 = sb("sc2", [P, 2, NK], on=over)
        cand = sb("cand", [P, 256], on=over)
        cand2 = sb("cand2", [P, 256], on=over)
        top = sb("top", [P, NH * 2, TOPK], on=over)
        topi = sb("topi", [P, NH * 2, TOPK], U32, on=over)
        topf = sb("topf", [P, NH * 2, TOPK], on=over)
        best = sb("best", [P, NH, TOPK], on=over)
        besti = sb("besti", [P, NH, TOPK], U32, on=over)
        bab = sb("bab", [P, 2, NH * TOPK], U32, on=over)
        babf = sb("babf", [P, 2, NH * TOPK], on=over)
        eq = sb("eq", [P, 2, NH * TOPK, TOPK], on=over)
        pick = sb("pick", [P, 3, NH * TOPK], on=over)
        ssum = sb("ssum", [P, NH], on=over)
        over.close()
        over = ExitStack()
        yout = sb("yout", [P, 2, DM], on=over)
        over.close()
        over = ExitStack()
        fout = sb("fout", [P, KD, 256], on=over)
        over.close()
        peer.close()
        ps = ctx.enter_context(nc.psum_tensor("ps", [P, 8, 512], F32))

        const_in = sem("const_in")
        unit_in = [sem(f"unit_in{s}") for s in range(RING)]
        keys_in = sem("keys_in")
        mcst_in = sem("mcst_in")
        x_held, x_back = sem("x_held"), sem("x_back")
        stored = sem("stored")
        used = [sem(f"used{s}") for s in range(RING)]
        dve_own, act_own = sem("dve_own"), sem("act_own")
        cond_ready, mod_row, mod_col, mod_done = sem("cond_ready"), sem("mod_row"), sem("mod_col"), sem("mod_done")
        s5_lam, s5_angle, s5_trig = sem("s5_lam"), sem("s5_angle"), sem("s5_trig")
        sq_ready, mean_ready, std_ready, h_ready = sem("sq_ready"), sem("mean_ready"), sem("std_ready"), sem("h_ready")
        proj_out = sem("proj_out")
        bu_ready, bu_copied = sem("bu_ready"), sem("bu_copied")
        phase_ready, table_ready = sem("phase_ready"), sem("table_ready")
        g_ready, prod_ready, cprime_ready, readout = sem("g_ready"), sem("prod_ready"), sem("cprime_ready"), sem("readout")
        rope_ps, roped = sem("rope_ps"), sem("roped")
        decay_arg, decay_ready = sem("decay_arg"), sem("decay_ready")
        score_ps, sd_ready, o_ps, o_copied = sem("score_ps"), sem("sd_ready"), sem("o_ps"), sem("o_copied")
        osq_ready, omean_ready, ostd_ready, yr_ready, ys_ready = (
            sem("osq_ready"), sem("omean_ready"), sem("ostd_ready"), sem("yr_ready"), sem("ys_ready"))
        gates_on, sg_ready, m_ready, x_ready = sem("gates_on"), sem("sg_ready"), sem("m_ready"), sem("x_ready")
        qr_ready, score_out, score_ready = sem("qr_ready"), sem("score_out"), sem("score_ready")
        exp_in, exp_out, pick_ready, pick_ps, pick_col = (
            sem("exp_in"), sem("exp_out"), sem("pick_ready"), sem("pick_ps"), sem("pick_col"))
        hot_ready, gate_ps, gate_ready = sem("hot_ready"), sem("gate_ps"), sem("gate_ready")
        uhi_ready, ulo_ready, vhi_ready, vlo_ready = sem("uhi_ready"), sem("ulo_ready"), sem("vhi_ready"), sem("vlo_ready")
        a_ready, act_ready, w_ready, y_ready, y_col = (
            sem("a_ready"), sem("act_ready"), sem("w_ready"), sem("y_ready"), sem("y_col"))
        y_copied = sem("y_copied")
        fin_ready = sem("fin_ready")

        ident = cst[:, C_ID:C_ID + P]
        iota = cst[:, C_IOTA:C_IOTA + P]
        eps = cst[:, C_EPS:C_EPS + 1]

        def sp_(k):
            return s5p[:, k, :] if k < 8 else s5w[:, k - 8, :]

        def arrived(eng, u, i=None, per=0):
            n = 16 * (u // RING + 1)
            eng.wait_ge(unit_in[u % RING], n if i is None else i * (16 * per // RING) + n)

        def unit_used(eng, u, i=None, per=0):
            n = u // RING + 1
            eng.wait_ge(used[u % RING], n if i is None else i * (per // RING) + n)

        def slot(u, k, n):
            return ring[:, u % RING, 0:k * n].rearrange("p (k n) -> p k n", n=n)

        CREDIT = {s.name: n for s, n in ((readout, 2), (g_ready, 4), (table_ready, 2), (prod_ready, 2), (bu_copied, 1),
                                         (mod_row, 4), (gate_ready, 4), (gate_ps, 4), (w_ready, 2))}

        def count(eng, s, n):
            eng.wait_ge(s, n + CREDIT[s.name])

        def layer_width(l):
            return (0, TL) if l < DEPTH - 1 else (CTX, TL)

        block = ctx.enter_context(nc.Block())

        @block.sync
        def _(sp):
            sp.dma_start(cst[:, :], a["consts"]).then_inc(const_in, 16)
            sp.dma_start(par[:, :], a["params"]).then_inc(const_in, 16)
            sp.dma_start(xT[:, :, :], a["x_t"]).then_inc(const_in, 16)

            def load(u, src, i=None, per=0):
                n = u // RING
                if i is None:
                    if n >= 1:
                        sp.wait_ge(used[u % RING], n)
                else:
                    sp.wait_ge(used[u % RING], i * (per // RING) + n)
                w = src.shape[-1]
                sp.dma_start(ring[:, u % RING, 0:w], src).then_inc(unit_in[u % RING], 16)

            def stream(u, src, count):
                head = RING if u < RING else 0
                for k in range(head):
                    load(u + k, src[k])
                turns_ = (count - head) // RING
                with sp.Fori(0, turns_) as i:
                    for k in range(RING):
                        load(u + head + k, src[bass.ds(i * RING + (head + k), 1)].rearrange("o p n -> (o p) n"), i, RING)

            for st in stages:
                kind, l, h = st
                u = BASE[st]
                if kind == "mod":
                    stream(u, a["w_mod"][0], MOD_UNITS)
                elif kind == "front":
                    for k in range(FRONT_UNITS):
                        load(u + k, a["w_front"][l, k])
                    sp.wait_ge(h_ready, norms_before(("norm1", l, 0)) + 1)
                    sp.dma_start(mcst[:, :], a["mixer_consts"]).then_inc(mcst_in, 16)
                elif kind == "s5":
                    with sp.Fori(0, S5_ITER) as i:
                        load(u, a["s5_bc"][l, bass.ds(i, 1)].rearrange("o p n -> (o p) n"), i, 4)
                        for k in range(3):
                            load(u + 1 + k, a["w_side"][l, bass.ds(i * 3 + k, 1)].rearrange("o p n -> (o p) n"), i, 4)
                elif kind == "ret":
                    load(u, a["dist"])
                elif kind == "merge":
                    stream(u, a["w_merge"][l], MERGE_UNITS)
                    stream(u + MERGE_UNITS, a["w_out"][l], OUT_UNITS)
                elif kind == "route":
                    stream(u, a["w_q"][l], WQ_UNITS)
                    sp.wait_ge(h_ready, norms_before(("norm2", l, h)) + 1)
                    sp.dma_start(keys[:, :, :], a["keys"][l]).then_inc(keys_in, 16)
                    if next_mod(st):
                        stream(u + WQ_UNITS, a["w_mod"][l + 1], MOD_UNITS)
                elif kind == "experts":
                    stream(u, a["experts"][l], NK)
                elif kind == "final":
                    sp.wait_ge(fin_ready, 1)
                    sp.dma_start(a["out"], fout[:, :, :]).then_inc(stored, 16)
                    sp.wait_ge(stored, 16)

        @block.gpsimd
        def _(pool):
            for st in stages:
                kind, l, h = st
                if kind == "s5":
                    with pool.Fori(0, S5_ITER) as i:
                        for n in range(8):
                            d = n % 2
                            count(pool, g_ready, i * 8 + (l * 32 + n + 1))
                            count(pool, readout, i * 8 + (l * 32 + n - 1))
                            lo = layer_width(l)[0]
                            w = TL - lo
                            for k in range(2):
                                src = gst[:, d, :, lo:TL]
                                t = tab[:, d, :, lo:TL] if k == 0 else tab[:, d, ::-1, lo:TL]
                                for c in range(2):
                                    dst = prod[:, d, 2 * k + c, 0:w]
                                    if d == 1:
                                        dst = dst.rearrange("p (h t) -> p h t", t=256)[:, :, ::-1]
                                        s_ = src[:, c, :].rearrange("p (h t) -> p h t", t=256)
                                        t_ = t[:, c, :].rearrange("p (h t) -> p h t", t=256)
                                    else:
                                        s_, t_ = src[:, c, :], t[:, c, :]
                                    last = pool.tensor_tensor(dst, s_, t_, ALU.mult)
                            last.then_inc(prod_ready, 1)
                elif kind == "experts":
                    p = passes_before(st)
                    pool.wait_ge(h_ready, norms_before(("norm2", l, h)) + 1)
                    pool.dma_start(a["x_scratch"], xT[:, :, :]).then_inc(x_held, 16)
                    pool.wait_ge(x_held, 16 * (p + 1))
                    pool.wait_ge(y_ready, p + 1)
                    pool.dma_start(xT[:, :, :], a["x_scratch"]).then_inc(x_back, 16)

        @block.tensor
        def _(pe):
            pe.wait_ge(const_in, 48)

            def mm(out, w, x, start, stop, **k):
                return pe.matmul(out, w, x, start=start, stop=stop, **k)

            def norm_mean(st, sqb, w):
                n = norms_before(st)
                pe.wait_ge(sq_ready, n + 1)
                for k in range(KD):
                    last = mm(ps[:, 7, 0:w], cst[:, C_ONES_D:C_ONES_D + P], sqb[:, k, :], k == 0, k == KD - 1)
                last.then_inc(mean_ready, 1)

            def mod_rows(u, l, first, n, bank):
                with pe.Fori(0, n // RING) as i:
                    for k in range(RING):
                        v = u + first + k
                        arrived(pe, v, i, RING)
                        count(pe, mod_row, i * RING + (l * MOD_UNITS + first + k - 3))
                        w = slot(v, KD, 256)
                        for c in range(KD):
                            last = mm(ps[0:2, bank + k, 0:256], par[:, N_C + 2 * c:N_C + 2 * c + 2], w[:, c, :],
                                      c == 0, c == KD - 1)
                        last.then_inc(used[v % RING], 1)

            def mod_columns(l, row, bank):
                count(pe, mod_row, (l + 1) * MOD_UNITS)
                for c in range(6 * KD):
                    last = mm(ps[:, bank, 2 * c:2 * c + 2], row[0:2, c * P:(c + 1) * P], ident[0:2, 0:2], True, True)
                last.then_inc(mod_col, 1)

            for st in stages:
                kind, l, h = st
                u = BASE[st]
                if kind == "mod":
                    pe.wait_ge(cond_ready, 1)
                    mod_rows(u, 0, 0, MOD_UNITS, 0)
                    mod_columns(0, mrow0, 4)
                elif kind == "norm1":
                    norm_mean(st, sq1, TL)
                elif kind == "norm2":
                    norm_mean(st, sq2, 256)
                elif kind == "final":
                    norm_mean(st, sq2, 256)
                elif kind == "front":
                    pe.wait_ge(h_ready, norms_before(("norm1", l, 0)) + 1)
                    for k in range(FRONT_UNITS):
                        arrived(pe, u + k)
                        if k >= 2:
                            pe.wait_ge(proj_out, 18 * l + k - 1)
                        b = 2 * (k % 2)
                        w = slot(u + k, 2 * KD, P)
                        if k in (2, 3):
                            for t in range(TL // P):
                                for j in range(2):
                                    for c in range(KD):
                                        last = mm(ps[:, b + t // 2, (t % 2) * 256 + j * P:(t % 2) * 256 + j * P + P],
                                                  hT[:, c, t * P:(t + 1) * P], w[:, j * KD + c, :], c == 0, c == KD - 1)
                        else:
                            for j in range(2):
                                for c in range(KD):
                                    last = mm(ps[:, b + j, :], w[:, j * KD + c, :], hT[:, c, :], c == 0, c == KD - 1)
                        last.then_inc(used[(u + k) % RING], 1)
                elif kind == "s5":
                    lo, hi = layer_width(l)
                    w_ = hi - lo
                    pe.wait_ge(proj_out, 18 * l + FRONT_UNITS)
                    bc = slot(u, 8, P)
                    with pe.Fori(0, S5_ITER) as i:
                        def drive(q):
                            count(pe, bu_copied, i * 4 + (l * 16 + q))
                            for c in range(2):
                                last = mm(ps[:, 4 + c, :], bc[:, 2 * q + c, :],
                                          uT[:, bass.ds(i, 1), :].rearrange("p o t -> p (o t)"), True, True)
                            last.then_inc(bu_ready, 1)

                        def side(k):
                            v = u + 1 + k
                            arrived(pe, v, i, 4)
                            pe.wait_ge(proj_out, i * 3 + (18 * l + FRONT_UNITS + max(k - 1, 0)))
                            b = 2 * (k % 2)
                            w = slot(v, 2 * KD, P)
                            for j in range(2):
                                for c in range(KD):
                                    last = mm(ps[:, b + j, 0:w_], w[:, j * KD + c, :], hT[:, c, lo:hi],
                                              c == 0, c == KD - 1)
                            last.then_inc(used[v % RING], 1)

                        def read(q):
                            for d in range(2):
                                n = 2 * q + d
                                count(pe, prod_ready, i * 8 + (l * 32 + n + 1))
                                pe.wait_ge(cprime_ready, i * 8 + (l * 32 + n + 1))
                                for k in range(4):
                                    last = mm(ps[32 * q:32 * q + 32, 6, 0:w_], cpr[:, d, (0, 1, 2, 2)[k], :],
                                              prod[:, d, k, 0:w_], n % 2 == 0 and k == 0, d == 1 and k == 3)
                                last.then_inc(readout, 1)

                        arrived(pe, u, i, 4)
                        drive(0)
                        side(0)
                        drive(1)
                        pe.wait_ge(used[u % RING], i + u // RING)
                        read(0)
                        side(1)
                        drive(2)
                        read(1)
                        side(2)
                        drive(3)
                        read(2)
                        read(3)
                elif kind == "ret":
                    lo = layer_width(l)[0]
                    pe.wait_ge(proj_out, 18 * (l + 1))
                    for j, src in enumerate((qT, kT)):
                        for hd in range(RH):
                            last = mm(ps[:, 2 * j + hd // 2, (hd % 2) * 256:(hd % 2) * 256 + 256],
                                      cst[:, C_PERM:C_PERM + P], src[:, hd, CTX:TL], True, True)
                        last.then_inc(rope_ps, 1)
                    pe.wait_ge(roped, 2 * (l + 1))

                    def outs(hd):
                        b = 3 * (hd % 2)
                        pe.wait_ge(sd_ready, l * RH + hd + 1)
                        if hd >= 2:
                            pe.wait_ge(o_copied, l * RH + hd - 1)
                        ob = ps[:, 6 + hd % 2, :]
                        for t in range(4):
                            last = mm(ob[:, CTX:TL], vN[:, t, hd * P:(hd + 1) * P], sd[:, hd % 2, t, :], t == 0, t == 3)
                        if lo == 0:
                            for t in range(2):
                                last = mm(ob[:, 0:CTX], vN[:, t, hd * P:(hd + 1) * P], sd[:, hd % 2, 4 + t, :],
                                          t == 0, t == 1)
                        last.then_inc(o_ps, 1)

                    for hd in range(RH):
                        b = 3 * (hd % 2)
                        if hd >= 2:
                            pe.wait_ge(sd_ready, l * RH + hd - 1)
                        for t in range(4):
                            last = mm(ps[:, b + t // 2, (t % 2) * 256:(t % 2) * 256 + 256], kT[:, hd, t * P:(t + 1) * P],
                                      qT[:, hd, CTX:TL], True, True)
                        if lo == 0:
                            for t in range(2):
                                last = mm(ps[:, b + 2, t * 256:t * 256 + 256], kT[:, hd, t * P:(t + 1) * P],
                                          qT[:, hd, 0:CTX], True, True)
                        last.then_inc(score_ps, 1)
                        if hd >= 1:
                            outs(hd - 1)
                    outs(RH - 1)
                    pe.wait_ge(osq_ready, l + 1)
                    for hd in range(RH):
                        last = mm(ps[:, hd, lo:TL], cst[:, C_ONES_H:C_ONES_H + P], osq[:, hd, lo:TL], True, True)
                    last.then_inc(omean_ready, 1)
                elif kind == "merge":
                    lo, hi = layer_width(l)
                    w_ = hi - lo
                    pe.wait_ge(ys_ready, l + 1)
                    pe.wait_ge(yr_ready, l + 1)
                    for j in range(MERGE_UNITS):
                        arrived(pe, u + j)
                        if j >= 2:
                            pe.wait_ge(m_ready, KD * l + j - 1)
                        w = slot(u + j, 12, P)
                        for part in range(3):
                            src = gT if part == 2 else uT
                            for c in range(CT):
                                last = mm(ps[:, 2 * part + j % 2, 0:w_], w[:, 4 * part + c, :], src[:, c, lo:hi],
                                          c == 0, c == CT - 1)
                        last.then_inc(used[(u + j) % RING], 1)
                    pe.wait_ge(m_ready, KD * (l + 1))
                    for j in range(OUT_UNITS):
                        v = u + MERGE_UNITS + j
                        arrived(pe, v)
                        if j >= 2:
                            pe.wait_ge(x_ready, X_COUNT[st] + j - 1)
                        w = slot(v, 2 * KD, P)
                        for t in range(2):
                            for c in range(KD):
                                last = mm(ps[:, 2 * (j % 2) + t, 0:w_], w[:, t * KD + c, :], mT[:, c, 0:w_],
                                          c == 0, c == KD - 1)
                        last.then_inc(used[v % RING], 1)
                elif kind == "route":
                    p = passes_before(st)
                    pe.wait_ge(h_ready, norms_before(("norm2", l, h)) + 1)
                    for k in range(WQ_UNITS):
                        arrived(pe, u + k)
                        if k >= 2:
                            pe.wait_ge(qr_ready, WQ_UNITS * p + k - 1)
                        w = slot(u + k, 2 * KD, P)
                        for j in range(2):
                            for c in range(KD):
                                last = mm(ps[:, k % 2, j * 256:j * 256 + 256], w[:, j * KD + c, :], h2T[:, c, :],
                                          c == 0, c == KD - 1)
                        last.then_inc(used[(u + k) % RING], 1)
                    pe.wait_ge(keys_in, 16 * (p + 1))
                    pe.wait_ge(qr_ready, WQ_UNITS * (p + 1))
                    for tb in range(2):
                        for hd in range(NH):
                            last = mm(ps[:, 4 * tb + hd // 2, (hd % 2) * 256:(hd % 2) * 256 + 256],
                                      qrT[:, hd, tb * P:(tb + 1) * P], keys[:, hd, :], True, True)
                        last.then_inc(score_out, 1)
                    pe.wait_ge(score_ready, 2 * p + 2)
                    for tb in range(2):
                        if next_mod(st):
                            mod_rows(u + WQ_UNITS, l + 1, tb * MOD_UNITS // 2, MOD_UNITS // 2, 4)
                            if tb:
                                mod_columns(l + 1, mrow1, 2)
                        pe.wait_ge(pick_ready, 2 * p + tb + 1)
                        for k in range(3):
                            last = pe.transpose(ps[:, tb, k * P:(k + 1) * P], pick[:, k, :], ident)
                        last.then_inc(pick_ps, 1)
                elif kind == "gates":
                    p = passes_before(st)
                    with pe.Fori(0, 16) as i:
                        for g in range(4):
                            count(pe, gate_ready, i * 4 + (64 * p + g - 3))
                            for t in range(4):
                                pe.wait_ge(hot_ready, i * 16 + (256 * p + 4 * g + t + 1))
                                last = mm(ps[:, 4 + g, t * P:(t + 1) * P], hot[:, 0, t, :], hot[:, 1, t, :], True, True)
                                last.then_inc(gate_ps, 1)
                elif kind == "experts":
                    p = passes_before(st)
                    count(pe, gate_ready, 64 * (p + 1))
                    pe.wait_ge(pick_col, 2 * (p + 1))
                    for b in range(4):
                        mm(ps[:, b, :], zeros[:, :], cst[:, 0:512], True, False)

                    def up(k, i):
                        v = u + k
                        pe.wait_ge(ulo_ready, i * RING + (NK * p + k + 1))
                        hi, lo_ = ehi[:, k % 2, :], elo[:, v % RING, 0:DM]
                        for c in range(KD):
                            s_ = slice(c * P, (c + 1) * P)
                            o = ps[:, 4 + k % 4, 0:256]
                            mm(o, hi[:, s_], h2h[:, c, :], c == 0, False)
                            mm(o, hi[:, s_], h2l[:, c, :], False, False)
                            last = mm(o, lo_[:, s_], h2h[:, c, :], False, c == KD - 1)
                        last.then_inc(a_ready, 1)

                    def down(k, i):
                        v = u + k
                        pe.wait_ge(vlo_ready, i * RING + (NK * p + k + 1))
                        count(pe, w_ready, i * RING + (NK * p + k + 1))
                        hi, lo_ = ehi[:, 2 + k % 2, :], elo[:, v % RING, DM:2 * DM]
                        for tb in range(2):
                            t_ = slice(tb * P, (tb + 1) * P)
                            for w_, val in ((wh, hi), (wh, lo_), (wl, hi)):
                                for n in range(2):
                                    last = mm(ps[:, 2 * tb + n, :], w_[:, k % 2, t_], val[:, n * 512:(n + 1) * 512],
                                              False, False)
                        last.then_inc(used[v % RING], 1)

                    up(0, 0)
                    with pe.Fori(0, NK // RING - 1) as i:
                        for k in range(RING):
                            up(k + 1, i)
                            down(k, i)
                    for k in range(RING):
                        if k < RING - 1:
                            up(k + 1, NK // RING - 1)
                        down(k, NK // RING - 1)
                    for b in range(4):
                        last = mm(ps[:, b, :], zeros[:, :], cst[:, 0:512], False, True)
                    last.then_inc(y_ready, 1)
                    for tb in range(2):
                        pe.wait_ge(y_copied, 2 * p + tb + 1)
                        for d in range(KD):
                            last = pe.transpose(ps[:, 4 + d // 2, (d % 2) * 256 + tb * P:(d % 2) * 256 + tb * P + P],
                                                yout[:, tb, d * P:(d + 1) * P], ident)
                    last.then_inc(y_col, 1)

        @block.scalar
        def _(act):
            own = Chain(act, act_own)
            act.wait_ge(const_in, 48)

            def squares(st, sqb, lo, w):
                act.activation(sqb[:, :, :], xT[:, :, lo:lo + w], ACT.Square).then_inc(sq_ready, 1)

            def stddev(st, rs, w):
                n = norms_before(st)
                act.wait_ge(mean_ready, n + 1)
                act.activation(rs[:, 0:w], ps[:, 7, 0:w], ACT.Sqrt, bias=eps).then_inc(std_ready, 1)

            def mod_rows(u, row, first, n, bank):
                with act.Fori(0, n // RING) as i:
                    for k in range(RING):
                        unit_used(act, u + first + k, i, RING)
                        act.activation(row[0:2, bass.ds(i * (256 * RING) + 256 * (first + k), 256)],
                                       ps[0:2, bank + k, 0:256], ACT.Copy).then_inc(mod_row, 1)

            for st in stages:
                kind, l, h = st
                u = BASE[st]
                if kind == "mod":
                    act.activation(par[:, N_C:N_C + 16], par[:, N_C:N_C + 16], ACT.Silu).then_inc(cond_ready, 1)
                    own.link(act.activation(lg[:, :], par[:, N_DEC:N_DEC + 16], ACT.Exp))
                    own.link(act.activation(lg[:, :], lg[:, :], ACT.Copy, scale=-1.0))
                    act.activation(sp_(S_DT), par[:, N_LAM + 128:N_LAM + 192], ACT.Exp).then_inc(s5_lam, 1)
                    act.wait_ge(s5_angle, 1)
                    act.activation(sp_(S_R), sp_(S_T0), ACT.Exp)
                    act.activation(sp_(S_SIN), sp_(S_T1), ACT.Sin)
                    act.activation(sp_(S_COS), sp_(S_T2), ACT.Sin, scale=-1.0,
                                   bias=cst[:, C_HPI:C_HPI + 1]).then_inc(s5_trig, 1)
                    mod_rows(u, mrow0, 0, MOD_UNITS, 0)
                elif kind == "norm1":
                    if l:
                        act.wait_ge(x_ready, X_COUNT[st])
                    else:
                        act.wait_ge(mod_done, 1)
                    squares(st, sq1, 0, TL)
                    stddev(st, rs1, TL)
                elif kind == "norm2" or kind == "final":
                    act.wait_ge(x_ready, X_COUNT[st])
                    squares(st, sq2, CTX * h, 256)
                    stddev(st, rs2, 256)
                elif kind == "front":
                    for k in range(FRONT_UNITS):
                        unit_used(act, u + k)
                        b = 2 * (k % 2)
                        if k in (2, 3):
                            dst = vN[:, :, (k - 2) * 256:(k - 1) * 256]
                            src = ps[:, b:b + 2, :].rearrange("p b (t c) -> p (b t) c", c=256)
                        elif k < 2:
                            dst, src = uT[:, 2 * k:2 * k + 2, :], ps[:, b:b + 2, :]
                        else:
                            dst, src = kT[:, 2 * k - 8:2 * k - 6, :], ps[:, b:b + 2, :]
                        act.activation(dst, src, ACT.Copy).then_inc(proj_out, 1)
                elif kind == "s5":
                    lo, hi = layer_width(l)
                    w_ = hi - lo
                    with act.Fori(0, S5_ITER) as i:
                        own.loop(i, 8)
                        for q in range(4):
                            act.wait_ge(bu_ready, i * 4 + (l * 16 + q + 1))
                            count(act, g_ready, i * 8 + (l * 32 + 2 * q - 2))
                            act.activation(bu[:, q % 2, :, :], ps[:, 4:6, :], ACT.Copy).then_inc(bu_copied, 1)
                            for d in range(2):
                                n = 2 * q + d
                                act.wait_ge(phase_ready, i * 8 + (l * 32 + n + 1))
                                count(act, prod_ready, i * 8 + (l * 32 + n - 1))
                                count(act, table_ready, i * 8 + (l * 32 + n))
                                own.link(act.activation(absp[:, :], phase[:, d, :], ACT.Abs))
                                act.activation(tab[:, d, 0, :], absp[:, :], ACT.Sin, scale=-TWO_PI_IN,
                                               bias=cst[:, C_HPI:C_HPI + 1])
                                act.activation(tab[:, d, 1, :], phase[:, d, :], ACT.Sin, scale=TWO_PI_IN
                                               ).then_inc(table_ready, 1)
                            if q < 3:
                                unit_used(act, u + 1 + q, i, 4)
                                b = 2 * (q % 2)
                                act.activation(pj[:, bass.ds(i * 6 + 2 * q, 2), lo:hi], ps[:, b:b + 2, 0:w_],
                                               ACT.Copy).then_inc(proj_out, 1)
                        own.end(S5_ITER)
                elif kind == "ret":
                    lo, hi = layer_width(l)
                    dist = slot(u, 4, 512)
                    act.wait_ge(decay_arg, l + 1)
                    act.activation(decay[:, :, 0, :], decay[:, :, 0, :], ACT.Exp)
                    for hd in range(RH):
                        f, b = 2 * l * RH + hd, (2 * l + 1) * RH + hd
                        act.activation(decay[:, hd, 1, :], dist[:, 2, :], ACT.Exp, scale=lg[:, f:f + 1])
                        last = act.activation(dtmp[:, hd, :], dist[:, 3, :], ACT.Exp, scale=lg[:, b:b + 1])
                    last.then_inc(decay_ready, 1)
                    for hd in range(RH):
                        act.wait_ge(o_ps, l * RH + hd + 1)
                        act.activation(oT[:, hd, lo:hi], ps[:, 6 + hd % 2, lo:hi], ACT.Copy).then_inc(o_copied, 1)
                    act.wait_ge(o_copied, RH * (l + 1))
                    act.activation(osq[:, :, lo:hi], oT[:, :, lo:hi], ACT.Square).then_inc(osq_ready, 1)
                    act.wait_ge(omean_ready, l + 1)
                    act.activation(osq[:, :, lo:hi], ps[:, 0:4, lo:hi], ACT.Sqrt, bias=eps).then_inc(ostd_ready, 1)
                    unit_used(act, BASE[("s5", l, 0)] + 12)
                    act.activation(uT[:, :, lo:hi], uT[:, :, lo:hi], ACT.Gelu_apprx_tanh).then_inc(ys_ready, 1)
                    act.activation(gT[:, :, lo:hi], gT[:, :, lo:hi], ACT.Silu).then_inc(gates_on, 1)
                    act.activation(pj[:, 8:24, lo:hi], pj[:, 8:24, lo:hi], ACT.Sigmoid).then_inc(gates_on, 1)
                elif kind == "merge":
                    lo, hi = layer_width(l)
                    w_ = hi - lo
                    act.wait_ge(yr_ready, l + 1)
                    for j in range(MERGE_UNITS):
                        unit_used(act, u + j)
                        if j >= 2:
                            act.wait_ge(m_ready, KD * l + j - 1)
                        act.activation(sgb[:, j % 2, 0:w_], ps[:, 2 + j % 2, 0:w_], ACT.Sigmoid).then_inc(sg_ready, 1)
                elif kind == "route":
                    p = passes_before(st)
                    for k in range(WQ_UNITS):
                        unit_used(act, u + k)
                        act.activation(qrT[:, 2 * k:2 * k + 2, :],
                                       ps[:, k % 2, :].rearrange("p (a b) -> p a b", a=2), ACT.Copy).then_inc(qr_ready, 1)
                    for tb in range(2):
                        act.wait_ge(score_out, 2 * p + tb + 1)
                        act.activation(sc[:, tb, :, :], ps[:, 4 * tb:4 * tb + 4, :], ACT.Copy).then_inc(score_ready, 1)
                    for tb in range(2):
                        if next_mod(st):
                            mod_rows(u + WQ_UNITS, mrow1, tb * MOD_UNITS // 2, MOD_UNITS // 2, 4)
                        act.wait_ge(exp_in, 2 * p + tb + 1)
                        act.activation(best[:, :, :], best[:, :, :], ACT.Exp).then_inc(exp_out, 1)
                    for tb in range(2):
                        act.wait_ge(pick_ps, 2 * p + tb + 1)
                        act.activation(idxT[:, :, tb * P:(tb + 1) * P],
                                       ps[:, tb, 0:3 * P].rearrange("p (a b) -> p a b", a=3), ACT.Copy
                                       ).then_inc(pick_col, 1)
                elif kind == "gates":
                    p = passes_before(st)
                    with act.Fori(0, 16) as i:
                        for g in range(4):
                            count(act, gate_ps, i * 16 + (256 * p + 4 * g + 4))
                            src = ps[:, 4 + g, :].rearrange("p (t n) -> p n t", n=P)
                            act.activation(gate[:, :, bass.ds(i * 16 + 4 * g, 4)], src, ACT.Copy).then_inc(gate_ready, 1)
                elif kind == "experts":
                    p = passes_before(st)
                    def u_high(k, i):
                        arrived(act, u + k, i, RING)
                        if k >= 2 or not isinstance(i, int):
                            act.wait_ge(a_ready, i * RING + (NK * p + k - 1))
                        act.activation(ehi[:, k % 2, :], ring[:, (u + k) % RING, 0:DM], ACT.Copy).then_inc(uhi_ready, 1)

                    act.wait_ge(x_held, 16 * (p + 1))
                    u_high(0, 0)
                    u_high(1, 0)

                    def step(k, i, ahead):
                        act.wait_ge(a_ready, i * RING + (NK * p + k + 1))
                        count(act, w_ready, i * RING + (NK * p + k - 1))
                        act.activation(actT[:, k % 2, :], ps[:, 4 + k % 4, 0:256], ACT.Gelu).then_inc(act_ready, 1)
                        unit_used(act, u + k - 2, i, RING)
                        act.activation(ehi[:, 2 + k % 2, :], ring[:, (u + k) % RING, DM:2 * DM], ACT.Copy
                                       ).then_inc(vhi_ready, 1)
                        if ahead:
                            u_high(k + 2, i)

                    with act.Fori(0, NK // RING - 1) as i:
                        for k in range(RING):
                            step(k, i, True)
                    for k in range(RING):
                        step(k, NK // RING - 1, k < 2)
                    act.wait_ge(y_ready, p + 1)
                    for tb in range(2):
                        act.activation(yout[:, tb, :], ps[:, 2 * tb:2 * tb + 2, :], ACT.Copy).then_inc(y_copied, 1)

        @block.vector
        def _(dve):
            own = Chain(dve, dve_own)
            link = own.link
            v = nc.vector
            dve.wait_ge(const_in, 48)
            for s_ in (readout, g_ready, table_ready, prod_ready, bu_copied, mod_row, gate_ready, gate_ps, w_ready):
                dve.sem_inc(s_, CREDIT[s_.name])


            def normed(st, rs, w, dst, lo, which):
                n = norms_before(st)
                dve.wait_ge(std_ready, n + 1)
                link(v.reciprocal(rs[:, 0:w], rs[:, 0:w]))
                halves = range(w // 256)
                for k in range(KD):
                    for hf in halves:
                        side = hf if w > 256 else lo // CTX
                        s_ = slice(hf * 256, hf * 256 + 256)
                        last = v.scalar_tensor_tensor(dst[:, k, s_], xT[:, k, lo + hf * 256:lo + hf * 256 + 256],
                                                      which[0](k, side), rs[:, s_], ALU.mult, ALU.mult)
                if which[1] is None:
                    return last
                link(last)
                for k in range(KD):
                    for hf in halves:
                        side = hf if w > 256 else lo // CTX
                        s_ = slice(hf * 256, hf * 256 + 256)
                        last = v.tensor_scalar(dst[:, k, s_], dst[:, k, s_], which[1](k, side), None, ALU.add)
                return last

            def mod_tables(l, bank):
                dve.wait_ge(mod_col, l + 1)
                b = par[:, N_BMOD + 48 * l:N_BMOD + 48 * l + 48].unsqueeze(2).to_broadcast([P, 48, 2])
                link(v.tensor_tensor(modT[:, l, :, :, :].rearrange("p s k c -> p (s k) c"),
                                     ps[:, bank, 0:96].rearrange("p (a c) -> p a c", c=2), b, ALU.add))
                for n in range(2):
                    g = par[:, N_G + 16 * l + 8 * n:N_G + 16 * l + 8 * n + 8].unsqueeze(2).to_broadcast([P, 8, 2])
                    link(v.tensor_scalar(gain[:, l, n, :, :], modT[:, l, 3 * n + 1, :, :], 1.0, None, ALU.add))
                    last = v.tensor_tensor(gain[:, l, n, :, :], gain[:, l, n, :, :], g, ALU.mult)
                    if n == 0:
                        link(last)
                last.then_inc(mod_done, 1)
                dve.wait_ge(mod_done, l + 1)

            for st in stages:
                kind, l, h = st
                u = BASE[st]
                if kind == "mod":
                    v.memset(zeros[:, :], 0.0)
                    lr, li = par[:, N_LAM:N_LAM + 64], par[:, N_LAM + 64:N_LAM + 128]
                    dve.wait_ge(s5_lam, 1)
                    link(v.tensor_tensor(sp_(S_TH), li, sp_(S_DT), ALU.mult))
                    v.tensor_tensor(sp_(S_T0), lr, sp_(S_DT), ALU.mult)
                    link(v.tensor_scalar(s5k[:, :], sp_(S_TH), INV2PI, None, ALU.mult))
                    link(v.tensor_copy(sp_(S_K), s5k[:, :]))
                    for part in (TP1, TP2, TP3):
                        link(v.scalar_tensor_tensor(sp_(S_TH), sp_(S_K), -part, sp_(S_TH), ALU.mult, ALU.add))
                    link(v.tensor_scalar(sp_(S_TH), sp_(S_TH), 3.1415925, -3.1415925, ALU.min, ALU.max))
                    link(v.tensor_scalar(sp_(S_RHO), sp_(S_TH), INV2PI, None, ALU.mult))
                    link(v.tensor_scalar(s5k[:, :], sp_(S_RHO), 32768.0, None, ALU.mult))
                    link(v.tensor_scalar(sp_(S_RHI), s5k[:, :], 1.0 / 32768.0, None, ALU.mult))
                    link(v.scalar_tensor_tensor(sp_(S_RLO), sp_(S_RHI), -TP1, sp_(S_TH), ALU.mult, ALU.add))
                    link(v.scalar_tensor_tensor(sp_(S_RLO), sp_(S_RHI), -TP2, sp_(S_RLO), ALU.mult, ALU.add))
                    link(v.tensor_scalar(sp_(S_RLO), sp_(S_RLO), INV2PI, None, ALU.mult))
                    link(v.tensor_copy(sp_(S_T1), sp_(S_TH)))
                    link(v.tensor_scalar(sp_(S_T2), sp_(S_TH), -1.0, None, ALU.mult))
                    v.tensor_tensor(sp_(S_T2), sp_(S_T2), sp_(S_TH), ALU.max).then_inc(s5_angle, 1)
                    dve.wait_ge(s5_trig, 1)
                    link(v.tensor_tensor(sp_(S_COS), sp_(S_COS), sp_(S_R), ALU.mult))
                    link(v.tensor_tensor(sp_(S_SIN), sp_(S_SIN), sp_(S_R), ALU.mult))
                    link(v.tensor_scalar(sp_(S_COS), sp_(S_COS), -1.0, None, ALU.add))
                    link(v.tensor_tensor(sp_(S_T0), lr, lr, ALU.mult))
                    link(v.tensor_tensor(sp_(S_T1), li, li, ALU.mult))
                    link(v.tensor_tensor(sp_(S_T0), sp_(S_T0), sp_(S_T1), ALU.add))
                    link(v.reciprocal(sp_(S_T2), sp_(S_T0)))
                    link(v.tensor_tensor(sp_(S_T0), sp_(S_COS), lr, ALU.mult))
                    link(v.tensor_tensor(sp_(S_T1), sp_(S_SIN), li, ALU.mult))
                    link(v.tensor_tensor(sp_(S_T0), sp_(S_T0), sp_(S_T1), ALU.add))
                    link(v.tensor_tensor(sp_(S_BR), sp_(S_T0), sp_(S_T2), ALU.mult))
                    link(v.tensor_tensor(sp_(S_T0), sp_(S_SIN), lr, ALU.mult))
                    link(v.tensor_tensor(sp_(S_T1), sp_(S_COS), li, ALU.mult))
                    link(v.tensor_tensor(sp_(S_T0), sp_(S_T0), sp_(S_T1), ALU.subtract))
                    link(v.tensor_tensor(sp_(S_BI), sp_(S_T0), sp_(S_T2), ALU.mult))
                    link(v.tensor_scalar(sp_(S_NBR), sp_(S_BR), -1.0, None, ALU.mult))
                    link(v.tensor_scalar(sp_(S_NBI), sp_(S_BI), -1.0, None, ALU.mult))
                    mod_tables(0, 4)
                elif kind == "norm1":
                    normed(st, rs1, TL, hT, 0,
                           (lambda k, s: gain[:, l, 0, k, s:s + 1], lambda k, s: modT[:, l, 0, k, s:s + 1])
                           ).then_inc(h_ready, 1)
                elif kind == "norm2":
                    link(normed(st, rs2, 256, h2T, CTX * h,
                                (lambda k, s: gain[:, l, 1, k, s:s + 1], lambda k, s: modT[:, l, 3, k, s:s + 1])))
                    link(v.tensor_copy(h2h[:, :, :], h2T[:, :, :]))
                    v.tensor_tensor(h2l[:, :, :], h2T[:, :, :], h2h[:, :, :].bitcast(F32), ALU.subtract).then_inc(h_ready, 1)
                elif kind == "final":
                    normed(st, rs2, 256, fout, CTX,
                           (lambda k, s: par[:, N_FG + k:N_FG + k + 1], None)).then_inc(fin_ready, 1)
                elif kind == "s5":
                    lo, hi = layer_width(l)
                    w_ = hi - lo
                    dve.wait_ge(mcst_in, 16 * (l + 1))
                    with dve.Fori(0, S5_ITER) as i:
                        own.loop(i, S5_LINKS)
                        C = ring[:, u % RING, 8 * P:8 * P + 8 * 32].rearrange("p (q c n) -> p q c n", q=4, c=2)

                        def lane(k, n):
                            return s5p[:, k, bass.ds(i * 4 + ((2 * l + n % 2) * NT + n // 2), 1)]

                        def phases(n):
                            d = n % 2
                            t = mcst[:, M_T:M_T + TL]
                            count(dve, table_ready, i * 8 + (l * 32 + n - 1))
                            link(v.tensor_scalar(turns[:, :], t, lane(S_RHO, n), None, ALU.mult))
                            link(v.scalar_tensor_tensor(phase[:, d, :], t, lane(S_RHI, n), turns[:, :], ALU.mult, ALU.subtract))
                            link(v.scalar_tensor_tensor(phase[:, d, :], t, lane(S_RLO, n), phase[:, d, :], ALU.mult, ALU.add))
                            v.tensor_scalar(phase[:, d, :], phase[:, d, :], 0.5, -0.5, ALU.min, ALU.max
                                            ).then_inc(phase_ready, 1)

                        phases(0)
                        arrived(dve, u, i, 4)
                        for n in range(8):
                            q, d = n // 2, n % 2
                            if n < 7:
                                phases(n + 1)
                            count(dve, readout, i * 8 + (l * 32 + n - 1))
                            v.tensor_scalar(ctmp[:, 0, :], C[:, q, 1, :], lane(S_NBI, n), None, ALU.mult)
                            link(v.tensor_scalar(ctmp[:, 1, :], C[:, q, 1, :], lane(S_NBR, n), None, ALU.mult))
                            link(v.scalar_tensor_tensor(cpr[:, d, 0, :], C[:, q, 0, :], lane(S_BR, n), ctmp[:, 0, :], ALU.mult, ALU.add))
                            v.tensor_scalar(cpr[:, d, 1, :], cpr[:, d, 0, :], -1.0, None, ALU.mult)
                            v.scalar_tensor_tensor(cpr[:, d, 2, :], C[:, q, 0, :], lane(S_NBI, n), ctmp[:, 1, :], ALU.mult, ALU.add
                                                   ).then_inc(cprime_ready, 1)
                            count(dve, table_ready, i * 8 + (l * 32 + n + 1))
                            count(dve, bu_copied, i * 4 + (l * 16 + q + 1))
                            T, G = tab[:, d, :, :], gst[:, d, :, :]

                            def turned(dst, t):
                                for c in range(2):
                                    b_ = bu[:, q % 2, c, :]
                                    if d:
                                        b_ = b_.rearrange("p (h t) -> p h t", t=256)[:, :, ::-1]
                                        v_ = v.tensor_tensor(dst[:, c, :].rearrange("p (h t) -> p h t", t=256), b_,
                                                             t[:, c, :].rearrange("p (h t) -> p h t", t=256), ALU.mult)
                                    else:
                                        v_ = v.tensor_tensor(dst[:, c, :], b_, t[:, c, :], ALU.mult)
                                return v_

                            own.mark(turned(rot[:, 0, :, :], T))
                            link(turned(rot[:, 1, :, :], T[:, ::-1, :]))
                            own.mark(v.tensor_tensor(G[:, 0, :], rot[:, 0, 0, :], rot[:, 0, 1, :], ALU.add))
                            link(v.tensor_tensor(G[:, 1, :], rot[:, 1, 1, :], rot[:, 1, 0, :], ALU.subtract))
                            r = lane(S_R, n).to_broadcast([P, TL])
                            for c in range(2):
                                last = v.tensor_tensor_scan(G[:, c, :], r, G[:, c, :], 0.0, ALU.mult, ALU.add)
                            last.then_inc(g_ready, 1)
                        count(dve, readout, i * 8 + (l * 32 + 8))
                        uq = uT[:, bass.ds(i, 1), lo:hi].rearrange("p o t -> p (o t)")
                        v.scalar_tensor_tensor(uq, uq, par[:, bass.ds(i + (N_D + 4 * l), 1)], ps[:, 6, 0:w_],
                                               ALU.mult, ALU.add).then_inc(used[u % RING], 1)
                        own.end(S5_ITER)
                elif kind == "ret":
                    lo, hi = layer_width(l)
                    dist = slot(u, 4, 512)
                    arrived(dve, u)
                    for hd in range(RH):
                        b = (2 * l + 1) * RH + hd
                        last = v.tensor_scalar(dtmp[:, hd, :], dist[:, 1, :], lg[:, b:b + 1], None, ALU.mult)
                    link(last)
                    for hd in range(RH):
                        f = 2 * l * RH + hd
                        last = v.scalar_tensor_tensor(decay[:, hd, 0, :], dist[:, 0, :], lg[:, f:f + 1], dtmp[:, hd, :],
                                                      ALU.mult, ALU.add)
                    last.then_inc(decay_arg, 1)
                    dve.wait_ge(decay_ready, l + 1)
                    v.tensor_tensor(decay[:, :, 1, :], decay[:, :, 1, :], dtmp[:, :, :], ALU.add).then_inc(used[u % RING], 1)
                    for j, src in enumerate((qT, kT)):
                        dve.wait_ge(rope_ps, 2 * l + j + 1)
                        cos = mcst[:, M_COS:M_COS + 256].unsqueeze(1).to_broadcast([P, RH, 256])
                        sin = mcst[:, M_SIN:M_SIN + 256].unsqueeze(1).to_broadcast([P, RH, 256])
                        pp = ps[:, 2 * j:2 * j + 2, :].rearrange("p b (a t) -> p (b a) t", a=2)
                        own.mark(v.tensor_tensor(oT[:, :, 0:256], pp, sin, ALU.mult))
                        link(v.tensor_tensor(src[:, :, CTX:TL], src[:, :, CTX:TL], cos, ALU.mult))
                        v.tensor_tensor(src[:, :, CTX:TL], src[:, :, CTX:TL], oT[:, :, 0:256], ALU.add).then_inc(roped, 1)
                        dve.wait_ge(roped, 2 * l + j + 1)
                    scale = P ** -0.5
                    for hd in range(RH):
                        b = 3 * (hd % 2)
                        dve.wait_ge(score_ps, l * RH + hd + 1)
                        if hd == 0:
                            unit_used(dve, u)
                        if hd >= 2:
                            dve.wait_ge(o_ps, l * RH + hd - 1)
                        for g, (bank, which) in enumerate(((0, 1), (1, 0), (2, 0))[:3 if lo == 0 else 2]):
                            last = v.scalar_tensor_tensor(
                                sd[:, hd % 2, 2 * g:2 * g + 2, :].rearrange("p a t -> p (a t)"), ps[:, b + bank, :],
                                scale, decay[:, hd, which, :], ALU.mult, ALU.mult)
                        last.then_inc(sd_ready, 1)
                    dve.wait_ge(ostd_ready, l + 1)
                    dve.wait_ge(o_copied, RH * (l + 1))
                    link(v.reciprocal(osq[:, :, lo:hi], osq[:, :, lo:hi]))
                    link(v.tensor_tensor(oT[:, :, lo:hi], oT[:, :, lo:hi], osq[:, :, lo:hi], ALU.mult))
                    dve.wait_ge(gates_on, 2 * l + 2)
                    v.tensor_tensor(gT[:, :, lo:hi], oT[:, :, lo:hi], gT[:, :, lo:hi], ALU.mult).then_inc(yr_ready, 1)
                elif kind == "merge":
                    lo, hi = layer_width(l)
                    w_ = hi - lo
                    for j in range(MERGE_UNITS):
                        dve.wait_ge(sg_ready, KD * l + j + 1)
                        unit_used(dve, u + j)
                        own.mark(v.tensor_tensor(mt1[:, j % 2, 0:w_], ps[:, j % 2, 0:w_], sgb[:, j % 2, 0:w_], ALU.mult))
                        link(v.tensor_tensor(mt2[:, j % 2, 0:w_], ps[:, 4 + j % 2, 0:w_], grT[:, j, lo:hi], ALU.mult))
                        link(v.tensor_tensor(mt1[:, j % 2, 0:w_], mt1[:, j % 2, 0:w_], gsT[:, j, lo:hi], ALU.mult))
                        v.tensor_tensor(mT[:, j, 0:w_], mt1[:, j % 2, 0:w_], mt2[:, j % 2, 0:w_], ALU.add).then_inc(m_ready, 1)
                    for j in range(OUT_UNITS):
                        unit_used(dve, u + MERGE_UNITS + j)
                        for t in range(2):
                            for side in range(lo // CTX, 2):
                                k = 2 * j + t
                                xs = xT[:, k, CTX * side:CTX * side + 256]
                                last = v.scalar_tensor_tensor(
                                    xs, ps[:, 2 * (j % 2) + t, CTX * side - lo:CTX * side - lo + 256],
                                    modT[:, l, 2, k, side:side + 1], xs, ALU.mult, ALU.add)
                        last.then_inc(x_ready, 1)
                elif kind == "route":
                    p = passes_before(st)
                    for tb in range(2):
                        dve.wait_ge(score_ready, 2 * p + tb + 1)
                        for hd in range(NH):
                            S = sc[:, tb, 2 * hd:2 * hd + 2, :]
                            tp = top[:, 2 * hd:2 * hd + 2, :]
                            ti = topi[:, 2 * hd:2 * hd + 2, :]
                            v.max(tp[:, 0, 0:8], S[:, 0, :])
                            link(v.max(tp[:, 1, 0:8], S[:, 1, :]))
                            for s_ in range(2):
                                v.max_index(ti[:, s_, 0:8], tp[:, s_, 0:8], S[:, s_, :])
                            v.match_replace(sc2[:, 0, :], tp[:, 0, 0:8], S[:, 0, :], -3e38)
                            link(v.match_replace(sc2[:, 1, :], tp[:, 1, 0:8], S[:, 1, :], -3e38))
                            v.max(tp[:, 0, 8:16], sc2[:, 0, :])
                            link(v.max(tp[:, 1, 8:16], sc2[:, 1, :]))
                            for s_ in range(2):
                                v.max_index(ti[:, s_, 8:16], tp[:, s_, 8:16], sc2[:, s_, :])
                            a_ = tp[:, 0, :].unsqueeze(2).to_broadcast([P, TOPK, TOPK])
                            b_ = tp[:, 1, :].unsqueeze(1).to_broadcast([P, TOPK, TOPK])
                            link(v.tensor_tensor(cand[:, :].rearrange("p (a b) -> p a b", a=TOPK), a_, b_, ALU.add))
                            be = best[:, hd, :]
                            bi = besti[:, hd, :]
                            link(v.max(be[:, 0:8], cand[:, :]))
                            v.max_index(bi[:, 0:8], be[:, 0:8], cand[:, :])
                            link(v.match_replace(cand2[:, :], be[:, 0:8], cand[:, :], -3e38))
                            link(v.max(be[:, 8:16], cand2[:, :]))
                            link(v.max_index(bi[:, 8:16], be[:, 8:16], cand2[:, :]))
                        top1 = best[:, :, 0:1].to_broadcast([P, NH, TOPK])
                        if tb or p:
                            dve.wait_ge(pick_ps, 2 * p + tb)
                        link(v.tensor_copy(pick[:, 2, :].rearrange("p (h k) -> p h k", h=NH), top1))
                        v.tensor_tensor(best[:, :, :], best[:, :, :], pick[:, 2, :].rearrange("p (h k) -> p h k", h=NH),
                                        ALU.subtract).then_inc(exp_in, 1)
                        v.tensor_copy(topf[:, :, :], topi[:, :, :])
                        bflat = besti[:, :, :].rearrange("p h k -> p (h k)")
                        v.tensor_scalar(bab[:, 0, :], bflat, 4, None, ALU.logical_shift_right)
                        link(v.tensor_scalar(bab[:, 1, :], bflat, 15, None, ALU.bitwise_and))
                        link(v.tensor_copy(babf[:, :, :], bab[:, :, :]))
                        i16 = cst[:, C_I16:C_I16 + TOPK].unsqueeze(1).to_broadcast([P, NH * TOPK, TOPK])
                        for s_ in range(2):
                            last = v.tensor_tensor(eq[:, s_, :, :], babf[:, s_, :].unsqueeze(2).to_broadcast([P, NH * TOPK, TOPK]),
                                                   i16, ALU.is_equal)
                        link(last)
                        for s_ in range(2):
                            e4 = eq[:, s_, :, :].rearrange("p (h k) a -> p h k a", h=NH)
                            t4 = topf[:, s_::2, :].unsqueeze(2).to_broadcast([P, NH, TOPK, TOPK])
                            last = v.tensor_tensor(e4, e4, t4, ALU.mult)
                        link(last)
                        for s_ in range(2):
                            v.tensor_reduce(pick[:, s_, :], eq[:, s_, :, :], AX_X, ALU.add)
                        dve.wait_ge(exp_out, 2 * p + tb + 1)
                        link(v.tensor_reduce(ssum[:, :], best[:, :, :], AX_X, ALU.add))
                        link(v.reciprocal(ssum[:, :], ssum[:, :]))
                        v.tensor_tensor(pick[:, 2, :].rearrange("p (h k) -> p h k", h=NH), best[:, :, :],
                                        ssum[:, :].unsqueeze(2).to_broadcast([P, NH, TOPK]), ALU.mult).then_inc(pick_ready, 1)
                    if next_mod(st):
                        mod_tables(l + 1, 2)
                elif kind == "gates":
                    p = passes_before(st)
                    dve.wait_ge(pick_col, 2 * (p + 1))
                    with dve.Fori(0, 16) as i:
                        for k in range(16):
                            count(dve, gate_ps, i * 16 + (256 * p + k - 3))
                            tok = [idxT[:, c, bass.ds(i * 16 + k, 1)] for c in range(3)]
                            v.tensor_scalar(hot[:, 0, k % 4, :], iota, tok[0], None, ALU.is_equal)
                            v.tensor_scalar(hot[:, 1, k % 4, :], iota, tok[1], tok[2], ALU.is_equal, ALU.mult
                                            ).then_inc(hot_ready, 1)
                elif kind == "experts":
                    p = passes_before(st)
                    def u_low(k, i):
                        dve.wait_ge(uhi_ready, i * RING + (NK * p + k + 1))
                        r = (u + k) % RING
                        v.tensor_tensor(elo[:, r, 0:DM], ring[:, r, 0:DM], ehi[:, k % 2, :].bitcast(F32), ALU.subtract
                                        ).then_inc(ulo_ready, 1)

                    u_low(0, 0)
                    u_low(1, 0)

                    def step(k, i, ahead):
                        dve.wait_ge(act_ready, i * RING + (NK * p + k + 1))
                        unit_used(dve, u + k - 2, i, RING)
                        g = gate[:, bass.ds(i * RING + k, 1), :].rearrange("p o t -> p (o t)")
                        b = k % 2
                        link(v.tensor_tensor(wf[:, b, :], actT[:, b, :], g, ALU.mult))
                        link(v.tensor_copy(wh[:, b, :], wf[:, b, :]))
                        v.tensor_tensor(wl[:, b, :], wf[:, b, :], wh[:, b, :].bitcast(F32), ALU.subtract
                                        ).then_inc(w_ready, 1)
                        dve.wait_ge(vhi_ready, i * RING + (NK * p + k + 1))
                        r = (u + k) % RING
                        v.tensor_tensor(elo[:, r, DM:2 * DM], ring[:, r, DM:2 * DM], ehi[:, 2 + b, :].bitcast(F32),
                                        ALU.subtract).then_inc(vlo_ready, 1)
                        if ahead:
                            u_low(k + 2, i)

                    with dve.Fori(0, NK // RING - 1) as i:
                        own.loop(i, 2 * RING)
                        for k in range(RING):
                            step(k, i, True)
                        own.end(NK // RING - 1)
                    for k in range(RING):
                        step(k, NK // RING - 1, k < 2)
                    dve.wait_ge(x_back, 16 * (p + 1))
                    dve.wait_ge(y_col, p + 1)
                    for k in range(KD):
                        xs = xT[:, k, CTX * h:CTX * h + 256]
                        last = v.scalar_tensor_tensor(xs, ps[:, 4 + k // 2, (k % 2) * 256:(k % 2) * 256 + 256],
                                                      modT[:, l, 5, k, h:h + 1], xs, ALU.mult, ALU.add)
                    last.then_inc(x_ready, 1)


def constants():
    c = np.zeros((P, C_N), np.float32)
    c[:, C_ID:C_ID + P] = np.eye(P)
    c[:, C_ONES_D:C_ONES_D + P] = 1.0 / DM
    c[:, C_ONES_H:C_ONES_H + P] = 1.0 / P
    c[:, C_IOTA:C_IOTA + P] = np.arange(P)
    for k in range(P):
        if k % 64 < 32:
            c[k + 32, C_PERM + k] = -1.0
        else:
            c[k - 32, C_PERM + k] = 1.0
    m = np.zeros((P, M_N), np.float32)
    m[:, M_T:M_T + TL] = np.arange(TL)
    c[:, C_I16:C_I16 + TOPK] = np.arange(TOPK)
    c[:, C_EPS] = EPS
    c[:, C_HPI] = np.float32(1.5707962)
    freqs = np.float32(10000.0) ** (-np.arange(32, dtype=np.float32) / np.float32(32))
    t = np.arange(SEQ)
    for d in range(P):
        at = (t // GRID_W if d < 64 else t % GRID_W).astype(np.float32) * freqs[d % 32]
        m[d, M_COS:M_COS + SEQ] = np.cos(at)
        m[d, M_SIN:M_SIN + SEQ] = np.sin(at)
    s = (np.arange(2)[None, :, None] * P + np.arange(P)[:, None, None]).astype(np.float32)
    tt = np.arange(256, dtype=np.float32)[None, None, :]
    d = np.stack([np.maximum(tt - s, 0), np.maximum(s - tt, 0), 256 + tt - s, 256 - tt + s], 1)
    return c, m, np.ascontiguousarray(d.reshape(P, 4 * 512), np.float32)


def layouts(i):
    f = lambda k: np.asarray(i[k])
    L = DEPTH
    out = {}
    out["x_t"] = np.concatenate([f("ctx")[0], f("x")[0]]).T.reshape(KD, P, TL).transpose(1, 0, 2)

    def tiles(w, per, n=P):
        k, m = w.shape[1:]
        return w.reshape(L, k // P, P, m // (n * per), per, n).transpose(0, 3, 2, 4, 1, 5)

    out["w_mod"] = tiles(f("w_mod"), 1, 256).reshape(L, MOD_UNITS, P, 2048)
    w_in = f("w_in")
    u, q, k, v, g, gs, gr = np.split(w_in, [512, 1024, 1536, 2048, 2560, 3584], axis=2)
    out["w_front"] = tiles(np.concatenate([u, v, k], 2), 2).reshape(L, FRONT_UNITS, P, 2048)
    out["w_side"] = tiles(np.concatenate([q, g, gs, gr], 2), 2).reshape(L, 12, P, 2048)
    glu, up = f("w_ssm_glu"), f("w_ret_up")
    parts = [tiles(w, 1).reshape(L, 8, P, 512) for w in (glu[:, :, :DM], glu[:, :, DM:], up)]
    out["w_merge"] = np.concatenate(parts, 3)
    out["w_out"] = tiles(f("w_out"), 2).reshape(L, OUT_UNITS, P, 2048)
    out["w_q"] = tiles(f("peer_w_q"), 2).reshape(L, WQ_UNITS, P, 2048)
    bc = np.zeros((L, 4, P, 8 * P + 256), np.float32)
    for c, (B, C) in enumerate((("ssm_B_re", "ssm_C_re"), ("ssm_B_im", "ssm_C_im"))):
        B, C = f(B).reshape(L, 4, 4, 2, 64, 16), f(C).reshape(L, 4, 4, 2, 16, 64)
        for q in range(4):
            for gi in range(2):
                r = 32 * q + 16 * gi
                bc[:, :, r:r + 16, (2 * q + c) * P + 64 * gi:(2 * q + c) * P + 64 * gi + 64] = B[:, :, q, gi].transpose(0, 1, 3, 2)
                at = 8 * P + (2 * q + c) * 32 + 16 * gi
                bc[:, :, 64 * gi:64 * gi + 64, at:at + 16] = C[:, :, q, gi].transpose(0, 1, 3, 2)
    out["s5_bc"] = bc
    keys = np.zeros((L, P, NH, 256), np.float32)
    sk = f("peer_sub_keys")
    for s in range(2):
        keys[:, 64 * s:64 * s + 64, :, P * s:P * s + P] = sk[:, :, s].transpose(0, 3, 1, 2)
    out["keys"] = keys
    ut = f("peer_u").reshape(L, NK, NK, KD, P).transpose(0, 2, 4, 3, 1).reshape(L, NK, P, DM)
    vt = f("peer_v").reshape(L, NK, NK, DM).transpose(0, 2, 1, 3)
    out["experts"] = np.concatenate([ut, vt], 3)
    p = np.zeros((P, N_N), np.float32)
    col = lambda w, n: w.reshape(L, n, P).transpose(2, 0, 1).reshape(P, L * n)
    p[:, N_BMOD:N_BMOD + 96] = col(f("b_mod"), 48)
    p[:, N_G:N_G + 32] = np.stack([f("norm1_g"), f("norm2_g")], 1).reshape(L, 2, 8, P).transpose(3, 0, 1, 2).reshape(P, 32)
    p[:, N_FG:N_FG + 8] = f("final_norm_g").reshape(8, P).T
    dirs = lambda w: np.stack([f(w + "_f"), f(w + "_b")], 1)
    lanes = lambda w: w.reshape(L, 2, NT, P).transpose(3, 0, 1, 2).reshape(P, 64)
    p[:, N_LAM:N_LAM + 64] = lanes(dirs("ssm_lam_re"))
    p[:, N_LAM + 64:N_LAM + 128] = lanes(dirs("ssm_lam_im"))
    p[:, N_LAM + 128:N_LAM + 192] = lanes(np.repeat(dirs("ssm_log_dt"), 64, axis=2))
    p[:, N_DEC:N_DEC + 16] = dirs("ret_decay").reshape(1, 16)
    p[:, N_D:N_D + 8] = col(f("ssm_D"), 4)
    p[:, N_C:N_C + 16] = np.stack([f("c_ctx"), f("c")[0]], 1).reshape(8, P, 2).transpose(1, 0, 2).reshape(P, 16)
    out["params"] = p
    out["consts"], out["mixer_consts"], out["dist"] = constants()
    return {k: np.ascontiguousarray(a, np.float32) if a.dtype != np.float32 else np.ascontiguousarray(a) for k, a in out.items()}


def kernel(**inputs):
    import concourse.bacc as bacc
    from concourse.bass_utils import run_bass_kernel_spmd

    nc = bacc.Bacc("TRN2", target_bir_lowering=False, num_devices=1)
    arrays = layouts(inputs)
    aps = {k: nc.dram_tensor(f"in_{k}", a.shape, F32, kind="ExternalInput").ap() for k, a in arrays.items()}
    aps["out"] = nc.dram_tensor("out_t", (P, KD, SEQ), F32, kind="ExternalOutput").ap()
    aps["x_scratch"] = nc.dram_tensor("x_scratch", (P, KD, TL), F32, kind="Internal").ap()
    build_program(nc, aps)
    r = run_bass_kernel_spmd(nc, [{f"in_{k}": a for k, a in arrays.items()}], core_ids=[0])
    got = r.results[0]["out_t"]
    return np.ascontiguousarray(got.transpose(1, 0, 2).reshape(DM, SEQ).T)[None]
```

```python
import math
from contextlib import ExitStack

import concourse.bass as bass
import numpy as np
from concourse import mybir

P = 128
DM = 1024
KD = DM // P
CTX, SEQ = 256, 256
TL = CTX + SEQ
DEPTH = 2
SSM = 512
NT = 16
CT = SSM // P
RH = 4
GRID_W = 64
EPS = 1e-6
NH, NK, TOPK = 8, 128, 16
CANDS = TOPK + (TOPK - 1) * TOPK // 2
HALF = 64
RING = 4
SLOT = 2048
MOD_UNITS = 24
FRONT_UNITS = 6
DIST_UNIT = 1
S5_ITER = 4
MERGE_UNITS, OUT_UNITS, WQ_UNITS = 8, 4, 4

F32 = mybir.dt.float32
F32R = mybir.dt.float32r
I32 = mybir.dt.int32
U32 = mybir.dt.uint32
ALU = mybir.AluOpType
ACT = mybir.ActivationFunctionType
AX_X = mybir.AxisListType.X

C_ID, C_ONES_D, C_ONES_H, C_IOTA, C_PERM, C_I16, C_EPS, C_HPI = 0, 128, 256, 384, 512, 640, 656, 657
C_N = 658
M_T, M_COS, M_SIN, M_N = 0, TL, TL + SEQ, TL + 2 * SEQ
N_BMOD, N_G, N_FG, N_LAM, N_DEC, N_D, N_C = 0, 96, 128, 136, 328, 344, 352
N_N = 368
TP1 = 6.28125
TP2 = float(np.float32(2 * math.pi - TP1))
TP3 = float(np.float32(2 * math.pi - TP1 - float(np.float32(2 * math.pi - TP1))))
INV2PI = float(np.float32(1 / (2 * math.pi)))
TWO_PI_IN = 6.283185
S_R, S_RHO, S_RHI, S_RLO, S_BR, S_BI, S_NBR, S_NBI = range(8)
S_DT, S_TH, S_T0, S_T1, S_T2, S_COS, S_SIN, S_K = range(8, 16)

STAGES = [("mod", 0, 0)]
for _l in range(DEPTH):
    STAGES += [("norm1", _l, 0), ("front", _l, 0), ("s5", _l, 0), ("ret", _l, 0), ("merge", _l, 0)]
    for _h in ((1, 0) if _l < DEPTH - 1 else (1,)):
        STAGES += [("norm2", _l, _h), ("route", _l, _h), ("gates", _l, _h), ("experts", _l, _h)]
STAGES += [("final", 0, 1)]


def next_mod(stage):
    return {("route", 0, 1): 0, ("route", 0, 0): 1}.get(stage)


def units_of(stage):
    return {"mod": MOD_UNITS, "front": FRONT_UNITS, "s5": 4 * S5_ITER, "ret": DIST_UNIT,
            "merge": MERGE_UNITS + OUT_UNITS, "route": WQ_UNITS + MOD_UNITS // 2 * (next_mod(stage) is not None), "experts": NK}.get(stage[0], 0)


def first_units():
    base, out = 0, {}
    for st in STAGES:
        out[st] = base
        base += units_of(st)
    return out


BASE = first_units()
X_COUNT, _n = {}, 0
for _st in STAGES:
    X_COUNT[_st] = _n
    _n += OUT_UNITS if _st[0] == "merge" else _st[0] == "experts"
S5_LINKS = 36


def passes_before(st):
    return [s for s in STAGES if s[0] == "norm2"].index(("norm2", st[1], st[2]))


def passes_done(st):
    return sum(s[0] == "experts" for s in STAGES[:STAGES.index(st)])


def norms_before(st):
    return [s for s in STAGES if s[0] in ("norm1", "norm2", "final")].index(st)


class Chain:

    def __init__(self, eng, sem):
        self.eng, self.sem, self.n, self.extra = eng, sem, 0, None

    def value(self):
        return self.n if self.extra is None else self.extra + self.n

    def link(self, ins):
        self.mark(ins)
        self.eng.wait_ge(self.sem, self.value())

    def mark(self, ins):
        ins.then_inc(self.sem, 1)
        self.n += 1

    def loop(self, i, per):
        self.start, self.per, self.extra = self.n, per, i * per

    def end(self, turns):
        assert self.n - self.start == self.per, (self.n - self.start, self.per)
        self.n, self.extra = self.start + turns * self.per, None


def build_program(nc, a, until=None):
    stages = STAGES if until is None else STAGES[:until]
    ctx = ExitStack()
    with ctx:
        def sb(name, shape, dt=F32, on=ctx):
            return on.enter_context(nc.sbuf_tensor(name, shape, dt))

        def sem(name):
            return ctx.enter_context(nc.semaphore(name))

        lend = ExitStack()
        xT = sb("xT", [P, KD, TL], on=lend)
        lend.close()
        lend = ExitStack()
        hot = sb("hot", [P, 4, 2, 4, P], on=lend)
        lend.close()
        ehi = sb("ehi", [P, 4, DM], F32R)
        cst = sb("cst", [P, C_N])
        par = sb("par", [P, N_N])
        s5p = sb("s5p", [P, 8, DEPTH * 2 * NT + 1])
        lg = sb("lg", [P, DEPTH * 2 * RH])
        modT = sb("modT", [P, DEPTH, 6, KD, 2])
        gain = sb("gain", [P, DEPTH, 2, KD, 2])
        lend = ExitStack()
        ring = sb("ring", [P, RING, SLOT], on=lend)
        lend.close()
        elo = sb("elo", [P, RING, SLOT], F32R)
        zeros = sb("zeros", [P, P])
        mix = ExitStack()
        mcst = sb("mcst", [P, M_N], on=mix)
        hT = sb("hT", [P, KD, TL], on=mix)
        uT = sb("uT", [P, CT, TL], on=mix)
        vN = sb("vN", [P, TL // P, SSM], on=mix)
        kT = sb("kT", [P, RH, TL], on=mix)
        pj = sb("pj", [P, 24, TL], on=mix)
        qT, gT, gsT, grT = pj[:, 0:4, :], pj[:, 4:8, :], pj[:, 8:16, :], pj[:, 16:24, :]
        sub = ExitStack()
        mrow0 = sb("mrow0", [2, 6 * DM], on=sub)
        s5w = sb("s5w", [P, 8, DEPTH * 2 * NT], on=sub)
        s5k = sb("s5k", [P, DEPTH * 2 * NT], I32, on=sub)
        sub.close()
        sub = ExitStack()
        sq1 = sb("sq1", [P, KD, TL], on=sub)
        sb("rows_space", [P, 3 * DM], on=sub)
        rs1 = sb("rs1", [P, TL], on=sub)
        sub.close()
        sub = ExitStack()
        phase = sb("phase", [P, 2, TL], on=sub)
        turns = sb("turns", [P, 2, TL], I32, on=sub)
        absp = sb("absp", [P, 2, TL], on=sub)
        tab = sb("tab", [P, 2, 2, TL], on=sub)
        bu = sb("bu", [P, 2, 2, TL], on=sub)
        rot = sb("rot", [P, 2, TL], on=sub)
        gst = sb("gst", [P, 2, 2, TL], on=sub)
        prod = sb("prod", [P, 2, 4, TL], on=sub)
        cpr = sb("cpr", [P, 2, 3, 4, 32], on=sub)
        ctmp = sb("ctmp", [P, 2, 4, 32], on=sub)
        sub.close()
        sub = ExitStack()
        decay = sb("decay", [P, RH, 2, 512], on=sub)
        dtmp = sb("dtmp", [P, RH, 512], on=sub)
        sd = sb("sd", [P, 2, 6, 256], on=sub)
        oT = sb("oT", [P, RH, TL], on=sub)
        osq = sb("osq", [P, RH, TL], on=sub)
        sub.close()
        sub = ExitStack()
        mT = sb("mT", [P, KD, TL], on=sub)
        sgb = sb("sgb", [P, 2, TL], on=sub)
        mt1 = sb("mt1", [P, 2, TL], on=sub)
        mt2 = sb("mt2", [P, 2, TL], on=sub)
        sub.close()
        mix.close()
        peer = ExitStack()
        h2h = sb("h2h", [P, KD, 256], F32R, on=peer)
        h2l = sb("h2l", [P, KD, 256], F32R, on=peer)
        tiny = ExitStack()
        idxT = sb("idxT", [P, 3, 256], on=tiny)
        tiny.close()
        tiny = ExitStack()
        actT = sb("actT", [P, 2, 256], on=tiny)
        wf = sb("wf", [P, 2, 256], on=tiny)
        wh = sb("wh", [P, 2, 256], F32R, on=tiny)
        wl = sb("wl", [P, 2, 256], F32R, on=tiny)
        tiny.close()
        sb("tiny_space", [P, 4 * 2 * 256], on=peer)
        over = ExitStack()
        gate = sb("gate", [P, NK, 256], on=over)
        over.close()
        over = ExitStack()
        sq2 = sb("sq2", [P, KD, 256], on=over)
        rs2 = sb("rs2", [P, 256], on=over)
        h2T = sb("h2T", [P, KD, 256], on=over)
        mrow1 = sb("mrow1", [2, 6 * DM], on=over)
        qrT = sb("qrT", [P, NH, 256], on=over)
        keys = sb("keys", [P, NH, 256], on=over)
        sc = sb("sc", [P, 2, NH * 2, NK], on=over)
        sc2 = sb("sc2", [P, 4, NK], on=over)
        cand = sb("cand", [P, 2, CANDS], on=over)
        cand2 = sb("cand2", [P, 2, CANDS], on=over)
        top = sb("top", [P, 2, NH * 2, TOPK], on=over)
        topi = sb("topi", [P, 2, NH * 2, TOPK], U32, on=over)
        topf = sb("topf", [P, 2, NH * 2, TOPK], on=over)
        best = sb("best", [P, 2, NH, TOPK], on=over)
        besti = sb("besti", [P, 2, NH, TOPK], U32, on=over)
        place = sb("place", [P, 2 * NH * TOPK], on=over)
        placei = sb("placei", [P, 2, 2 * NH * TOPK], U32, on=over)
        rank = sb("rank", [P, 2, 2, NH * TOPK], on=over)
        eq = sb("eq", [P, 2, 2, NH * TOPK, TOPK], on=over)
        pick = sb("pick", [P, 2, 3, NH * TOPK], on=over)
        ssum = sb("ssum", [P, 2 * NH], on=over)
        over.close()
        over = ExitStack()
        yout = sb("yout", [P, 2, DM], on=over)
        over.close()
        over = ExitStack()
        fout = sb("fout", [P, KD, 256], on=over)
        over.close()
        peer.close()
        ps = ctx.enter_context(nc.psum_tensor("ps", [P, 8, 512], F32))

        const_in = sem("const_in")
        unit_in = [sem(f"unit_in{s}") for s in range(RING)]
        keys_in = sem("keys_in")
        mcst_in = sem("mcst_in")
        x_held = sem("x_held")
        x_low_back, x_half_back, x_back = sem("x_low_back"), sem("x_half_back"), sem("x_back")
        stored = sem("stored")
        used = [sem(f"used{s}") for s in range(RING)]
        dve_own, act_own = sem("dve_own"), sem("act_own")
        cond_ready, mod_row, mod_col, mod_done = sem("cond_ready"), sem("mod_row"), sem("mod_col"), sem("mod_done")
        s5_lam, s5_angle, s5_trig = sem("s5_lam"), sem("s5_angle"), sem("s5_trig")
        sq_ready, mean_ready, std_ready, h_ready = sem("sq_ready"), sem("mean_ready"), sem("std_ready"), sem("h_ready")
        h_scaled = sem("h_scaled")
        proj_out = sem("proj_out")
        bu_ready, bu_copied = sem("bu_ready"), sem("bu_copied")
        phase_ready, table_ready = sem("phase_ready"), sem("table_ready")
        g_ready, prod_ready, cprime_ready, readout = sem("g_ready"), sem("prod_ready"), sem("cprime_ready"), sem("readout")
        turned = sem("turned")
        turns_ready, y_out = sem("turns_ready"), sem("y_out")
        eq_ready, eq_times = sem("eq_ready"), sem("eq_times")
        hot_eq = sem("hot_eq")
        rope_ps, roped = sem("rope_ps"), sem("roped")
        decay_arg, decay_ready = sem("decay_arg"), sem("decay_ready")
        score_ps, sd_ready, o_ps, o_copied = sem("score_ps"), sem("sd_ready"), sem("o_ps"), sem("o_copied")
        osq_ready, omean_ready, ostd_ready, yr_ready, ys_ready = (
            sem("osq_ready"), sem("omean_ready"), sem("ostd_ready"), sem("yr_ready"), sem("ys_ready"))
        gates_on, sg_ready, m_ready, x_ready = sem("gates_on"), sem("sg_ready"), sem("m_ready"), sem("x_ready")
        qr_ready, score_out, score_ready = sem("qr_ready"), sem("score_out"), sem("score_ready")
        exp_in, exp_out, pick_ready, pick_ps, pick_col = (
            sem("exp_in"), sem("exp_out"), sem("pick_ready"), sem("pick_ps"), sem("pick_col"))
        hot_ready, gate_ps, gate_ready = sem("hot_ready"), sem("gate_ps"), sem("gate_ready")
        uhi_ready, ulo_ready, vhi_ready, vlo_ready = sem("uhi_ready"), sem("ulo_ready"), sem("vhi_ready"), sem("vlo_ready")
        a_ready, act_ready, w_ready, y_ready, y_col = (
            sem("a_ready"), sem("act_ready"), sem("w_ready"), sem("y_ready"), sem("y_col"))
        y_copied = sem("y_copied")
        fin_ready = sem("fin_ready")

        ident = cst[:, C_ID:C_ID + P]
        iota = cst[:, C_IOTA:C_IOTA + P]
        eps = cst[:, C_EPS:C_EPS + 1]

        def sp_(k):
            return s5p[:, k, 0:DEPTH * 2 * NT] if k < 8 else s5w[:, k - 8, :]

        def lane(k, n, l, i):
            return s5p[:, k, bass.ds(i * 4 + ((2 * l + n % 2) * NT + n // 2), 1)]

        def arrived(eng, u, i=None, per=0):
            n = 16 * (u // RING + 1)
            eng.wait_ge(unit_in[u % RING], n if i is None else i * (16 * per // RING) + n)

        def unit_used(eng, u, i=None, per=0):
            n = u // RING + 1
            eng.wait_ge(used[u % RING], n if i is None else i * (per // RING) + n)

        def slot(u, k, n):
            return ring[:, u % RING, 0:k * n].rearrange("p (k n) -> p k n", n=n)

        CREDIT = {s.name: n for s, n in ((readout, 2), (g_ready, 4), (phase_ready, 3), (table_ready, 2), (prod_ready, 2), (bu_copied, 1),
                                         (mod_row, 4), (gate_ready, 4), (gate_ps, 4), (w_ready, 2), (y_out, 1))}

        def count(eng, s, n):
            eng.wait_ge(s, n + CREDIT[s.name])

        def pool_turns(l):
            return layer_width(l)[0] > 0

        def layer_width(l):
            return (0, TL) if l < DEPTH - 1 else (CTX, TL)

        block = ctx.enter_context(nc.Block())

        @block.sync
        def _(sp):
            sp.dma_start(cst[:, :], a["consts"]).then_inc(const_in, 16)
            sp.dma_start(par[:, :], a["params"]).then_inc(const_in, 16)
            sp.dma_start(xT[:, :, :], a["x_t"]).then_inc(const_in, 16)

            def load(u, src, i=None, per=0):
                n = u // RING
                if i is None:
                    if n >= 1:
                        sp.wait_ge(used[u % RING], n)
                else:
                    sp.wait_ge(used[u % RING], i * (per // RING) + n)
                w = src.shape[-1]
                sp.dma_start(ring[:, u % RING, 0:w], src).then_inc(unit_in[u % RING], 16)

            def stream(u, src, count):
                head = RING if u < RING else 0
                for k in range(head):
                    load(u + k, src[k])
                turns_ = (count - head) // RING
                with sp.Fori(0, turns_) as i:
                    for k in range(RING):
                        load(u + head + k, src[bass.ds(i * RING + (head + k), 1)].rearrange("o p n -> (o p) n"), i, RING)

            for st in stages:
                kind, l, h = st
                u = BASE[st]
                if kind == "mod":
                    stream(u, a["w_mod"][0], MOD_UNITS)
                elif kind == "front":
                    for k in range(FRONT_UNITS):
                        load(u + k, a["w_front"][l, k])
                    sp.wait_ge(h_ready, KD * (norms_before(("norm1", l, 0)) + 1))
                    sp.dma_start(mcst[:, :], a["mixer_consts"]).then_inc(mcst_in, 16)
                elif kind == "s5":
                    load(u, a["s5_bc"][l, 0])
                    for k in range(3):
                        load(u + 1 + k, a["w_side"][l, k])
                    with sp.Fori(1, S5_ITER) as i:
                        for k in (0, None, 1, 2):
                            if k is None:
                                load(u, a["s5_bc"][l, bass.ds(i, 1)].rearrange("o p n -> (o p) n"), i, 4)
                            else:
                                load(u + 1 + k, a["w_side"][l, bass.ds(i * 3 + k, 1)].rearrange("o p n -> (o p) n"), i, 4)
                elif kind == "ret":
                    load(u, a["dist"])
                elif kind == "merge":
                    stream(u, a["w_merge"][l], MERGE_UNITS)
                    stream(u + MERGE_UNITS, a["w_out"][l], OUT_UNITS)
                elif kind == "route":
                    stream(u, a["w_q"][l], WQ_UNITS)
                    sp.wait_ge(h_ready, KD * (norms_before(("norm2", l, h)) + 1))
                    sp.dma_start(keys[:, :, :], a["keys"][l]).then_inc(keys_in, 16)
                    half = next_mod(st)
                    if half is not None:
                        stream(u + WQ_UNITS, a["w_mod"][l + 1, MOD_UNITS // 2 * half:MOD_UNITS // 2 * (half + 1)], MOD_UNITS // 2)
                elif kind == "experts":
                    stream(u, a["experts"][l], NK)
                elif kind == "final":
                    sp.wait_ge(fin_ready, KD)
                    sp.dma_start(a["out"], fout[:, :, :]).then_inc(stored, 16)
                    sp.wait_ge(stored, 16)

        @block.gpsimd
        def _(pool):
            for st in stages:
                kind, l, h = st
                if kind == "s5":
                    lo = layer_width(l)[0]
                    w = TL - lo

                    def turned_part(n, i):
                        count(pool, table_ready, i * 8 + (l * 33 + n + 1))
                        count(pool, bu_copied, i * 4 + (l * 16 + n // 2 + 1))
                        dst, b_, t_ = rot[:, 1, :], bu[:, (n // 2) % 2, 0, :], tab[:, n % 2, 1, :]
                        if n % 2:
                            dst, b_, t_ = (x.rearrange("p (h t) -> p h t", t=256) for x in (dst, b_, t_))
                            b_ = b_[:, :, ::-1]
                        pool.tensor_tensor(dst, b_, t_, ALU.mult).then_inc(turned, 1)

                    def products(n, i):
                        d = n % 2
                        count(pool, readout, i * 8 + (l * 32 + n - 1))
                        for k in range(2):
                            src = gst[:, d, :, lo:TL]
                            t = tab[:, d, :, lo:TL] if k == 0 else tab[:, d, ::-1, lo:TL]
                            for c in range(2):
                                dst = prod[:, d, 2 * k + c, 0:w]
                                s_, t_ = src[:, c, :], t[:, c, :]
                                if d == 1:
                                    dst = dst.rearrange("p (h t) -> p h t", t=256)[:, :, ::-1]
                                    s_ = s_.rearrange("p (h t) -> p h t", t=256)
                                    t_ = t_.rearrange("p (h t) -> p h t", t=256)
                                last = pool.tensor_tensor(dst, s_, t_, ALU.mult)
                        last.then_inc(prod_ready, 1)

                    def turn(i, ahead):
                        for n in range(8):
                            count(pool, g_ready, i * 8 + (l * 32 + n + 1))
                            if pool_turns(l) and n < 7:
                                turned_part(n + 1, i)
                            elif pool_turns(l) and ahead:
                                turned_part(0, i + 1)
                            products(n, i)

                    if pool_turns(l):
                        turned_part(0, 0)
                    with pool.Fori(0, S5_ITER - 1) as i:
                        turn(i, True)
                    turn(S5_ITER - 1, False)
                elif kind == "route":
                    p = passes_before(st)
                    pool.wait_ge(h_ready, KD * (norms_before(("norm2", l, h)) + 1))
                    pool.dma_start(a["x_scratch"], xT[:, :, :]).then_inc(x_held, 16)
                    for tb in range(2):
                        pool.wait_ge(eq_ready, 2 * p + tb + 1)
                        e4 = eq[:, tb, 0, :, :].rearrange("p (h k) a -> p h k a", h=NH)
                        t4 = topf[:, tb, 0::2, :].unsqueeze(2).to_broadcast([P, NH, TOPK, TOPK])
                        pool.tensor_tensor(e4, e4, t4, ALU.mult).then_inc(eq_times, 1)
                elif kind == "gates":
                    p = passes_before(st)
                    with pool.Fori(0, 16) as i:
                        for g in range(4):
                            pool.wait_ge(hot_eq, i * 4 + (64 * p + g + 1))
                            pool.wait_ge(x_held, 16 * (p + 1))
                            g_ = idxT[:, 2, bass.ds(i * 16 + 4 * g, 4)].unsqueeze(2).to_broadcast([P, 4, P])
                            o = hot[:, g, 1, :, :]
                            pool.tensor_tensor(o, o, g_, ALU.mult).then_inc(hot_ready, 1)
                elif kind == "experts":
                    p = passes_before(st)
                    lo_, up_ = slice(0, KD // 2), slice(KD // 2, KD)
                    mine, other = slice(CTX * h, CTX * h + 256), slice(CTX - CTX * h, CTX - CTX * h + 256)
                    pool.wait_ge(a_ready, NK * (p + 1))
                    pool.dma_start(xT[:, lo_, :], a["x_scratch"][:, lo_, :]).then_inc(x_low_back, 16)
                    pool.wait_ge(y_ready, p + 1)
                    pool.dma_start(xT[:, up_, mine], a["x_scratch"][:, up_, mine]).then_inc(x_half_back, 16)
                    pool.dma_start(xT[:, up_, other], a["x_scratch"][:, up_, other]).then_inc(x_back, 16)

        @block.tensor
        def _(pe):
            pe.wait_ge(const_in, 48)

            def mm(out, w, x, start, stop, **k):
                return pe.matmul(out, w, x, start=start, stop=stop, **k)

            def norm_mean(st, sqb, w):
                n = norms_before(st)
                for k in range(KD):
                    pe.wait_ge(sq_ready, KD * n + k + 1)
                    last = mm(ps[:, 7, 0:w], cst[:, C_ONES_D:C_ONES_D + P], sqb[:, k, :], k == 0, k == KD - 1)
                last.then_inc(mean_ready, 1)

            def mod_rows(u, l, first, n, bank):
                with pe.Fori(0, n // RING) as i:
                    for k in range(RING):
                        v = u + k
                        arrived(pe, v, i, RING)
                        count(pe, mod_row, i * RING + (l * MOD_UNITS + first + k - 3))
                        w = slot(v, KD, 256)
                        for c in range(KD):
                            last = mm(ps[0:2, bank + k, 0:256], par[:, N_C + 2 * c:N_C + 2 * c + 2], w[:, c, :],
                                      c == 0, c == KD - 1)
                        last.then_inc(used[v % RING], 1)

            def mod_columns(l, s0, s1, row, bank):
                count(pe, mod_row, l * MOD_UNITS + MOD_UNITS // 6 * s1)
                for c in range(s0 * KD, s1 * KD):
                    last = mm(ps[:, bank, 2 * c:2 * c + 2], row[0:2, c * P:(c + 1) * P], ident[0:2, 0:2], True, True)
                last.then_inc(mod_col, 1)

            for st in stages:
                kind, l, h = st
                u = BASE[st]
                if kind == "mod":
                    norm_mean(("norm1", 0, 0), hT, TL)
                    pe.wait_ge(cond_ready, 1)
                    mod_rows(u, 0, 0, MOD_UNITS, 0)
                    mod_columns(0, 0, 6, mrow0, 4)
                elif kind == "norm1" and l:
                    norm_mean(st, sq1, TL)
                elif kind == "norm2":
                    norm_mean(st, sq2, 256)
                elif kind == "final":
                    norm_mean(st, sq2, 256)
                elif kind == "front":
                    for k in range(FRONT_UNITS):
                        arrived(pe, u + k)
                        if k >= 2:
                            pe.wait_ge(proj_out, 18 * l + k - 1)
                        b = 2 * (k % 2)
                        w = slot(u + k, 2 * KD, P)
                        if k in (2, 3):
                            for t in range(TL // P):
                                for j in range(2):
                                    for c in range(KD):
                                        last = mm(ps[:, b + t // 2, (t % 2) * 256 + j * P:(t % 2) * 256 + j * P + P],
                                                  hT[:, c, t * P:(t + 1) * P], w[:, j * KD + c, :], c == 0, c == KD - 1)
                        else:
                            for j in range(2):
                                for c in range(KD):
                                    if k + j == 0:
                                        pe.wait_ge(h_ready, KD * norms_before(("norm1", l, 0)) + c + 1)
                                    last = mm(ps[:, b + j, :], w[:, j * KD + c, :], hT[:, c, :], c == 0, c == KD - 1)
                        last.then_inc(used[(u + k) % RING], 1)
                elif kind == "s5":
                    lo, hi = layer_width(l)
                    w_ = hi - lo
                    pe.wait_ge(proj_out, 18 * l + FRONT_UNITS)
                    bc = slot(u, 8, P)

                    def drive(q, i):
                        count(pe, bu_copied, i * 4 + (l * 16 + q))
                        for c in range(2):
                            last = mm(ps[:, 4 + c, :], bc[:, 2 * q + c, :],
                                      uT[:, bass.ds(i, 1), :].rearrange("p o t -> p (o t)"), True, True)
                        last.then_inc(bu_ready, 1)

                    def side(k, i):
                        v = u + 1 + k
                        arrived(pe, v, i, 4)
                        pe.wait_ge(proj_out, i * 3 + (18 * l + FRONT_UNITS + max(k - 1, 0)))
                        b = 2 * (k % 2)
                        w = slot(v, 2 * KD, P)
                        for j in range(2):
                            for c in range(KD):
                                last = mm(ps[:, b + j, 0:w_], w[:, j * KD + c, :], hT[:, c, lo:hi],
                                          c == 0, c == KD - 1)
                        last.then_inc(used[v % RING], 1)

                    def read(q, i):
                        for d in range(2):
                            n = 2 * q + d
                            count(pe, prod_ready, i * 8 + (l * 32 + n + 1))
                            pe.wait_ge(cprime_ready, i + (l * 4 + 1))
                            for k in range(4):
                                last = mm(ps[32 * q:32 * q + 32, 6, 0:w_], cpr[:, d, (0, 1, 2, 2)[k], q, :],
                                          prod[:, d, k, 0:w_], n % 2 == 0 and k == 0, d == 1 and k == 3)
                                if n == 0 and k == 0:
                                    last.then_inc(used[u % RING], 1)
                            last.then_inc(readout, 1)

                    def turn(i, ahead):
                        side(0, i)
                        drive(3, i)
                        count(pe, y_out, i + 4 * l)
                        read(0, i)
                        side(1, i)
                        if ahead:
                            arrived(pe, u, i + 1, 4)
                            drive(0, i + 1)
                        read(1, i)
                        side(2, i)
                        if ahead:
                            drive(1, i + 1)
                        read(2, i)
                        if ahead:
                            drive(2, i + 1)
                        read(3, i)

                    arrived(pe, u)
                    for q in range(3):
                        drive(q, 0)
                    with pe.Fori(0, S5_ITER - 1) as i:
                        turn(i, True)
                    turn(S5_ITER - 1, False)
                elif kind == "ret":
                    lo = layer_width(l)[0]
                    pe.wait_ge(proj_out, 18 * (l + 1))
                    for j, src in enumerate((qT, kT)):
                        for hd in range(RH):
                            last = mm(ps[:, 2 * j + hd // 2, (hd % 2) * 256:(hd % 2) * 256 + 256],
                                      cst[:, C_PERM:C_PERM + P], src[:, hd, CTX:TL], True, True)
                        last.then_inc(rope_ps, 1)
                    pe.wait_ge(roped, 2 * (l + 1))

                    def outs(hd):
                        b = 3 * (hd % 2)
                        pe.wait_ge(sd_ready, l * RH + hd + 1)
                        if hd >= 2:
                            pe.wait_ge(o_copied, l * RH + hd - 1)
                        ob = ps[:, 6 + hd % 2, :]
                        for t in range(4):
                            last = mm(ob[:, CTX:TL], vN[:, t, hd * P:(hd + 1) * P], sd[:, hd % 2, t, :], t == 0, t == 3)
                        if lo == 0:
                            for t in range(2):
                                last = mm(ob[:, 0:CTX], vN[:, t, hd * P:(hd + 1) * P], sd[:, hd % 2, 4 + t, :],
                                          t == 0, t == 1)
                        last.then_inc(o_ps, 1)

                    for hd in range(RH):
                        b = 3 * (hd % 2)
                        if hd >= 2:
                            pe.wait_ge(sd_ready, l * RH + hd - 1)
                        for t in range(4):
                            last = mm(ps[:, b + t // 2, (t % 2) * 256:(t % 2) * 256 + 256], kT[:, hd, t * P:(t + 1) * P],
                                      qT[:, hd, CTX:TL], True, True)
                        if lo == 0:
                            for t in range(2):
                                last = mm(ps[:, b + 2, t * 256:t * 256 + 256], kT[:, hd, t * P:(t + 1) * P],
                                          qT[:, hd, 0:CTX], True, True)
                        last.then_inc(score_ps, 1)
                        if hd >= 1:
                            outs(hd - 1)
                    outs(RH - 1)
                    pe.wait_ge(osq_ready, l + 1)
                    for hd in range(RH):
                        last = mm(ps[:, hd, lo:TL], cst[:, C_ONES_H:C_ONES_H + P], osq[:, hd, lo:TL], True, True)
                    last.then_inc(omean_ready, 1)
                elif kind == "merge":
                    lo, hi = layer_width(l)
                    w_ = hi - lo
                    pe.wait_ge(ys_ready, l + 1)
                    pe.wait_ge(yr_ready, l + 1)
                    for j in range(MERGE_UNITS):
                        arrived(pe, u + j)
                        if j >= 2:
                            pe.wait_ge(m_ready, KD * l + j - 1)
                        w = slot(u + j, 12, P)
                        for part in range(3):
                            src = gT if part == 2 else uT
                            for c in range(CT):
                                last = mm(ps[:, 2 * part + j % 2, 0:w_], w[:, 4 * part + c, :], src[:, c, lo:hi],
                                          c == 0, c == CT - 1)
                        last.then_inc(used[(u + j) % RING], 1)
                    pe.wait_ge(m_ready, KD * (l + 1))
                    for j in range(OUT_UNITS):
                        v = u + MERGE_UNITS + j
                        arrived(pe, v)
                        if j >= 2:
                            pe.wait_ge(x_ready, X_COUNT[st] + j - 1)
                        w = slot(v, 2 * KD, P)
                        for t in range(2):
                            for c in range(KD):
                                last = mm(ps[:, 2 * (j % 2) + t, 0:w_], w[:, t * KD + c, :], mT[:, c, 0:w_],
                                          c == 0, c == KD - 1)
                        last.then_inc(used[v % RING], 1)
                elif kind == "route":
                    p = passes_before(st)

                    def queries(k):
                        arrived(pe, u + k)
                        if k >= 2:
                            pe.wait_ge(qr_ready, WQ_UNITS * p + k - 1)
                        w = slot(u + k, 2 * KD, P)
                        for j in range(2):
                            for c in range(KD):
                                if k + j == 0:
                                    pe.wait_ge(h_ready, KD * norms_before(("norm2", l, h)) + c + 1)
                                last = mm(ps[:, k % 2, j * 256:j * 256 + 256], w[:, j * KD + c, :], h2T[:, c, :],
                                          c == 0, c == KD - 1)
                        last.then_inc(used[(u + k) % RING], 1)

                    def scores(k):
                        pe.wait_ge(qr_ready, WQ_UNITS * p + k + 1)
                        if k >= 2:
                            pe.wait_ge(score_ready, WQ_UNITS * p + k - 1)
                        for tb in range(2):
                            for j in range(2):
                                last = mm(ps[:, 2 + 2 * (k % 2) + tb, j * 256:j * 256 + 256],
                                          qrT[:, 2 * k + j, tb * P:(tb + 1) * P], keys[:, 2 * k + j, :], True, True)
                        last.then_inc(score_out, 1)

                    queries(0)
                    pe.wait_ge(keys_in, 16 * (p + 1))
                    for k in range(1, WQ_UNITS):
                        queries(k)
                        scores(k - 1)
                    scores(WQ_UNITS - 1)
                    pe.wait_ge(score_ready, WQ_UNITS * (p + 1))
                    half = next_mod(st)
                    if half is not None:
                        mod_rows(u + WQ_UNITS, l + 1, MOD_UNITS // 2 * half, MOD_UNITS // 2, 4)
                        mod_columns(l + 1, 3 * half, 3 * half + 3, mrow1, 2)
                    pe.wait_ge(pick_ready, p + 1)
                    for tb in range(2):
                        for k in range(3):
                            last = pe.transpose(ps[:, tb, k * P:(k + 1) * P], pick[:, tb, k, :], ident)
                    last.then_inc(pick_ps, 1)
                elif kind == "gates":
                    p = passes_before(st)
                    with pe.Fori(0, 16) as i:
                        for g in range(4):
                            count(pe, gate_ready, i * 4 + (64 * p + g - 3))
                            pe.wait_ge(hot_ready, i * 4 + (64 * p + g + 1))
                            for t in range(4):
                                last = mm(ps[:, 4 + g, t * P:(t + 1) * P], hot[:, g, 0, t, :], hot[:, g, 1, t, :],
                                          True, True)
                            last.then_inc(gate_ps, 1)
                elif kind == "experts":
                    p = passes_before(st)
                    count(pe, gate_ready, 64 * (p + 1))
                    pe.wait_ge(pick_col, p + 1)
                    for b in range(4):
                        mm(ps[:, b, :], zeros[:, :], cst[:, 0:512], True, False)

                    def up(k, i):
                        v = u + k
                        pe.wait_ge(ulo_ready, i * RING + (NK * p + k + 1))
                        hi, lo_ = ehi[:, k % 2, :], elo[:, v % RING, 0:DM]
                        for c in range(KD):
                            s_ = slice(c * P, (c + 1) * P)
                            o = ps[:, 4 + k % 4, 0:256]
                            mm(o, hi[:, s_], h2h[:, c, :], c == 0, False)
                            mm(o, hi[:, s_], h2l[:, c, :], False, False)
                            last = mm(o, lo_[:, s_], h2h[:, c, :], False, c == KD - 1)
                        last.then_inc(a_ready, 1)

                    def down(k, i):
                        v = u + k
                        pe.wait_ge(vlo_ready, i * RING + (NK * p + k + 1))
                        count(pe, w_ready, i * RING + (NK * p + k + 1))
                        hi, lo_ = ehi[:, 2 + k % 2, :], elo[:, v % RING, DM:2 * DM]
                        for tb in range(2):
                            t_ = slice(tb * P, (tb + 1) * P)
                            for w_, val in ((wh, hi), (wh, lo_), (wl, hi)):
                                for n in range(2):
                                    last = mm(ps[:, 2 * tb + n, :], w_[:, k % 2, t_], val[:, n * 512:(n + 1) * 512],
                                              False, False)
                        last.then_inc(used[v % RING], 1)

                    up(0, 0)
                    with pe.Fori(0, NK // RING - 1) as i:
                        for k in range(RING):
                            up(k + 1, i)
                            down(k, i)
                    for k in range(RING):
                        if k < RING - 1:
                            up(k + 1, NK // RING - 1)
                        down(k, NK // RING - 1)
                    for b in range(4):
                        last = mm(ps[:, b, :], zeros[:, :], cst[:, 0:512], False, True)
                    last.then_inc(y_ready, 1)
                    for tb in range(2):
                        pe.wait_ge(y_copied, 2 * p + tb + 1)
                        for d in range(KD):
                            last = pe.transpose(ps[:, 4 + d // 2, (d % 2) * 256 + tb * P:(d % 2) * 256 + tb * P + P],
                                                yout[:, tb, d * P:(d + 1) * P], ident)
                    last.then_inc(y_col, 1)

        @block.scalar
        def _(act):
            own = Chain(act, act_own)
            act.wait_ge(const_in, 48)

            def squares(st, sqb, lo, w):
                for k in range(KD):
                    act.activation(sqb[:, k, :], xT[:, k, lo:lo + w], ACT.Square).then_inc(sq_ready, 1)

            def stddev(st, rs, w):
                n = norms_before(st)
                act.wait_ge(mean_ready, n + 1)
                act.activation(rs[:, 0:w], ps[:, 7, 0:w], ACT.Sqrt, bias=eps).then_inc(std_ready, 1)

            def shifted(st, dst, w, lo, row):
                n = norms_before(st)
                for k in range(KD):
                    act.wait_ge(h_scaled, KD * n + k + 1)
                    for hf in range(w // 256):
                        side = hf if w > 256 else lo // CTX
                        d = dst[:, k, hf * 256:hf * 256 + 256]
                        last = act.activation(d, d, ACT.Identity, bias=modT[:, st[1], row, k, side:side + 1])
                    last.then_inc(h_ready, 1)

            def mod_rows(u, row, first, n, bank):
                with act.Fori(0, n // RING) as i:
                    for k in range(RING):
                        unit_used(act, u + k, i, RING)
                        act.activation(row[0:2, bass.ds(i * (256 * RING) + 256 * (first + k), 256)],
                                       ps[0:2, bank + k, 0:256], ACT.Copy).then_inc(mod_row, 1)

            for st in stages:
                kind, l, h = st
                u = BASE[st]
                if kind == "mod":
                    act.activation(par[:, N_C:N_C + 16], par[:, N_C:N_C + 16], ACT.Silu).then_inc(cond_ready, 1)
                    squares(("norm1", 0, 0), hT, 0, TL)
                    own.link(act.activation(lg[:, :], par[:, N_DEC:N_DEC + 16], ACT.Exp))
                    own.link(act.activation(lg[:, :], lg[:, :], ACT.Copy, scale=-1.0))
                    act.activation(sp_(S_DT), par[:, N_LAM + 128:N_LAM + 192], ACT.Exp).then_inc(s5_lam, 1)
                    act.wait_ge(s5_angle, 1)
                    act.activation(sp_(S_R), sp_(S_T0), ACT.Exp)
                    act.activation(sp_(S_SIN), sp_(S_T1), ACT.Sin)
                    act.activation(sp_(S_COS), sp_(S_T2), ACT.Sin, scale=-1.0,
                                   bias=cst[:, C_HPI:C_HPI + 1]).then_inc(s5_trig, 1)
                    stddev(("norm1", 0, 0), rs1, TL)
                    mod_rows(u, mrow0, 0, MOD_UNITS, 0)
                elif kind == "norm1":
                    if l:
                        act.wait_ge(x_ready, X_COUNT[st])
                        act.wait_ge(x_back, 16 * passes_done(st))
                        squares(st, sq1, 0, TL)
                        stddev(st, rs1, TL)
                    shifted(st, hT, TL, 0, 0)
                elif kind == "norm2" or kind == "final":
                    act.wait_ge(x_ready, X_COUNT[st])
                    if passes_done(st):
                        act.wait_ge(x_back, 16 * passes_done(st))
                    squares(st, sq2, CTX * h, 256)
                    stddev(st, rs2, 256)
                    if kind == "norm2":
                        shifted(st, h2T, 256, CTX * h, 3)
                elif kind == "front":
                    for k in range(FRONT_UNITS):
                        unit_used(act, u + k)
                        b = 2 * (k % 2)
                        if k in (2, 3):
                            dst = vN[:, :, (k - 2) * 256:(k - 1) * 256]
                            src = ps[:, b:b + 2, :].rearrange("p b (t c) -> p (b t) c", c=256)
                        elif k < 2:
                            dst, src = uT[:, 2 * k:2 * k + 2, :], ps[:, b:b + 2, :]
                        else:
                            dst, src = kT[:, 2 * k - 8:2 * k - 6, :], ps[:, b:b + 2, :]
                        act.activation(dst, src, ACT.Copy).then_inc(proj_out, 1)
                elif kind == "s5":
                    lo, hi = layer_width(l)
                    w_ = hi - lo
                    act.wait_ge(mcst_in, 16 * (l + 1))

                    def whole(n, i):
                        count(act, phase_ready, i * 8 + (l * 33 + n - 1))
                        act.activation(turns[:, n % 2, :], mcst[:, M_T:M_T + TL], ACT.Copy, scale=lane(S_RHO, n, l, i)
                                       ).then_inc(turns_ready, 1)

                    def table(n, i):
                        d = n % 2
                        count(act, phase_ready, i * 8 + (l * 33 + n + 1))
                        count(act, prod_ready, i * 8 + (l * 32 + n - 1))
                        own.link(act.activation(absp[:, d, :], phase[:, d, :], ACT.Abs))
                        act.activation(tab[:, d, 0, :], absp[:, d, :], ACT.Sin, scale=-TWO_PI_IN,
                                       bias=cst[:, C_HPI:C_HPI + 1])
                        act.activation(tab[:, d, 1, :], phase[:, d, :], ACT.Sin, scale=TWO_PI_IN
                                       ).then_inc(table_ready, 1)

                    def copy_drive(q, i):
                        act.wait_ge(bu_ready, i * 4 + (l * 16 + q + 1))
                        count(act, g_ready, i * 8 + (l * 32 + 2 * q - 2))
                        act.activation(bu[:, q % 2, :, :], ps[:, 4:6, :], ACT.Copy).then_inc(bu_copied, 1)

                    def turn(i, ahead):
                        for q in range(4):
                            if q < 3:
                                copy_drive(q + 1, i)
                            elif ahead:
                                copy_drive(0, i + 1)
                            for n in (2 * q, 2 * q + 1):
                                whole(n + 2, i)
                                table(n + 1, i)
                                if n % 2 == 0 and q > 0:
                                    k = q - 1
                                    unit_used(act, u + 1 + k, i, 4)
                                    b = 2 * (k % 2)
                                    act.activation(pj[:, bass.ds(i * 6 + 2 * k, 2), lo:hi], ps[:, b:b + 2, 0:w_],
                                                   ACT.Copy).then_inc(proj_out, 1)

                    whole(0, 0)
                    whole(1, 0)
                    table(0, 0)
                    copy_drive(0, 0)
                    with act.Fori(0, S5_ITER - 1) as i:
                        own.loop(i, 8)
                        turn(i, True)
                        own.end(S5_ITER - 1)
                    turn(S5_ITER - 1, False)
                elif kind == "ret":
                    lo, hi = layer_width(l)
                    dist = slot(u, 4, 512)
                    act.wait_ge(decay_arg, l + 1)
                    act.activation(decay[:, :, 0, :], decay[:, :, 0, :], ACT.Exp)
                    for hd in range(RH):
                        f, b = 2 * l * RH + hd, (2 * l + 1) * RH + hd
                        act.activation(decay[:, hd, 1, :], dist[:, 2, :], ACT.Exp, scale=lg[:, f:f + 1])
                        last = act.activation(dtmp[:, hd, :], dist[:, 3, :], ACT.Exp, scale=lg[:, b:b + 1])
                    last.then_inc(decay_ready, 1)
                    for hd in range(RH):
                        act.wait_ge(o_ps, l * RH + hd + 1)
                        act.activation(oT[:, hd, lo:hi], ps[:, 6 + hd % 2, lo:hi], ACT.Copy).then_inc(o_copied, 1)
                    act.wait_ge(o_copied, RH * (l + 1))
                    act.activation(osq[:, :, lo:hi], oT[:, :, lo:hi], ACT.Square).then_inc(osq_ready, 1)
                    act.wait_ge(omean_ready, l + 1)
                    act.activation(osq[:, :, lo:hi], ps[:, 0:4, lo:hi], ACT.Sqrt, bias=eps).then_inc(ostd_ready, 1)
                    count(act, y_out, 4 * (l + 1))
                    act.activation(uT[:, :, lo:hi], uT[:, :, lo:hi], ACT.Gelu_apprx_tanh).then_inc(ys_ready, 1)
                    act.activation(gT[:, :, lo:hi], gT[:, :, lo:hi], ACT.Silu).then_inc(gates_on, 1)
                    act.activation(pj[:, 8:24, lo:hi], pj[:, 8:24, lo:hi], ACT.Sigmoid).then_inc(gates_on, 1)
                elif kind == "merge":
                    lo, hi = layer_width(l)
                    w_ = hi - lo
                    act.wait_ge(yr_ready, l + 1)
                    for j in range(MERGE_UNITS):
                        unit_used(act, u + j)
                        if j >= 2:
                            act.wait_ge(m_ready, KD * l + j - 1)
                        act.activation(sgb[:, j % 2, 0:w_], ps[:, 2 + j % 2, 0:w_], ACT.Sigmoid).then_inc(sg_ready, 1)
                elif kind == "route":
                    p = passes_before(st)

                    def scores_out(k):
                        act.wait_ge(score_out, WQ_UNITS * p + k + 1)
                        b = 2 + 2 * (k % 2)
                        act.activation(sc[:, :, 4 * k:4 * k + 4, :].rearrange("p t a n -> p t (a n)"), ps[:, b:b + 2, :],
                                       ACT.Copy).then_inc(score_ready, 1)

                    for k in range(WQ_UNITS):
                        unit_used(act, u + k)
                        act.activation(qrT[:, 2 * k:2 * k + 2, :],
                                       ps[:, k % 2, :].rearrange("p (a b) -> p a b", a=2), ACT.Copy).then_inc(qr_ready, 1)
                        if k:
                            scores_out(k - 1)
                    scores_out(WQ_UNITS - 1)
                    half = next_mod(st)
                    if half is not None:
                        mod_rows(u + WQ_UNITS, mrow1, MOD_UNITS // 2 * half, MOD_UNITS // 2, 4)
                    act.wait_ge(exp_in, p + 1)
                    act.activation(best[:, :, :, :], best[:, :, :, :], ACT.Exp).then_inc(exp_out, 1)
                    act.wait_ge(pick_ps, p + 1)
                    act.activation(idxT[:, :, :].rearrange("p k (b t) -> p b k t", b=2),
                                   ps[:, 0:2, 0:3 * P].rearrange("p b (k t) -> p b k t", k=3), ACT.Copy
                                   ).then_inc(pick_col, 1)
                elif kind == "gates":
                    p = passes_before(st)
                    with act.Fori(0, 16) as i:
                        for g in range(4):
                            count(act, gate_ps, i * 4 + (64 * p + g + 1))
                            src = ps[:, 4 + g, :].rearrange("p (t n) -> p n t", n=P)
                            act.activation(gate[:, :, bass.ds(i * 16 + 4 * g, 4)], src, ACT.Copy).then_inc(gate_ready, 1)
                elif kind == "experts":
                    p = passes_before(st)
                    def u_high(k, i):
                        arrived(act, u + k, i, RING)
                        if k >= 2 or not isinstance(i, int):
                            act.wait_ge(a_ready, i * RING + (NK * p + k - 1))
                        act.activation(ehi[:, k % 2, :], ring[:, (u + k) % RING, 0:DM], ACT.Copy).then_inc(uhi_ready, 1)

                    act.wait_ge(x_held, 16 * (p + 1))
                    u_high(0, 0)
                    u_high(1, 0)

                    def step(k, i, ahead):
                        act.wait_ge(a_ready, i * RING + (NK * p + k + 1))
                        count(act, w_ready, i * RING + (NK * p + k - 1))
                        act.activation(actT[:, k % 2, :], ps[:, 4 + k % 4, 0:256], ACT.Gelu).then_inc(act_ready, 1)
                        unit_used(act, u + k - 2, i, RING)
                        act.activation(ehi[:, 2 + k % 2, :], ring[:, (u + k) % RING, DM:2 * DM], ACT.Copy
                                       ).then_inc(vhi_ready, 1)
                        if ahead:
                            u_high(k + 2, i)

                    with act.Fori(0, NK // RING - 1) as i:
                        for k in range(RING):
                            step(k, i, True)
                    for k in range(RING):
                        step(k, NK // RING - 1, k < 2)
                    act.wait_ge(y_ready, p + 1)
                    for tb in range(2):
                        act.activation(yout[:, tb, :], ps[:, 2 * tb:2 * tb + 2, :], ACT.Copy).then_inc(y_copied, 1)

        @block.vector
        def _(dve):
            own = Chain(dve, dve_own)
            link = own.link
            v = nc.vector
            dve.wait_ge(const_in, 48)
            for s_ in (readout, g_ready, phase_ready, table_ready, prod_ready, bu_copied, mod_row, gate_ready, gate_ps, w_ready, y_out):
                dve.sem_inc(s_, CREDIT[s_.name])


            def inverted(st, rs, w):
                dve.wait_ge(std_ready, norms_before(st) + 1)
                link(v.reciprocal(rs[:, 0:w], rs[:, 0:w]))

            def normed(st, rs, w, dst, lo, gains, done):
                if st != ("norm1", 0, 0):
                    inverted(st, rs, w)
                for k in range(KD):
                    for hf in range(w // 256):
                        side = hf if w > 256 else lo // CTX
                        s_ = slice(hf * 256, hf * 256 + 256)
                        last = v.scalar_tensor_tensor(dst[:, k, s_], xT[:, k, lo + hf * 256:lo + hf * 256 + 256],
                                                      gains(k, side), rs[:, s_], ALU.mult, ALU.mult)
                    last.then_inc(done, 1)

            def mod_tables(l, s0, s1, bank):
                n_done = 1 if l == 0 else 2 * l + s0 // 3
                dve.wait_ge(mod_col, n_done)
                b = par[:, N_BMOD + 48 * l + KD * s0:N_BMOD + 48 * l + KD * s1].unsqueeze(2).to_broadcast([P, KD * (s1 - s0), 2])
                link(v.tensor_tensor(modT[:, l, s0:s1, :, :].rearrange("p s k c -> p (s k) c"),
                                     ps[:, bank, 2 * KD * s0:2 * KD * s1].rearrange("p (a c) -> p a c", c=2), b, ALU.add))
                for n in range(s0 // 3, s1 // 3):
                    g = par[:, N_G + 16 * l + 8 * n:N_G + 16 * l + 8 * n + 8].unsqueeze(2).to_broadcast([P, 8, 2])
                    link(v.tensor_scalar(gain[:, l, n, :, :], modT[:, l, 3 * n + 1, :, :], 1.0, None, ALU.add))
                    last = v.tensor_tensor(gain[:, l, n, :, :], gain[:, l, n, :, :], g, ALU.mult)
                    if 3 * n + 3 < s1:
                        link(last)
                last.then_inc(mod_done, 1)
                dve.wait_ge(mod_done, n_done)

            for st in stages:
                kind, l, h = st
                u = BASE[st]
                if kind == "mod":
                    v.memset(zeros[:, :], 0.0)
                    v.memset(s5p[:, :, DEPTH * 2 * NT:DEPTH * 2 * NT + 1], 0.0)
                    lr, li = par[:, N_LAM:N_LAM + 64], par[:, N_LAM + 64:N_LAM + 128]
                    dve.wait_ge(s5_lam, 1)
                    link(v.tensor_tensor(sp_(S_TH), li, sp_(S_DT), ALU.mult))
                    v.tensor_tensor(sp_(S_T0), lr, sp_(S_DT), ALU.mult)
                    link(v.tensor_scalar(s5k[:, :], sp_(S_TH), INV2PI, None, ALU.mult))
                    link(v.tensor_copy(sp_(S_K), s5k[:, :]))
                    for part in (TP1, TP2, TP3):
                        link(v.scalar_tensor_tensor(sp_(S_TH), sp_(S_K), -part, sp_(S_TH), ALU.mult, ALU.add))
                    link(v.tensor_scalar(sp_(S_TH), sp_(S_TH), 3.1415925, -3.1415925, ALU.min, ALU.max))
                    link(v.tensor_scalar(sp_(S_RHO), sp_(S_TH), INV2PI, None, ALU.mult))
                    link(v.tensor_scalar(s5k[:, :], sp_(S_RHO), 32768.0, None, ALU.mult))
                    link(v.tensor_scalar(sp_(S_RHI), s5k[:, :], 1.0 / 32768.0, None, ALU.mult))
                    link(v.scalar_tensor_tensor(sp_(S_RLO), sp_(S_RHI), -TP1, sp_(S_TH), ALU.mult, ALU.add))
                    link(v.scalar_tensor_tensor(sp_(S_RLO), sp_(S_RHI), -TP2, sp_(S_RLO), ALU.mult, ALU.add))
                    link(v.tensor_scalar(sp_(S_RLO), sp_(S_RLO), INV2PI, None, ALU.mult))
                    link(v.tensor_copy(sp_(S_T1), sp_(S_TH)))
                    link(v.tensor_scalar(sp_(S_T2), sp_(S_TH), -1.0, None, ALU.mult))
                    v.tensor_tensor(sp_(S_T2), sp_(S_T2), sp_(S_TH), ALU.max).then_inc(s5_angle, 1)
                    dve.wait_ge(s5_trig, 1)
                    link(v.tensor_tensor(sp_(S_COS), sp_(S_COS), sp_(S_R), ALU.mult))
                    link(v.tensor_tensor(sp_(S_SIN), sp_(S_SIN), sp_(S_R), ALU.mult))
                    link(v.tensor_scalar(sp_(S_COS), sp_(S_COS), -1.0, None, ALU.add))
                    link(v.tensor_tensor(sp_(S_T0), lr, lr, ALU.mult))
                    link(v.tensor_tensor(sp_(S_T1), li, li, ALU.mult))
                    link(v.tensor_tensor(sp_(S_T0), sp_(S_T0), sp_(S_T1), ALU.add))
                    link(v.reciprocal(sp_(S_T2), sp_(S_T0)))
                    link(v.tensor_tensor(sp_(S_T0), sp_(S_COS), lr, ALU.mult))
                    link(v.tensor_tensor(sp_(S_T1), sp_(S_SIN), li, ALU.mult))
                    link(v.tensor_tensor(sp_(S_T0), sp_(S_T0), sp_(S_T1), ALU.add))
                    link(v.tensor_tensor(sp_(S_BR), sp_(S_T0), sp_(S_T2), ALU.mult))
                    link(v.tensor_tensor(sp_(S_T0), sp_(S_SIN), lr, ALU.mult))
                    link(v.tensor_tensor(sp_(S_T1), sp_(S_COS), li, ALU.mult))
                    link(v.tensor_tensor(sp_(S_T0), sp_(S_T0), sp_(S_T1), ALU.subtract))
                    link(v.tensor_tensor(sp_(S_BI), sp_(S_T0), sp_(S_T2), ALU.mult))
                    link(v.tensor_scalar(sp_(S_NBR), sp_(S_BR), -1.0, None, ALU.mult))
                    link(v.tensor_scalar(sp_(S_NBI), sp_(S_BI), -1.0, None, ALU.mult))
                    inverted(("norm1", 0, 0), rs1, TL)
                    mod_tables(0, 0, 6, 4)
                elif kind == "norm1":
                    normed(st, rs1, TL, hT, 0, lambda k, s: gain[:, l, 0, k, s:s + 1], h_scaled)
                elif kind == "norm2":
                    normed(st, rs2, 256, h2T, CTX * h, lambda k, s: gain[:, l, 1, k, s:s + 1], h_scaled)
                    dve.wait_ge(h_ready, KD * (norms_before(st) + 1))
                    link(v.tensor_copy(h2h[:, :, :], h2T[:, :, :]))
                    v.tensor_tensor(h2l[:, :, :], h2T[:, :, :], h2h[:, :, :].bitcast(F32), ALU.subtract)
                elif kind == "final":
                    normed(st, rs2, 256, fout, CTX, lambda k, s: par[:, N_FG + k:N_FG + k + 1], fin_ready)
                elif kind == "s5":
                    lo, hi = layer_width(l)
                    w_ = hi - lo
                    dve.wait_ge(mcst_in, 16 * (l + 1))
                    C = ring[:, u % RING, 8 * P:8 * P + 8 * 32].rearrange("p (q c n) -> p q c n", q=4, c=2)

                    def phases(n, i):
                        d = n % 2
                        t = mcst[:, M_T:M_T + TL]
                        dve.wait_ge(turns_ready, i * 8 + (l * 34 + n + 1))
                        count(dve, table_ready, i * 8 + (l * 33 + n - 1))
                        link(v.scalar_tensor_tensor(phase[:, d, :], t, lane(S_RHI, n, l, i), turns[:, d, :], ALU.mult, ALU.subtract))
                        link(v.scalar_tensor_tensor(phase[:, d, :], t, lane(S_RLO, n, l, i), phase[:, d, :], ALU.mult, ALU.add))
                        v.tensor_scalar(phase[:, d, :], phase[:, d, :], 0.5, -0.5, ALU.min, ALU.max
                                        ).then_inc(phase_ready, 1)

                    def step(n, i):
                        q, d = n // 2, n % 2
                        phases(n + 1, i)
                        count(dve, table_ready, i * 8 + (l * 33 + n + 1))
                        count(dve, bu_copied, i * 4 + (l * 16 + q + 1))
                        count(dve, prod_ready, i * 8 + (l * 32 + n - 1))
                        T, G, B = tab[:, d, :, :], gst[:, d, :, :], bu[:, q % 2, :, :]

                        def times(dst, b_, t_):
                            if d:
                                return v.tensor_tensor(dst.rearrange("p (h t) -> p h t", t=256),
                                                       b_.rearrange("p (h t) -> p h t", t=256)[:, :, ::-1],
                                                       t_.rearrange("p (h t) -> p h t", t=256), ALU.mult)
                            return v.tensor_tensor(dst, b_, t_, ALU.mult)

                        times(G[:, 0, :], B[:, 0, :], T[:, 0, :])
                        times(G[:, 1, :], B[:, 1, :], T[:, 0, :])
                        last = times(rot[:, 0, :], B[:, 1, :], T[:, 1, :])
                        if not pool_turns(l):
                            last = times(rot[:, 1, :], B[:, 0, :], T[:, 1, :])
                        link(last)
                        v.tensor_tensor(G[:, 0, :], G[:, 0, :], rot[:, 0, :], ALU.add)
                        if pool_turns(l):
                            dve.wait_ge(turned, i * 8 + n + 1)
                        link(v.tensor_tensor(G[:, 1, :], G[:, 1, :], rot[:, 1, :], ALU.subtract))
                        r = lane(S_R, n, l, i).to_broadcast([P, TL])
                        for c in range(2):
                            last = v.tensor_tensor_scan(G[:, c, :], r, G[:, c, :], 0.0, ALU.mult, ALU.add)
                        last.then_inc(g_ready, 1)

                    def c_prime(i):
                        arrived(dve, u, i, 4)
                        for d in range(2):
                            f = {k: s5p[:, k, bass.ds(i * 4 + (2 * l + d) * NT, 4)].unsqueeze(2).to_broadcast([P, 4, 32])
                                 for k in (S_BR, S_NBR, S_NBI)}
                            v.tensor_tensor(ctmp[:, 0, :, :], C[:, :, 1, :], f[S_NBI], ALU.mult)
                            v.tensor_tensor(ctmp[:, 1, :, :], C[:, :, 1, :], f[S_NBR], ALU.mult)
                            v.tensor_tensor(cpr[:, d, 0, :, :], C[:, :, 0, :], f[S_BR], ALU.mult)
                            link(v.tensor_tensor(cpr[:, d, 2, :, :], C[:, :, 0, :], f[S_NBI], ALU.mult))
                            v.tensor_tensor(cpr[:, d, 2, :, :], cpr[:, d, 2, :, :], ctmp[:, 1, :, :], ALU.add)
                            link(v.tensor_tensor(cpr[:, d, 0, :, :], cpr[:, d, 0, :, :], ctmp[:, 0, :, :], ALU.add))
                            last = v.tensor_scalar(cpr[:, d, 1, :, :], cpr[:, d, 0, :, :], -1.0, None, ALU.mult)
                        last.then_inc(cprime_ready, 1)

                    def take_y(m, after):
                        count(dve, readout, after)
                        uq = uT[:, bass.ds(m, 1), lo:hi].rearrange("p o t -> p (o t)")
                        dq = par[:, bass.ds(m + (N_D + 4 * l), 1)]
                        v.scalar_tensor_tensor(uq, uq, dq, ps[:, 6, 0:w_], ALU.mult, ALU.add).then_inc(y_out, 1)

                    phases(0, 0)
                    step(0, 0)
                    c_prime(0)
                    for n in range(1, 8):
                        step(n, 0)
                    with dve.Fori(1, S5_ITER) as i:
                        own.loop(i, S5_LINKS)
                        own.extra = (i - 1) * S5_LINKS
                        step(0, i)
                        take_y(i - 1, i * 8 + l * 32)
                        c_prime(i)
                        for n in range(1, 8):
                            step(n, i)
                        own.end(S5_ITER - 1)
                    take_y(S5_ITER - 1, (l + 1) * 32)
                elif kind == "ret":
                    lo, hi = layer_width(l)
                    dist = slot(u, 4, 512)
                    arrived(dve, u)
                    for hd in range(RH):
                        b = (2 * l + 1) * RH + hd
                        last = v.tensor_scalar(dtmp[:, hd, :], dist[:, 1, :], lg[:, b:b + 1], None, ALU.mult)
                    link(last)
                    count(dve, table_ready, 33 * (l + 1))
                    for hd in range(RH):
                        f = 2 * l * RH + hd
                        last = v.scalar_tensor_tensor(decay[:, hd, 0, :], dist[:, 0, :], lg[:, f:f + 1], dtmp[:, hd, :],
                                                      ALU.mult, ALU.add)
                    last.then_inc(decay_arg, 1)
                    dve.wait_ge(decay_ready, l + 1)
                    v.tensor_tensor(decay[:, :, 1, :], decay[:, :, 1, :], dtmp[:, :, :], ALU.add).then_inc(used[u % RING], 1)
                    for j, src in enumerate((qT, kT)):
                        dve.wait_ge(rope_ps, 2 * l + j + 1)
                        cos = mcst[:, M_COS:M_COS + 256].unsqueeze(1).to_broadcast([P, RH, 256])
                        sin = mcst[:, M_SIN:M_SIN + 256].unsqueeze(1).to_broadcast([P, RH, 256])
                        pp = ps[:, 2 * j:2 * j + 2, :].rearrange("p b (a t) -> p (b a) t", a=2)
                        own.mark(v.tensor_tensor(oT[:, :, 0:256], pp, sin, ALU.mult))
                        link(v.tensor_tensor(src[:, :, CTX:TL], src[:, :, CTX:TL], cos, ALU.mult))
                        v.tensor_tensor(src[:, :, CTX:TL], src[:, :, CTX:TL], oT[:, :, 0:256], ALU.add).then_inc(roped, 1)
                        dve.wait_ge(roped, 2 * l + j + 1)
                    scale = P ** -0.5
                    for hd in range(RH):
                        b = 3 * (hd % 2)
                        dve.wait_ge(score_ps, l * RH + hd + 1)
                        if hd == 0:
                            unit_used(dve, u)
                        if hd >= 2:
                            dve.wait_ge(o_ps, l * RH + hd - 1)
                        for g, (bank, which) in enumerate(((0, 1), (1, 0), (2, 0))[:3 if lo == 0 else 2]):
                            last = v.scalar_tensor_tensor(
                                sd[:, hd % 2, 2 * g:2 * g + 2, :].rearrange("p a t -> p (a t)"), ps[:, b + bank, :],
                                scale, decay[:, hd, which, :], ALU.mult, ALU.mult)
                        last.then_inc(sd_ready, 1)
                    dve.wait_ge(ostd_ready, l + 1)
                    dve.wait_ge(o_copied, RH * (l + 1))
                    link(v.reciprocal(osq[:, :, lo:hi], osq[:, :, lo:hi]))
                    link(v.tensor_tensor(oT[:, :, lo:hi], oT[:, :, lo:hi], osq[:, :, lo:hi], ALU.mult))
                    dve.wait_ge(gates_on, 2 * l + 2)
                    v.tensor_tensor(gT[:, :, lo:hi], oT[:, :, lo:hi], gT[:, :, lo:hi], ALU.mult).then_inc(yr_ready, 1)
                elif kind == "merge":
                    lo, hi = layer_width(l)
                    w_ = hi - lo
                    for j in range(MERGE_UNITS):
                        dve.wait_ge(sg_ready, KD * l + j + 1)
                        unit_used(dve, u + j)
                        own.mark(v.tensor_tensor(mt1[:, j % 2, 0:w_], ps[:, j % 2, 0:w_], sgb[:, j % 2, 0:w_], ALU.mult))
                        link(v.tensor_tensor(mt2[:, j % 2, 0:w_], ps[:, 4 + j % 2, 0:w_], grT[:, j, lo:hi], ALU.mult))
                        link(v.tensor_tensor(mt1[:, j % 2, 0:w_], mt1[:, j % 2, 0:w_], gsT[:, j, lo:hi], ALU.mult))
                        v.tensor_tensor(mT[:, j, 0:w_], mt1[:, j % 2, 0:w_], mt2[:, j % 2, 0:w_], ALU.add).then_inc(m_ready, 1)
                    for j in range(OUT_UNITS):
                        unit_used(dve, u + MERGE_UNITS + j)
                        for t in range(2):
                            for side in range(lo // CTX, 2):
                                k = 2 * j + t
                                xs = xT[:, k, CTX * side:CTX * side + 256]
                                last = v.scalar_tensor_tensor(
                                    xs, ps[:, 2 * (j % 2) + t, CTX * side - lo:CTX * side - lo + 256],
                                    modT[:, l, 2, k, side:side + 1], xs, ALU.mult, ALU.add)
                        last.then_inc(x_ready, 1)
                elif kind == "route":
                    p = passes_before(st)
                    streams = [(tb, s_) for tb in range(2) for s_ in range(2)]
                    for hd in range(NH + 1):
                        key, sums = hd < NH, hd > 0
                        if key and hd % 2 == 0:
                            dve.wait_ge(score_ready, WQ_UNITS * p + hd // 2 + 1)
                        K = [(sc[:, tb, 2 * hd + s_, :], top[:, tb, 2 * hd + s_, :], topi[:, tb, 2 * hd + s_, :],
                              sc2[:, 2 * tb + s_, :]) for tb, s_ in streams if key]
                        S = [(cand[:, tb, :], best[:, tb, hd - 1, :], besti[:, tb, hd - 1, :], cand2[:, tb, :])
                             for tb in range(2) if sums]
                        for a_, t_, _i, _o in K + S:
                            last = v.max(t_[:, 0:8], a_)
                        link(last)
                        for a_, t_, i_, _o in K + S:
                            v.max_index(i_[:, 0:8], t_[:, 0:8], a_)
                        for a_, t_, _i, o_ in K + S:
                            last = v.match_replace(o_, t_[:, 0:8], a_, -3e38)
                        link(last)
                        for _a, t_, _i, o_ in K + S:
                            last = v.max(t_[:, 8:16], o_)
                        link(last)
                        for _a, t_, i_, o_ in K + S:
                            last = v.max_index(i_[:, 8:16], t_[:, 8:16], o_)
                        if key:
                            for tb in range(2):
                                one, two = top[:, tb, 2 * hd, :], top[:, tb, 2 * hd + 1, :]
                                v.tensor_scalar(cand[:, tb, 0:TOPK], two, one[:, 0:1], None, ALU.add)
                                last = v.tensor_tensor(
                                    cand[:, tb, TOPK:CANDS].rearrange("p (a b) -> p a b", b=8),
                                    one[:, 1:TOPK].unsqueeze(2).to_broadcast([P, TOPK - 1, 8]),
                                    two[:, 0:8].unsqueeze(1).to_broadcast([P, TOPK - 1, 8]), ALU.add)
                        link(last)
                    b3 = best[:, :, :, :].rearrange("p t h k -> p (t h) k")
                    g3 = place[:, :].rearrange("p (t k) -> p t k", k=TOPK)
                    link(v.tensor_copy(g3, b3[:, :, 0:1].to_broadcast([P, 2 * NH, TOPK])))
                    v.tensor_tensor(b3, b3, g3, ALU.subtract).then_inc(exp_in, 1)
                    v.tensor_copy(topf[:, :, :, :], topi[:, :, :, :])
                    dve.wait_ge(exp_in, p + 1)
                    link(v.tensor_copy(place[:, :], besti[:, :, :, :].rearrange("p t h k -> p (t h k)")))
                    link(v.tensor_scalar(placei[:, 0, :], place[:, :], -8.0, 0.0, ALU.add, ALU.max))
                    link(v.tensor_scalar(placei[:, 1, :], placei[:, 0, :], 3, None, ALU.logical_shift_right))
                    ra, rb = rank[:, 0, :, :].rearrange("p t k -> p (t k)"), rank[:, 1, :, :].rearrange("p t k -> p (t k)")
                    link(v.tensor_copy(ra, placei[:, 1, :]))
                    v.tensor_scalar(rb, ra, 1.0, -8.0, ALU.min, ALU.mult)
                    link(v.scalar_tensor_tensor(place[:, :], ra, -8.0, place[:, :], ALU.mult, ALU.add))
                    link(v.tensor_tensor(rb, rb, place[:, :], ALU.add))
                    i16 = cst[:, C_I16:C_I16 + TOPK].unsqueeze(1).to_broadcast([P, NH * TOPK, TOPK])
                    for tb in range(2):
                        for s_ in range(2):
                            last = v.tensor_tensor(eq[:, tb, s_, :, :],
                                                   rank[:, s_, tb, :].unsqueeze(2).to_broadcast([P, NH * TOPK, TOPK]),
                                                   i16, ALU.is_equal)
                            if s_ == 0:
                                last.then_inc(eq_ready, 1)
                    link(last)
                    for tb in range(2):
                        e4 = eq[:, tb, 1, :, :].rearrange("p (h k) a -> p h k a", h=NH)
                        t4 = topf[:, tb, 1::2, :].unsqueeze(2).to_broadcast([P, NH, TOPK, TOPK])
                        last = v.tensor_tensor(e4, e4, t4, ALU.mult)
                    link(last)
                    for tb in range(2):
                        v.tensor_reduce(pick[:, tb, 1, :], eq[:, tb, 1, :, :], AX_X, ALU.add)
                    dve.wait_ge(exp_out, p + 1)
                    link(v.tensor_reduce(ssum[:, :], b3, AX_X, ALU.add))
                    link(v.reciprocal(ssum[:, :], ssum[:, :]))
                    for tb in range(2):
                        v.tensor_tensor(pick[:, tb, 2, :].rearrange("p (h k) -> p h k", h=NH), best[:, tb, :, :],
                                        ssum[:, NH * tb:NH * tb + NH].unsqueeze(2).to_broadcast([P, NH, TOPK]), ALU.mult)
                    for tb in range(2):
                        dve.wait_ge(eq_times, 2 * p + tb + 1)
                        last = v.tensor_reduce(pick[:, tb, 0, :], eq[:, tb, 0, :, :], AX_X, ALU.add)
                    last.then_inc(pick_ready, 1)
                    half = next_mod(st)
                    if half is not None:
                        mod_tables(l + 1, 3 * half, 3 * half + 3, 2)
                elif kind == "gates":
                    p = passes_before(st)
                    dve.wait_ge(pick_col, p + 1)
                    dve.wait_ge(x_held, 16 * (p + 1))
                    with dve.Fori(0, 16) as i:
                        for g in range(4):
                            count(dve, gate_ps, i * 4 + (64 * p + g - 3))
                            v.tensor_tensor(hot[:, g, :, :, :],
                                            iota.unsqueeze(1).unsqueeze(1).to_broadcast([P, 2, 4, P]),
                                            idxT[:, 0:2, bass.ds(i * 16 + 4 * g, 4)].unsqueeze(3).to_broadcast([P, 2, 4, P]),
                                            ALU.is_equal).then_inc(hot_eq, 1)
                elif kind == "experts":
                    p = passes_before(st)
                    def u_low(k, i):
                        dve.wait_ge(uhi_ready, i * RING + (NK * p + k + 1))
                        r = (u + k) % RING
                        v.tensor_tensor(elo[:, r, 0:DM], ring[:, r, 0:DM], ehi[:, k % 2, :].bitcast(F32), ALU.subtract
                                        ).then_inc(ulo_ready, 1)

                    u_low(0, 0)
                    u_low(1, 0)

                    def step(k, i, ahead):
                        dve.wait_ge(act_ready, i * RING + (NK * p + k + 1))
                        unit_used(dve, u + k - 2, i, RING)
                        g = gate[:, bass.ds(i * RING + k, 1), :].rearrange("p o t -> p (o t)")
                        b = k % 2
                        link(v.tensor_tensor(wf[:, b, :], actT[:, b, :], g, ALU.mult))
                        link(v.tensor_copy(wh[:, b, :], wf[:, b, :]))
                        v.tensor_tensor(wl[:, b, :], wf[:, b, :], wh[:, b, :].bitcast(F32), ALU.subtract
                                        ).then_inc(w_ready, 1)
                        dve.wait_ge(vhi_ready, i * RING + (NK * p + k + 1))
                        r = (u + k) % RING
                        v.tensor_tensor(elo[:, r, DM:2 * DM], ring[:, r, DM:2 * DM], ehi[:, 2 + b, :].bitcast(F32),
                                        ALU.subtract).then_inc(vlo_ready, 1)
                        if ahead:
                            u_low(k + 2, i)

                    with dve.Fori(0, NK // RING - 1) as i:
                        own.loop(i, 2 * RING)
                        for k in range(RING):
                            step(k, i, True)
                        own.end(NK // RING - 1)
                    for k in range(RING):
                        step(k, NK // RING - 1, k < 2)
                    dve.wait_ge(x_low_back, 16 * (p + 1))
                    dve.wait_ge(y_col, p + 1)
                    for k in range(KD):
                        if k == KD // 2:
                            dve.wait_ge(x_half_back, 16 * (p + 1))
                        xs = xT[:, k, CTX * h:CTX * h + 256]
                        last = v.scalar_tensor_tensor(xs, ps[:, 4 + k // 2, (k % 2) * 256:(k % 2) * 256 + 256],
                                                      modT[:, l, 5, k, h:h + 1], xs, ALU.mult, ALU.add)
                    last.then_inc(x_ready, 1)


def constants():
    c = np.zeros((P, C_N), np.float32)
    c[:, C_ID:C_ID + P] = np.eye(P)
    c[:, C_ONES_D:C_ONES_D + P] = 1.0 / DM
    c[:, C_ONES_H:C_ONES_H + P] = 1.0 / P
    c[:, C_IOTA:C_IOTA + P] = np.arange(P)
    for k in range(P):
        if k % 64 < 32:
            c[k + 32, C_PERM + k] = -1.0
        else:
            c[k - 32, C_PERM + k] = 1.0
    m = np.zeros((P, M_N), np.float32)
    m[:, M_T:M_T + TL] = np.arange(TL)
    c[:, C_I16:C_I16 + TOPK] = np.arange(TOPK)
    c[:, C_EPS] = EPS
    c[:, C_HPI] = np.float32(1.5707962)
    freqs = np.float32(10000.0) ** (-np.arange(32, dtype=np.float32) / np.float32(32))
    t = np.arange(SEQ)
    for d in range(P):
        at = (t // GRID_W if d < 64 else t % GRID_W).astype(np.float32) * freqs[d % 32]
        m[d, M_COS:M_COS + SEQ] = np.cos(at)
        m[d, M_SIN:M_SIN + SEQ] = np.sin(at)
    s = (np.arange(2)[None, :, None] * P + np.arange(P)[:, None, None]).astype(np.float32)
    tt = np.arange(256, dtype=np.float32)[None, None, :]
    d = np.stack([np.maximum(tt - s, 0), np.maximum(s - tt, 0), 256 + tt - s, 256 - tt + s], 1)
    return c, m, np.ascontiguousarray(d.reshape(P, 4 * 512), np.float32)


def layouts(i):
    f = lambda k: np.asarray(i[k])
    L = DEPTH
    out = {}
    out["x_t"] = np.concatenate([f("ctx")[0], f("x")[0]]).T.reshape(KD, P, TL).transpose(1, 0, 2)

    def tiles(w, per, n=P):
        k, m = w.shape[1:]
        return w.reshape(L, k // P, P, m // (n * per), per, n).transpose(0, 3, 2, 4, 1, 5)

    out["w_mod"] = tiles(f("w_mod"), 1, 256).reshape(L, MOD_UNITS, P, 2048)
    w_in = f("w_in")
    u, q, k, v, g, gs, gr = np.split(w_in, [512, 1024, 1536, 2048, 2560, 3584], axis=2)
    out["w_front"] = tiles(np.concatenate([u, v, k], 2), 2).reshape(L, FRONT_UNITS, P, 2048)
    out["w_side"] = tiles(np.concatenate([q, g, gs, gr], 2), 2).reshape(L, 12, P, 2048)
    glu, up = f("w_ssm_glu"), f("w_ret_up")
    parts = [tiles(w, 1).reshape(L, 8, P, 512) for w in (glu[:, :, :DM], glu[:, :, DM:], up)]
    out["w_merge"] = np.concatenate(parts, 3)
    out["w_out"] = tiles(f("w_out"), 2).reshape(L, OUT_UNITS, P, 2048)
    out["w_q"] = tiles(f("peer_w_q"), 2).reshape(L, WQ_UNITS, P, 2048)
    bc = np.zeros((L, 4, P, 8 * P + 256), np.float32)
    for c, (B, C) in enumerate((("ssm_B_re", "ssm_C_re"), ("ssm_B_im", "ssm_C_im"))):
        B, C = f(B).reshape(L, 4, 4, 2, 64, 16), f(C).reshape(L, 4, 4, 2, 16, 64)
        for q in range(4):
            for gi in range(2):
                r = 32 * q + 16 * gi
                bc[:, :, r:r + 16, (2 * q + c) * P + 64 * gi:(2 * q + c) * P + 64 * gi + 64] = B[:, :, q, gi].transpose(0, 1, 3, 2)
                at = 8 * P + (2 * q + c) * 32 + 16 * gi
                bc[:, :, 64 * gi:64 * gi + 64, at:at + 16] = C[:, :, q, gi].transpose(0, 1, 3, 2)
    out["s5_bc"] = bc
    keys = np.zeros((L, P, NH, 256), np.float32)
    sk = f("peer_sub_keys")
    for s in range(2):
        keys[:, 64 * s:64 * s + 64, :, P * s:P * s + P] = sk[:, :, s].transpose(0, 3, 1, 2)
    out["keys"] = keys
    ut = f("peer_u").reshape(L, NK, NK, KD, P).transpose(0, 2, 4, 3, 1).reshape(L, NK, P, DM)
    vt = f("peer_v").reshape(L, NK, NK, DM).transpose(0, 2, 1, 3)
    out["experts"] = np.concatenate([ut, vt], 3)
    p = np.zeros((P, N_N), np.float32)
    col = lambda w, n: w.reshape(L, n, P).transpose(2, 0, 1).reshape(P, L * n)
    p[:, N_BMOD:N_BMOD + 96] = col(f("b_mod"), 48)
    p[:, N_G:N_G + 32] = np.stack([f("norm1_g"), f("norm2_g")], 1).reshape(L, 2, 8, P).transpose(3, 0, 1, 2).reshape(P, 32)
    p[:, N_FG:N_FG + 8] = f("final_norm_g").reshape(8, P).T
    dirs = lambda w: np.stack([f(w + "_f"), f(w + "_b")], 1)
    lanes = lambda w: w.reshape(L, 2, NT, P).transpose(3, 0, 1, 2).reshape(P, 64)
    p[:, N_LAM:N_LAM + 64] = lanes(dirs("ssm_lam_re"))
    p[:, N_LAM + 64:N_LAM + 128] = lanes(dirs("ssm_lam_im"))
    p[:, N_LAM + 128:N_LAM + 192] = lanes(np.repeat(dirs("ssm_log_dt"), 64, axis=2))
    p[:, N_DEC:N_DEC + 16] = dirs("ret_decay").reshape(1, 16)
    p[:, N_D:N_D + 8] = col(f("ssm_D"), 4)
    p[:, N_C:N_C + 16] = np.stack([f("c_ctx"), f("c")[0]], 1).reshape(8, P, 2).transpose(1, 0, 2).reshape(P, 16)
    out["params"] = p
    out["consts"], out["mixer_consts"], out["dist"] = constants()
    return {k: np.ascontiguousarray(a, np.float32) if a.dtype != np.float32 else np.ascontiguousarray(a) for k, a in out.items()}


def kernel(**inputs):
    import concourse.bacc as bacc
    from concourse.bass_utils import run_bass_kernel_spmd

    nc = bacc.Bacc("TRN2", target_bir_lowering=False, num_devices=1)
    arrays = layouts(inputs)
    aps = {k: nc.dram_tensor(f"in_{k}", a.shape, F32, kind="ExternalInput").ap() for k, a in arrays.items()}
    aps["out"] = nc.dram_tensor("out_t", (P, KD, SEQ), F32, kind="ExternalOutput").ap()
    aps["x_scratch"] = nc.dram_tensor("x_scratch", (P, KD, TL), F32, kind="Internal").ap()
    build_program(nc, aps)
    r = run_bass_kernel_spmd(nc, [{f"in_{k}": a for k, a in arrays.items()}], core_ids=[0])
    got = r.results[0]["out_t"]
    return np.ascontiguousarray(got.transpose(1, 0, 2).reshape(DM, SEQ).T)[None]
```
